# Optimizing a Trainium2 kernel written in Bass

```python
import jax, jax.numpy as jnp
from jax import lax
import numpy as np
import math

D_MODEL = 1024
BATCH = 1
SEQ = 512
DEPTH = 2

CHUNK = 64
N_A_LAYERS = DEPTH // 2
N_B_LAYERS = DEPTH - N_A_LAYERS
GMLP_BLOCK = 128
GMLP_WIDTH = D_MODEL
GMLP_GROUPS = 8
GMLP_GROUP_DIM = GMLP_WIDTH // GMLP_GROUPS
N_HEADS = 16
HEAD_DIM = D_MODEL // N_HEADS
LEFT_CHUNKS = 8
BAND = (LEFT_CHUNKS + 1) * CHUNK
PAD = LEFT_CHUNKS * CHUNK
REL_CLIP = 128
REL_SIZE = 2 * REL_CLIP + 1
D_FF = ((8 * D_MODEL // 3 + 127) // 128) * 128
CONV_WIDTH = 3
EPS = 1e-6
NEG_INF = -1e30


def rmsnorm(x, g):
    xf = x.astype(jnp.float32)
    y = xf * lax.rsqrt(jnp.mean(xf * xf, axis=-1, keepdims=True) + EPS)
    return (y * g.astype(jnp.float32)).astype(x.dtype)

def gmlp_mixer(h, w_in, v_norm_g, w_s, b_s, w_out):
    B, S, _ = h.shape
    z = jax.nn.gelu(h @ w_in)
    u, v = jnp.split(z, 2, axis=-1)
    v = rmsnorm(v, v_norm_g)
    pos_chunk = jnp.arange(GMLP_BLOCK) // CHUNK
    mask = pos_chunk[:, None] >= pos_chunk[None, :]
    w = jnp.where(mask[None], w_s, 0)
    v = v.reshape(B, S // GMLP_BLOCK, GMLP_BLOCK, GMLP_GROUPS, GMLP_GROUP_DIM)
    s = jnp.einsum('gij,bnjgc->bnigc', w, v) + b_s.T[None, None, :, :, None]
    out = u * s.reshape(B, S, GMLP_WIDTH)
    return out @ w_out

def chunk_attention(h, k, v, w_q, rel_bias, w_o):
    B, S, _ = h.shape
    nc = S // CHUNK
    scale = HEAD_DIM ** -0.5
    q = (h @ w_q).reshape(B, nc, CHUNK, N_HEADS, HEAD_DIM) * scale
    qc = jnp.moveaxis(q, 1, 0)
    kp = jnp.pad(k, ((0, 0), (PAD, 0), (0, 0), (0, 0)))
    vp = jnp.pad(v, ((0, 0), (PAD, 0), (0, 0), (0, 0)))
    qi = jnp.arange(CHUNK)[:, None]
    kj = jnp.arange(BAND)[None, :]
    rel_idx = jnp.clip(qi - kj + PAD, -REL_CLIP, REL_CLIP) + REL_CLIP
    bias = rel_bias[:, rel_idx].astype(jnp.float32)

    def one_chunk(args):
        c, qb = args
        start = c * CHUNK
        kb = lax.dynamic_slice_in_dim(kp, start, BAND, axis=1)
        vb = lax.dynamic_slice_in_dim(vp, start, BAND, axis=1)
        sc = jnp.einsum('bqhd,bkhd->bhqk', qb, kb).astype(jnp.float32) + bias
        valid = (start - PAD + jnp.arange(BAND)) >= 0
        sc = jnp.where(valid[None, None, None, :], sc, NEG_INF)
        p = jax.nn.softmax(sc, axis=-1).astype(vb.dtype)
        return jnp.einsum('bhqk,bkhd->bqhd', p, vb)

    o = lax.map(one_chunk, (jnp.arange(nc), qc))
    o = jnp.moveaxis(o, 0, 1).reshape(B, S, N_HEADS * HEAD_DIM)
    return o @ w_o

def conv_ffn(h, w_in, conv_w, conv_b, w_down):
    a = h @ w_in
    C = a.shape[-1]
    a = lax.conv_general_dilated(
        a, conv_w[:, None, :].astype(a.dtype), window_strides=(1,),
        padding=[(CONV_WIDTH - 1, 0)], dimension_numbers=('NWC', 'WIO', 'NWC'),
        feature_group_count=C) + conv_b
    up, gate = jnp.split(a, 2, axis=-1)
    return (jax.nn.silu(gate) * up) @ w_down

def first_inputs(seed: int = 0) -> dict:
    key = jax.random.key(seed)
    ks = jax.random.split(key, 20)
    nrm = lambda k, shape, s: jax.random.normal(k, shape, jnp.float32) * s
    gain = lambda k, shape: 1.0 + nrm(k, shape, 0.02)
    HD = N_HEADS * HEAD_DIM
    return {
        "x": nrm(ks[0], (BATCH, SEQ, D_MODEL), 1.0),
        "a_norm_g": gain(ks[1], (N_A_LAYERS, D_MODEL)),
        "a_w_in": nrm(ks[2], (N_A_LAYERS, D_MODEL, 2 * GMLP_WIDTH), D_MODEL ** -0.5),
        "a_v_norm_g": gain(ks[3], (N_A_LAYERS, GMLP_WIDTH)),
        "a_w_s": nrm(ks[4], (N_A_LAYERS, GMLP_GROUPS, GMLP_BLOCK, GMLP_BLOCK), GMLP_BLOCK ** -0.5),
        "a_b_s": 1.0 + nrm(ks[5], (N_A_LAYERS, GMLP_GROUPS, GMLP_BLOCK), 0.01),
        "a_w_out": nrm(ks[6], (N_A_LAYERS, GMLP_WIDTH, D_MODEL), GMLP_WIDTH ** -0.5),
        "kv_norm_g": gain(ks[7], (D_MODEL,)),
        "w_kv": nrm(ks[8], (D_MODEL, 2 * HD), D_MODEL ** -0.5),
        "b_norm_g": gain(ks[9], (N_B_LAYERS, D_MODEL)),
        "b_w_q": nrm(ks[10], (N_B_LAYERS, D_MODEL, HD), D_MODEL ** -0.5),
        "b_rel_bias": nrm(ks[11], (N_B_LAYERS, N_HEADS, REL_SIZE), 0.5),
        "b_w_o": nrm(ks[12], (N_B_LAYERS, HD, D_MODEL), HD ** -0.5),
        "f_norm_g": gain(ks[13], (DEPTH, D_MODEL)),
        "f_w_in": nrm(ks[14], (DEPTH, D_MODEL, 2 * D_FF), D_MODEL ** -0.5),
        "f_conv_w": nrm(ks[15], (DEPTH, CONV_WIDTH, 2 * D_FF), CONV_WIDTH ** -0.5),
        "f_conv_b": nrm(ks[16], (DEPTH, 2 * D_FF), 0.01),
        "f_w_down": nrm(ks[17], (DEPTH, D_FF, D_MODEL), D_FF ** -0.5),
        "final_norm_g": gain(ks[18], (D_MODEL,)),
    }

def first_block(x, a_norm_g, a_w_in, a_v_norm_g, a_w_s, a_b_s, a_w_out,
              kv_norm_g, w_kv, b_norm_g, b_w_q, b_rel_bias, b_w_o,
              f_norm_g, f_w_in, f_conv_w, f_conv_b, f_w_down, final_norm_g):
    B, S, _ = x.shape
    h = x
    k_shared = v_shared = None
    for l in range(DEPTH):
        if l < N_A_LAYERS:
            h = h + gmlp_mixer(rmsnorm(h, a_norm_g[l]), a_w_in[l], a_v_norm_g[l],
                               a_w_s[l], a_b_s[l], a_w_out[l])
        else:
            if l == N_A_LAYERS:
                kv = rmsnorm(h, kv_norm_g) @ w_kv
                k_shared, v_shared = jnp.split(kv, 2, axis=-1)
                k_shared = k_shared.reshape(B, S, N_HEADS, HEAD_DIM)
                v_shared = v_shared.reshape(B, S, N_HEADS, HEAD_DIM)
            j = l - N_A_LAYERS
            h = h + chunk_attention(rmsnorm(h, b_norm_g[j]), k_shared, v_shared,
                                    b_w_q[j], b_rel_bias[j], b_w_o[j])
        h = h + conv_ffn(rmsnorm(h, f_norm_g[l]), f_w_in[l], f_conv_w[l],
                         f_conv_b[l], f_w_down[l])
    return rmsnorm(h, final_norm_g)


DEPTH_2 = 1

HEAD_DIM_2 = 64
FOX_HEADS = D_MODEL // 2 // HEAD_DIM_2
RWKV_HEADS = D_MODEL // 2 // HEAD_DIM_2
FOX_WIDTH = FOX_HEADS * HEAD_DIM_2
RWKV_WIDTH = RWKV_HEADS * HEAD_DIM_2
D_MIX = FOX_WIDTH + RWKV_WIDTH
Q_BLOCK = 128
RMS_EPS = 1e-6
LNX_EPS = 64e-5
DECAY_LORA = max(32, int(round(1.8 * D_MODEL ** 0.5 / 32)) * 32)
ICLR_LORA = max(32, int(round(1.8 * D_MODEL ** 0.5 / 32)) * 32)
GATE_LORA = max(32, int(round(0.6 * D_MODEL ** 0.8 / 32)) * 32)
FOX_SPLITS = [FOX_WIDTH, FOX_WIDTH, FOX_WIDTH, FOX_WIDTH, FOX_HEADS, FOX_HEADS, FOX_HEADS]
RWKV_SPLITS = [RWKV_WIDTH, RWKV_WIDTH, RWKV_WIDTH, DECAY_LORA, ICLR_LORA, GATE_LORA]
FOX_COLS = sum(FOX_SPLITS)
RWKV_COLS = sum(RWKV_SPLITS)
D_IN_PROJ = FOX_COLS + RWKV_COLS
FORGET_BIAS_MEAN = 3.0
N_EXPERTS = 64
N_GROUPS = 8
TOPK_GROUPS = 4
TOP_K = 6
D_EXPERT = 256
D_SHARED = 256
ROUTED_SCALE = 2.5
EXPERT_BLOCK = 256


def rms_norm(x, gain, eps=RMS_EPS):
    xf = x.astype(jnp.float32)
    y = xf * lax.rsqrt(jnp.mean(xf * xf, axis=-1, keepdims=True) + eps)
    return (y * gain.astype(jnp.float32)).astype(x.dtype)

def shift_prev(z):
    pad = [(0, 0), (1, 0)] + [(0, 0)] * (z.ndim - 2)
    return jnp.pad(z, pad)[:, :-1]

def split_cols(z, sizes):
    cuts = [int(s) for s in np.cumsum(sizes)[:-1]]
    return jnp.split(z, cuts, axis=-1)

def swiglu(x, wg, wu, wd):
    return (jax.nn.silu(x @ wg) * (x @ wu)) @ wd

def fox_attention(q, k, v, cum):
    B, T, H, D = q.shape
    nb = T // Q_BLOCK
    scale = D ** -0.5
    qb = q.reshape(B, nb, Q_BLOCK, H, D).transpose(1, 0, 3, 2, 4)
    cb = cum.reshape(B, nb, Q_BLOCK, H).transpose(1, 0, 3, 2)
    kh = k.transpose(0, 2, 1, 3)
    vh = v.transpose(0, 2, 1, 3)
    ck = cum.transpose(0, 2, 1)
    key_pos = jnp.arange(T)

    def block(args):
        q_blk, c_blk, i = args
        s = jnp.einsum('bhqd,bhkd->bhqk', q_blk, kh).astype(jnp.float32) * scale
        s = s + (c_blk[..., :, None] - ck[:, :, None, :])
        q_pos = i * Q_BLOCK + jnp.arange(Q_BLOCK)
        s = jnp.where(key_pos[None, :] <= q_pos[:, None], s, -jnp.inf)
        p = jax.nn.softmax(s, axis=-1)
        return jnp.einsum('bhqk,bhkd->bhqd', p.astype(vh.dtype), vh)

    o = lax.map(block, (qb, cb, jnp.arange(nb)))
    return o.transpose(1, 0, 3, 2, 4).reshape(B, T, H, D)

def fox_mixer(zf, qn_g, kn_g, on_g, forget_b):
    B, T, _ = zf.shape
    q, k, v, g, f_logit, a_k, a_v = split_cols(zf, FOX_SPLITS)
    heads = lambda t: t.reshape(B, T, FOX_HEADS, HEAD_DIM_2)
    q, k, v = heads(q), heads(k), heads(v)
    a_k = jax.nn.sigmoid(a_k)[..., None]
    a_v = jax.nn.sigmoid(a_v)[..., None]
    k = a_k * shift_prev(k) + (1 - a_k) * k
    v = a_v * shift_prev(v) + (1 - a_v) * v
    q = rms_norm(q, qn_g)
    k = rms_norm(k, kn_g)
    log_f = jax.nn.log_sigmoid((f_logit + forget_b).astype(jnp.float32))
    cum = jnp.cumsum(log_f, axis=1)
    o = fox_attention(q, k, v, cum)
    o = rms_norm(o, on_g) * jax.nn.sigmoid(heads(g))
    return o.reshape(B, T, FOX_WIDTH)

def wkv7_scan(r, w, k, v, a, b):
    B, T, H, N = r.shape

    def step(S, inp):
        r_t, w_t, k_t, v_t, a_t, b_t = inp
        Sa = jnp.einsum('bhij,bhj->bhi', S, a_t)
        S = S * w_t[:, :, None, :] + Sa[..., None] * b_t[:, :, None, :] + v_t[..., None] * k_t[:, :, None, :]
        return S, jnp.einsum('bhij,bhj->bhi', S, r_t)

    xs = tuple(t.transpose(1, 0, 2, 3) for t in (r, w, k, v, a, b))
    S0 = jnp.zeros((B, H, N, N), jnp.float32)
    _, ys = lax.scan(step, S0, xs)
    return ys.transpose(1, 0, 2, 3)

def rwkv7_mixer(zr, mu, w0, decay_up, a0, iclr_up, gate_up, k_k, k_a, r_k, lnx_g, lnx_b):
    B, T, _ = zr.shape
    f32 = jnp.float32
    zr = zr + mu * (shift_prev(zr) - zr)
    r, k, v, wd, ad, gd = split_cols(zr, RWKV_SPLITS)
    w_log = -jax.nn.softplus(-(w0 + jnp.tanh(wd) @ decay_up).astype(f32)) - 0.5
    decay = jnp.exp(-jnp.exp(w_log))
    a = jax.nn.sigmoid((a0 + ad @ iclr_up).astype(f32))
    g = jax.nn.sigmoid(gd) @ gate_up
    heads = lambda t: t.astype(f32).reshape(B, T, RWKV_HEADS, HEAD_DIM_2)
    kk = heads(k * k_k)
    kk = kk / jnp.maximum(jnp.sqrt(jnp.sum(kk * kk, axis=-1, keepdims=True)), 1e-12)
    k = k.astype(f32) * (1 + (a - 1) * k_a.astype(f32))
    rh, kh, vh, ah, wh = heads(r), heads(k), heads(v), heads(a), heads(decay)
    o = wkv7_scan(rh, wh, kh, vh, -kk, kk * ah)
    mean = jnp.mean(o, axis=-1, keepdims=True)
    var = jnp.mean(jnp.square(o - mean), axis=-1, keepdims=True)
    o = (o - mean) * lax.rsqrt(var + LNX_EPS)
    o = o * lnx_g.astype(f32).reshape(RWKV_HEADS, HEAD_DIM_2) + lnx_b.astype(f32).reshape(RWKV_HEADS, HEAD_DIM_2)
    o = o + jnp.sum(rh * kh * r_k.astype(f32), axis=-1, keepdims=True) * vh
    return (o.reshape(B, T, RWKV_WIDTH) * g.astype(f32)).astype(zr.dtype)

def routed_experts(h, idx, wts, w_gate, w_up, w_down):
    n_tok, d = h.shape
    n_assign = n_tok * TOP_K
    flat_e = idx.reshape(-1).astype(jnp.int32)
    order = jnp.argsort(flat_e)
    sorted_e = flat_e[order]
    counts = jnp.bincount(flat_e, length=N_EXPERTS).astype(jnp.int32)
    padded = (counts + EXPERT_BLOCK - 1) // EXPERT_BLOCK * EXPERT_BLOCK
    pad_end = jnp.cumsum(padded)
    pad_start = pad_end - padded
    grp_start = jnp.cumsum(counts) - counts
    dest = pad_start[sorted_e] + jnp.arange(n_assign, dtype=jnp.int32) - grp_start[sorted_e]
    n_blocks = -(-n_assign // EXPERT_BLOCK) + N_EXPERTS
    n_rows = n_blocks * EXPERT_BLOCK
    row_tok = jnp.zeros((n_rows,), jnp.int32).at[dest].set((order // TOP_K).astype(jnp.int32))
    row_w = jnp.zeros((n_rows,), wts.dtype).at[dest].set(wts.reshape(-1)[order])
    blk_start = jnp.arange(n_blocks, dtype=pad_end.dtype) * EXPERT_BLOCK
    blk_e = jnp.minimum(jnp.searchsorted(pad_end, blk_start, side='right'), N_EXPERTS - 1)

    def block(args):
        tok, w, e = args
        y = swiglu(h[tok], w_gate[e], w_up[e], w_down[e])
        return y * w[:, None]

    ys = lax.map(block, (row_tok.reshape(n_blocks, EXPERT_BLOCK), row_w.reshape(n_blocks, EXPERT_BLOCK), blk_e))
    return jax.ops.segment_sum(ys.reshape(n_rows, d), row_tok, num_segments=n_tok)

def moe_ffn(h, router_w, router_bias, w_gate, w_up, w_down, sw_gate, sw_up, sw_down):
    B, T, D = h.shape
    hf = h.reshape(B * T, D)
    n = hf.shape[0]
    scores = jax.nn.sigmoid((hf @ router_w).astype(jnp.float32))
    sel = scores + router_bias.astype(jnp.float32)
    grp = sel.reshape(n, N_GROUPS, N_EXPERTS // N_GROUPS)
    grp_score = jnp.sum(lax.top_k(grp, 2)[0], axis=-1)
    _, top_g = lax.top_k(grp_score, TOPK_GROUPS)
    gmask = jnp.any(top_g[..., None] == jnp.arange(N_GROUPS), axis=-2)
    emask = jnp.repeat(gmask, N_EXPERTS // N_GROUPS, axis=-1)
    _, idx = lax.top_k(jnp.where(emask, sel, -jnp.inf), TOP_K)
    wts = jnp.take_along_axis(scores, idx, axis=-1)
    wts = wts / jnp.sum(wts, axis=-1, keepdims=True) * ROUTED_SCALE
    routed = routed_experts(hf, idx, wts.astype(h.dtype), w_gate, w_up, w_down)
    shared = swiglu(hf, sw_gate, sw_up, sw_down)
    return (routed + shared).reshape(B, T, D)

def second_inputs(seed: int = 0) -> dict:
    key = jax.random.key(seed)
    ks = iter(jax.random.split(key, 40))
    nrm = lambda shape, s: jax.random.normal(next(ks), shape, jnp.float32) * s
    gain = lambda shape: 1.0 + nrm(shape, 0.02)
    L, D = DEPTH_2, D_MODEL
    return {
        "x": nrm((BATCH, SEQ, D), 1.0),
        "c": nrm((BATCH, D), 1.0),
        "norm1_g": gain((L, D)),
        "norm2_g": gain((L, D)),
        "ada_w": nrm((L, D, 6 * D), 0.5 * D ** -0.5),
        "ada_b": nrm((L, 6 * D), 0.02),
        "w_in": nrm((L, D, D_IN_PROJ), D ** -0.5),
        "w_out": nrm((L, D_MIX, D), D_MIX ** -0.5),
        "fox_qn_g": gain((L, FOX_HEADS, HEAD_DIM_2)),
        "fox_kn_g": gain((L, FOX_HEADS, HEAD_DIM_2)),
        "fox_on_g": gain((L, FOX_HEADS, HEAD_DIM_2)),
        "fox_forget_b": FORGET_BIAS_MEAN + nrm((L, FOX_HEADS), 0.5),
        "rw_mu": jax.random.uniform(next(ks), (L, RWKV_COLS), jnp.float32),
        "rw_w0": jax.random.uniform(next(ks), (L, RWKV_WIDTH), jnp.float32, -6.0, -1.0),
        "rw_decay_up": nrm((L, DECAY_LORA, RWKV_WIDTH), 0.1 * DECAY_LORA ** -0.5),
        "rw_a0": nrm((L, RWKV_WIDTH), 0.1),
        "rw_iclr_up": nrm((L, ICLR_LORA, RWKV_WIDTH), 0.1 * ICLR_LORA ** -0.5),
        "rw_gate_up": nrm((L, GATE_LORA, RWKV_WIDTH), GATE_LORA ** -0.5),
        "rw_k_k": 0.85 + nrm((L, RWKV_WIDTH), 0.05),
        "rw_k_a": 1.0 + nrm((L, RWKV_WIDTH), 0.05),
        "rw_r_k": nrm((L, RWKV_HEADS, HEAD_DIM_2), 0.1),
        "rw_lnx_g": gain((L, RWKV_WIDTH)),
        "rw_lnx_b": nrm((L, RWKV_WIDTH), 0.02),
        "router_w": nrm((L, D, N_EXPERTS), D ** -0.5),
        "router_bias": nrm((L, N_EXPERTS), 0.01),
        "exp_w_gate": nrm((L, N_EXPERTS, D, D_EXPERT), D ** -0.5),
        "exp_w_up": nrm((L, N_EXPERTS, D, D_EXPERT), D ** -0.5),
        "exp_w_down": nrm((L, N_EXPERTS, D_EXPERT, D), D_EXPERT ** -0.5),
        "sh_w_gate": nrm((L, D, D_SHARED), D ** -0.5),
        "sh_w_up": nrm((L, D, D_SHARED), D ** -0.5),
        "sh_w_down": nrm((L, D_SHARED, D), D_SHARED ** -0.5),
        "final_g": gain((D,)),
    }

def second_block(x, c, norm1_g, norm2_g, ada_w, ada_b, w_in, w_out,
              fox_qn_g, fox_kn_g, fox_on_g, fox_forget_b,
              rw_mu, rw_w0, rw_decay_up, rw_a0, rw_iclr_up, rw_gate_up, rw_k_k, rw_k_a, rw_r_k, rw_lnx_g, rw_lnx_b,
              router_w, router_bias, exp_w_gate, exp_w_up, exp_w_down, sh_w_gate, sh_w_up, sh_w_down, final_g):
    for l in range(DEPTH_2):
        mod = jax.nn.silu(c) @ ada_w[l] + ada_b[l]
        sh1, sc1, g1, sh2, sc2, g2 = jnp.split(mod[:, None, :], 6, axis=-1)
        h = rms_norm(x, norm1_g[l]) * (1 + sc1) + sh1
        z = h @ w_in[l]
        y_fox = fox_mixer(z[..., :FOX_COLS], fox_qn_g[l], fox_kn_g[l], fox_on_g[l], fox_forget_b[l])
        y_rwkv = rwkv7_mixer(z[..., FOX_COLS:], rw_mu[l], rw_w0[l], rw_decay_up[l], rw_a0[l], rw_iclr_up[l],
                             rw_gate_up[l], rw_k_k[l], rw_k_a[l], rw_r_k[l], rw_lnx_g[l], rw_lnx_b[l])
        x = x + g1 * (jnp.concatenate([y_fox, y_rwkv], axis=-1) @ w_out[l])
        h = rms_norm(x, norm2_g[l]) * (1 + sc2) + sh2
        x = x + g2 * moe_ffn(h, router_w[l], router_bias[l], exp_w_gate[l], exp_w_up[l], exp_w_down[l],
                             sh_w_gate[l], sh_w_up[l], sh_w_down[l])
    return rms_norm(x, final_g)


def setup_inputs(seed=0):
    out = dict(first_inputs(seed))
    for name, value in second_inputs(seed + 1).items():
        if name != "x":
            out[name + "_2"] = value
    return out


def reference(
    x, a_norm_g, a_w_in, a_v_norm_g, a_w_s, a_b_s, a_w_out, kv_norm_g, w_kv, b_norm_g, b_w_q,
    b_rel_bias, b_w_o, f_norm_g, f_w_in, f_conv_w, f_conv_b, f_w_down, final_norm_g, c_2,
    norm1_g_2, norm2_g_2, ada_w_2, ada_b_2, w_in_2, w_out_2, fox_qn_g_2, fox_kn_g_2, fox_on_g_2,
    fox_forget_b_2, rw_mu_2, rw_w0_2, rw_decay_up_2, rw_a0_2, rw_iclr_up_2, rw_gate_up_2,
    rw_k_k_2, rw_k_a_2, rw_r_k_2, rw_lnx_g_2, rw_lnx_b_2, router_w_2, router_bias_2,
    exp_w_gate_2, exp_w_up_2, exp_w_down_2, sh_w_gate_2, sh_w_up_2, sh_w_down_2, final_g_2,
):
    x = first_block(
        x, a_norm_g, a_w_in, a_v_norm_g, a_w_s, a_b_s, a_w_out, kv_norm_g, w_kv, b_norm_g,
        b_w_q, b_rel_bias, b_w_o, f_norm_g, f_w_in, f_conv_w, f_conv_b, f_w_down, final_norm_g,
    )
    return second_block(
        x, c_2, norm1_g_2, norm2_g_2, ada_w_2, ada_b_2, w_in_2, w_out_2, fox_qn_g_2, fox_kn_g_2,
        fox_on_g_2, fox_forget_b_2, rw_mu_2, rw_w0_2, rw_decay_up_2, rw_a0_2, rw_iclr_up_2,
        rw_gate_up_2, rw_k_k_2, rw_k_a_2, rw_r_k_2, rw_lnx_g_2, rw_lnx_b_2, router_w_2,
        router_bias_2, exp_w_gate_2, exp_w_up_2, exp_w_down_2, sh_w_gate_2, sh_w_up_2,
        sh_w_down_2, final_g_2,
    )


_drawn_inputs = setup_inputs


def setup_inputs(seed=0):
    import zlib

    import numpy as np

    out = dict(_drawn_inputs(seed))
    spreads = {}
    factors = {'kv_norm_g': 3.061,
     'b_norm_g': 5.455,
     'norm1_g_2': 3.347,
     'fox_qn_g_2': 7.299,
     'fox_kn_g_2': 8.0,
     'fox_on_g_2': 18.885,
     'rw_decay_up_2': 8.0,
     'rw_a0_2': 3.077,
     'rw_iclr_up_2': 3.083,
     'rw_lnx_g_2': 21.804,
     'rw_lnx_b_2': 24.329,
     'final_g_2': 7.917,
     'norm2_g_2': 3.243}
    for name, (base, spread) in spreads.items():
        noise = np.random.default_rng([zlib.crc32(name.encode()), seed]).standard_normal(out[name].shape)
        drawn = base * np.exp(spread * noise) if base else spread * noise
        out[name] = __import__('jax').numpy.asarray(drawn.astype(out[name].dtype))
    for name, factor in factors.items():
        out[name] = (out[name] * factor).astype(out[name].dtype)
    return out
```

```python
from contextlib import ExitStack

import concourse.bass as bass
from concourse import mybir

ALU = mybir.AluOpType
ACT = mybir.ActivationFunctionType
AX = mybir.AxisListType
F32 = mybir.dt.float32
U32 = mybir.dt.uint32

P = 128
D = 1024
KB = D // P
T = 512
TT = T // P
FF = 2816
FB = FF // P
PAIRS = 8
HD = 64
EPS = 1e-6
NEG = -1e30
REL = 257
RELW = 384
RW = 2072
E_DECAY = 0.6065306597126334

C_A, C_KV, C_B, C_F, C_FIN, C_N1, C_N2, C_FIN2, C_ADAB, C_VN = 0, 8, 16, 24, 40, 48, 56, 64, 72, 120
C_CONV = 128
C5 = 640
C_C, C_QN, C_KN, C_ON, C_W0, C_A0, C_KK, C_KA, C_RK, C_LG, C_LB, C_MU = [
    C5 + n for n in (0, 8, 12, 16, 20, 24, 28, 32, 36, 40, 44, 48)]
PARAM_ROWS = (128, 88, 88, 88, 88, 63)


def wait(eng, sem, count):
    if not isinstance(count, int) or count > 0:
        eng.wait_ge(sem, count)


class Order:

    def __init__(self, eng, sem, consts=None):
        self.eng, self.sem, self.n, self.off, self.consts = eng, sem, 0, 0, consts

    def __call__(self, ins):
        self.n += 1
        ins.then_inc(self.sem, 1)
        self.eng.wait_ge(self.sem, self.n + self.off)
        if not isinstance(self.off, int):
            self.eng.wait_ge(*self.consts)

    def round(self, i, steps):
        assert self.n in (0, steps), self.n
        self.n, self.off = 0, i * steps


def looped(eng, n, body):
    body(0, True)
    if n == 2:
        body(1, False)
    elif n > 2:
        with eng.Fori(1, n) as i:
            body(i, False)


def program(nc, a, out):
    with ExitStack() as ctx:
        def sb(name, *shape, dt=F32):
            return ctx.enter_context(nc.sbuf_tensor(name, list(shape), dt))

        def sem(name):
            return ctx.enter_context(nc.semaphore(name))

        def scratch(name, *shape):
            return nc.dram_tensor(name, list(shape), F32, kind="Internal").ap()

        ps = [ctx.enter_context(nc.psum_tensor(f"bank{i}", [P, 512], F32)) for i in range(8)]

        xT = sb("xT", P, KB, T)
        hT = sb("hT", P, KB, T)
        two = sb("two", P, 2 * KB * T)
        gT = two[:, 0:KB * T].rearrange("p (b t) -> p b t", b=KB)
        yT = sb("yT", P, KB, T)
        sq = sb("sq", P, KB, T)
        big = sb("big", P, FB * T)
        ring = sb("ring", P, 2, FB * P)
        prow = sb("prow", P, 6, P)
        col = sb("col", P, 6 * P)
        ident = sb("ident", P, P)
        mean = sb("mean", P, P)
        rstd = sb("rstd", P, T)
        rms = sb("rms", P, T)
        epsc = sb("epsc", P, 1)
        mod = sb("mod", P, 48)
        csil = sb("csil", P, 8)
        ss4 = sb("ss4", P, 16)
        biasT = two[:, KB * T:].rearrange("p (h k) -> p h k", h=16)
        small = sb("small", P, 64)
        relE, relR = sb("relE", 16, RELW), sb("relR", 16, RELW)
        rel_dram = scratch("rel_dram", 16, P, RELW + 1)

        x_tok = sq[:].rearrange("p b t -> p (b t)").rearrange("p (t d) -> p t d", t=TT)
        act = big[:].rearrange("p (b t) -> p b t", b=FB)
        vtok = big[:, 0:4096].rearrange("p (t d) -> p t d", t=TT)
        wsraw = big[:, 4096:5120].rearrange("p (g j) -> p g j", g=8)
        wsT = big[:, 5120:6144].rearrange("p (g j) -> p g j", g=8)
        bsb = big[:, 6144:7168].rearrange("p (g j) -> p g j", g=8)
        sptmp = big[:, 7168:7680]
        ffw = sb("ffw", P, 6 * T)
        conv = [[ffw[:, (2 * j + b) * T:(2 * j + b + 1) * T] for b in range(2)] for j in range(2)]
        sil = [ffw[:, (4 + j) * T:(5 + j) * T] for j in range(2)]

        def carve(start, *shapes):
            got, at = [], start
            for s in shapes:
                n = s if isinstance(s, int) else s[0] * s[1]
                t = big[:, at:at + n]
                got.append(t if isinstance(s, int) else t.rearrange("p (a b) -> p a b", a=s[0]))
                at += n
            assert at <= FB * T, at
            return got

        qT, kT, vt, s_sb, p_sb, pT, o_sb, negm, rsum, mx, rinv = carve(
            0, 512, 512, (4, 128), (2, 512), (2, 512), (2, 512), 512, 8, 8, 8, 8)

        kpad, vpad, qraw, akb, avb, sqq, sqk, gsig = carve_from = carve(
            5696, 520, 520, 512, 512, 512, 512, 512, 512)
        ckb = two[:, 0:1024].rearrange("p (h t) -> p h t", h=2)
        sig24 = two[0:24, 1024:1536]
        fx8 = [two[0:8, 2048 + 512 * n:2560 + 512 * n] for n in range(4)]
        rq, rk, oraw, kmix, vmix = [two[:, 4096 + 512 * n:4608 + 512 * n] for n in range(5)]
        cq = small[:, 0:32].rearrange("p (t h) -> p t h", t=TT)
        gmod = small[:, 32:48]
        qn8 = small[:, 48:52]
        favw = sb("favw", P, KB, 24)
        fbias = sb("fbias", 8, 1)
        ones8 = sb("ones8", 8, T)
        tri = sb("tri", P, P)
        bdiag = sb("bdiag", P, P)
        halfm = sb("halfm", P, P)
        maskAR = sb("maskAR", P, 256)
        mask1 = sb("mask1", P, P)
        maskT = [sb(f"maskT{n}", P, P) for n in range(6)]
        cmask = sb("cmask", P, T)
        onec = sb("onec", P, 1)
        lnxe = sb("lnxe", P, 1)
        sig_dram, cum_dram = scratch("sig_dram", 16, T), scratch("cum_dram", 8, T)

        rp, kp, vp, dd, rr, k0, vv, ld, aa, gg, Lc, Pt, Pinv, Pprev, kkn, sqr, nrm, BT, KT, AR_ = carve(
            0, *[520] * 3, *[512] * 16, 1024)
        AR = AR_.rearrange("p (t w c) -> p t w c", t=TT, w=2)
        tokA, tokB, tokK, tokV, Gm, ApT, Wm, Usb = [two[:, 512 * n:512 * n + 512] for n in range(8)]
        tiles4 = lambda x: x.rearrange("p (t c) -> p t c", t=TT)
        tokA, tokB, tokK, tokV, Gm, Wm, Usb = map(tiles4, (tokA, tokB, tokK, tokV, Gm, Wm, Usb))
        ABT = [two[:, 4096 + 1024 * h:5120 + 1024 * h].rearrange("p (t c) -> p t c", t=TT) for h in range(2)]
        AKT = [two[:, 6144 + 1024 * h:7168 + 1024 * h].rearrange("p (t c) -> p t c", t=TT) for h in range(2)]
        sqf = sq[:].rearrange("p b t -> p (b t)")
        Dm, DT, Xm = [[tiles4(sqf[:, 1024 * n + 512 * h:1024 * n + 512 * h + 512]) for h in range(2)] for n in range(3)]
        Zs = sqf[:, 3072:4096].rearrange("p (c n) -> p c n", c=8)
        Am = [tiles4(ffw[:, 512 * h:512 * h + 512]) for h in range(2)]
        ztmp = ffw[:, 1024:1152]
        y_sb, y_sq = ffw[:, 2048:2560], ffw[:, 2560:3072]
        st8 = ss4
        lwa, lg0 = rms[:], rstd[:]
        lg1 = prow[0:32, 0:4, :].rearrange("p a b -> p (a b)")

        rwt = sb("rwt", P, KB, 64)
        rbias = sb("rbias", P, 64)
        cm8 = sb("cm8", P, 32)
        exw = [big[:, 0:6144], two[:, 0:6144]]
        w_dram = scratch("w_dram", 64, T)
        rt = two[:, 6144:8192]
        r4 = lambda n, w: rt[:, n:n + 4 * w].rearrange("p (t e) -> p t e", t=TT)
        sco, sel, eqm, pos, wtok = [r4(256 * n, 64) for n in range(5)]
        srt = rt[:, 1280:1536].rearrange("p (u e) -> p u e", e=8)
        gsc, gsrt, gmask, geq, gpos, esrt = [r4(1536 + 32 * n, 8) for n in range(6)]
        room, wsum = r4(1728, 1), r4(1732, 1)
        wT = rt[0:64, 0:512]
        wbc = [sqf[:, 512 * n:512 * n + 512] for n in range(2)]
        xact = [sqf[:, 1024 + 1024 * n:2048 + 1024 * n].rearrange("p (b t) -> p b t", b=2) for n in range(2)]
        xsil = sqf[:, 3072:4096].rearrange("p (b t) -> p b t", b=2)
        out_tok = sqf.rearrange("p (t d) -> p t d", t=TT)

        S = {}
        bc4 = lambda m: m.unsqueeze(1).to_broadcast([P, TT, P])

        def s(name):
            if name not in S:
                S[name] = sem(name)
            return S[name]

        for n in ("ring0_loaded", "ring1_loaded", "ff_prod", "exp0_loaded", "exp1_loaded", "wbc0_loaded",
                  "wbc1_loaded", "exp_act", "exp_raw", "x_loaded", "rw_y_ready", "exp_down", "out_ready",
                  "out_stored", "params_loaded", "pool_order", "consts", "pool_consts", "fav_loaded",
                  "rt_loaded", "ws_loaded", "bsb_loaded", "rel_loaded", "rel_ext", "rel_stored", "bias_loaded",
                  "fav_sig", "sig_stored", "cum_ready", "fx_mixed", "att_sc_added", "fx_rows", "rw_smt",
                  "rw_x", "rw_am", "wT_ready", "w_stored", "norm_sq_ready", "norm_ss_ready", "lin_added",
                  "norm_h_ready", "ff_tap0", "ff_act", "x_turned", "x_ready", "params_turned", "ws_masked",
                  "ws_turned", "c_silu", "mod_ready", "mod_prod", "ws_ready", "gv_taken", "norm_rms_ready",
                  "gv_prod", "gu_taken", "gu_prod", "vn_ready", "sp_prod", "gated", "qk_taken", "qkv_prod",
                  "o_ready", "att_sc_prod", "att_p_ready", "att_pt_taken", "att_pt_prod", "v_taken",
                  "att_o_norm", "att_av_prod", "att_ot_prod", "fav_prod", "cq_turned", "cq_ready", "fx_rms",
                  "fx_o_taken", "fx_prod", "fx_sq", "fx_ms", "fx_vturned", "fx_taken", "fx_qk", "lora_prod",
                  "lora_ready", "rw_prod", "rw_sq", "rw_ms", "rw_ops", "rw_taken", "rw_turned", "rw_nrm",
                  "rw_bonus", "rw_sm", "rw_tok", "rw_d0", "rw_dt", "rw_xt", "rw_dd", "rw_g", "rw_gt", "rw_zt",
                  "rw_u", "rw_ut", "rw_z", "rw_yprod", "rw_yn", "rw_yturned", "rt_prod", "w_ready", "w_turned",
                  "exp_gu", "exp_added", "out_turned", "act_order", "ff_tap2", "ff_silu", "col_ready",
                  "vrms_ready", "att_negm_ready", "f_abs", "f_log", "fx_y_ready", "pads", "lora_taken",
                  "lora_mixed", "rw_kk", "rw_L", "rw_P", "rw_yt", "rw_yc", "rw_ysq", "rw_yvar", "rw_ystd",
                  "rt_sig", "exp_sil", "dve_order", "lin_prod", "ff_tap1", "att_sc_max", "att_r_inv",
                  "fx_order", "rw_order", "moe_added"):
            s(n)
        NORMS = ["a", "f0", "att", "f1", "fin", "n1", "n2", "fin2"]
        nth = lambda n, h=False: NORMS.index(n) + 1 + (h and NORMS.index(n) >= 2)
        LINEARS = ["go", "f0dn", "wo", "f1dn", "w_out"]

        plan, steps, loads, before = {}, {}, [0, 0], None
        STAGES = [("ada", 24, 1, 1, "mod_prod", 1), ("gv", 4, 1, 1, "gv_prod", 4), ("gu", 4, 1, 1, "gu_prod", 2),
                  ("go", 4, 1, 1, "lin_prod", 2), ("f0in", 22, 2, 2, "ff_prod", 2), ("f0dn", 8, 1, 1, "lin_prod", 1),
                  ("att", 16, 2, 1, "qkv_prod", (2, 3)), ("wo", 4, 1, 1, "lin_prod", 2),
                  ("f1in", 22, 2, 2, "ff_prod", 2), ("f1dn", 8, 1, 1, "lin_prod", 1),
                  ("fx", 8, 2, 2, "fx_prod", 2), ("lora", 2, 1, 1, "lora_prod", (1, 3)),
                  ("rw", 8, 2, 5, "rw_prod", (2, 6)), ("w_out", 4, 1, 1, "lin_prod", 2)]
        for name, units, d0, d1, used, per in STAGES:
            plan[name] = (units, list(loads), (d0, d1), used, per, before, steps.get(used, 0))
            steps[used] = steps.get(used, 0) + (units // 2 * per[1] if isinstance(per, tuple) else units * per)
            loads[0] += 16 * d0 * units // 2
            loads[1] += 16 * d1 * units // 2
            before = name

        def steps_of(stage):
            per = plan[stage][4]
            return per if isinstance(per, tuple) else (per, 2 * per)

        def used_count(stage, m):
            odd, both = steps_of(stage)
            return plan[stage][6] + both * (m // 2) + odd * (m % 2)

        def ring_ready(eng, stage, i, j):
            _, base, d, *_ = plan[stage]
            wait(eng, (S["ring0_loaded"], S["ring1_loaded"])[j], base[j] + 16 * d[j] * (i + 1))

        def slot(j, k, n):
            return ring[:, j, 0:k * n].rearrange("p (k n) -> p k n", k=k)

        def wcols(w, c0, n):
            return w.rearrange("(k p) n -> p k n", p=P)[:, :, bass.ds(c0, n)]

        w_in, w_kv, w_q = a["a_w_in"][0], a["w_kv"], a["b_w_q"][0]

        def unit_loads(stage, i, j):
            u = 2 * i + j
            if stage == "ada":
                return [(slot(j, 8, 256), wcols(a["ada_w_2"][0], u * 256, 256))]
            if stage == "gv":
                return [(slot(j, 8, 256), wcols(w_in, D + u * 256, 256))]
            if stage == "gu":
                return [(slot(j, 8, 256), wcols(w_in, u * 256, 256))]
            if stage in ("go", "wo", "w_out"):
                w = {"go": a["a_w_out"][0], "wo": a["b_w_o"][0], "w_out": a["w_out_2"][0]}[stage]
                return [(slot(j, 8, 256), wcols(w, u * 256, 256))]
            if stage in ("f0in", "f1in"):
                w = a["f_w_in"][int(stage[1])]
                return [(slot(j, 8, 256)[:, :, b * P:(b + 1) * P], wcols(w, b * FF + u * P, P)) for b in range(2)]
            if stage in ("f0dn", "f1dn"):
                return [(slot(j, FB, P), wcols(a["f_w_down"][int(stage[1])], u * P, P))]
            if stage == "att":
                if j == 0:
                    return [(slot(0, 8, 256)[:, :, 0:P], wcols(w_q, i * P, P)),
                            (slot(0, 8, 256)[:, :, P:256], wcols(w_kv, i * P, P))]
                return [(slot(1, 8, P), wcols(w_kv, D + i * P, P))]
            w2 = a["w_in_2"][0]
            if stage == "fx":
                return [(slot(j, 8, 256)[:, :, b * P:(b + 1) * P], wcols(w2, (2 * j + b) * 512 + i * P, P))
                        for b in range(2)]
            if stage == "lora":
                return [(slot(j, 8, (P, 160)[j]), wcols(w2, (RW + 1536, RW + 1664)[j], (P, 160)[j]))]
            if stage == "rw":
                if j == 0:
                    return [(slot(0, 8, 256)[:, :, b * P:(b + 1) * P], wcols(w2, RW + b * 512 + i * P, P))
                            for b in range(2)]
                own = bass.ds(i * P, P)
                return [(slot(1, 8, P), wcols(w2, RW + 1024 + i * P, P)),
                        (ring[0:64, 1, 1024:1152], a["rw_decay_up_2"][0][:, own]),
                        (ring[64:128, 1, 1024:1152], a["rw_iclr_up_2"][0][:, own]),
                        (ring[:, 1, 1152:1280], a["rw_gate_up_2"][0][0:P, own]),
                        (ring[0:32, 1, 1280:1408], a["rw_gate_up_2"][0][P:160, own])]
            raise AssertionError(stage)

        block = ctx.enter_context(nc.Block())
        NCONST = 5
        NPARAM = 10 + 6 + 13

        def settle(eng, sem, count):
            wait(eng, sem, count)
            if not isinstance(count, int):
                eng.wait_ge(S["consts"], NCONST)

        @block.sync
        def _(sp):
            def stage_loads(stage):
                units, _, _, used, per, before, base = plan[stage]

                def load(i, first):
                    for j in range(2):
                        if first and before is not None:
                            sp.wait_ge(S[plan[before][3]], used_count(before, plan[before][0] - 1 + j))
                        elif not first:
                            even, both = steps_of(stage)
                            sp.wait_ge(S[used], both * i + base - (both - even if j == 0 else 0))
                        for dst, src in unit_loads(stage, i, j):
                            sp.dma_start(dst, src).then_inc(S[f"ring{j}_loaded"], 16)
                looped(sp, units // 2, load)

            sp.dma_start(x_tok, a["x"][0].rearrange("(t p) d -> p t d", p=P)).then_inc(s("x_loaded"), 16)
            for name, *_ in STAGES:
                stage_loads(name)

            def expert_loads(par, wg, wu, wd):
                w = exw[par]
                for k, src in ((0, wg), (2048, wu)):
                    sp.dma_start(w[:, k:k + 2048].rearrange("p (k n) -> p k n", k=KB),
                                 src.rearrange("(k p) n -> p k n", p=P)).then_inc(s(f"exp{par}_loaded"), 16)
                sp.dma_start(w[:, 4096:6144].rearrange("p (k n) -> p k n", k=2),
                             wd.rearrange("(k p) n -> p k n", p=P)).then_inc(s(f"exp{par}_loaded"), 16)

            def experts(i, first):
                for par in range(2):
                    if first:
                        sp.wait_ge(s("rw_y_ready"), 4)
                    else:
                        sp.wait_ge(s("exp_down"), 16 * i + 8 * par - 8)
                    e = bass.ds(2 * i + par, 1)
                    one = lambda n: a[n][0][e].rearrange("o r c -> (o r) c")
                    expert_loads(par, one("exp_w_gate_2"), one("exp_w_up_2"), one("exp_w_down_2"))
            looped(sp, 32, experts)
            sp.wait_ge(s("exp_down"), 504)
            expert_loads(0, a["sh_w_gate_2"][0], a["sh_w_up_2"][0], a["sh_w_down_2"][0])
            sp.wait_ge(s("out_ready"), 8)
            sp.dma_start(out[0].rearrange("(t p) d -> p t d", p=P), out_tok).then_inc(s("out_stored"), 16)
            sp.wait_ge(s("out_stored"), 16)

        @block.gpsimd
        def _(pool):
            rows = lambda ap: ap.rearrange("(r c) -> r c", c=P)
            nload = 0

            def row_load(tile, r0, flat, n=None):
                nonlocal nload
                src = rows(flat)
                pool.dma_start(prow[r0:r0 + src.shape[0], tile, 0:P], src).then_inc(s("params_loaded"), 16)
                nload += 1

            pool.memset(prow[:, 5, :], 0.0).then_inc(s("pool_order"), 1)
            pool.memset(ident[:], 0.0).then_inc(s("pool_order"), 1)
            pool.memset(mean[:], 1.0 / D).then_inc(s("consts"), 1)
            pool.memset(epsc[:], EPS).then_inc(s("consts"), 1)
            pool.wait_ge(s("pool_order"), 2)
            pool.affine_select(out=ident[:], in_=ident[:], compare_op=ALU.not_equal, fill=1.0, base=0,
                               pattern=[[-1, P]], channel_multiplier=1).then_inc(s("consts"), 1)
            porder = Order(pool, s("pool_consts"))
            porder(pool.memset(lnxe[:], 64e-5))
            porder(pool.memset(ones8[:], 1.0))
            porder(pool.memset(cmask[:], 1.0))
            porder(pool.memset(cmask[:].rearrange("p (c n) -> p c n", n=64)[:, :, 0:1], 0.0))
            porder(pool.memset(cm8[:], 1.0))
            porder(pool.memset(cm8[:].rearrange("p (c n) -> p c n", n=8)[:, :, 0:1], 0.0))
            porder(pool.memset(tri[:], 0.0))
            porder(pool.affine_select(out=tri[:], in_=tri[:], compare_op=ALU.is_ge, fill=NEG, base=0,
                               pattern=[[-1, P]], channel_multiplier=1))
            for tile, v in ((bdiag, 1.0), (halfm, 1.0 / HD)):
                porder(pool.memset(tile[:], v))
                porder(pool.memset(tile[0:64, 64:128], 0.0))
                porder(pool.memset(tile[64:128, 0:64], 0.0))
            porder(pool.memset(maskAR[:], 1.0))
            for w, op in ((0, ALU.is_gt), (1, ALU.is_ge)):
                half = maskAR[:, w * P:(w + 1) * P]
                porder(pool.affine_select(out=half, in_=half, compare_op=op, fill=0.0, base=0,
                                          pattern=[[1, P]], channel_multiplier=-1))
                porder(pool.memset(maskAR[0:64, w * P + 64:(w + 1) * P], 0.0))
            porder(pool.memset(mask1[:], 0.0))
            view = mask1[:].rearrange("p (b w) -> p b w", w=2)
            porder(pool.memset(view[:, :, 0:1], 1.0))
            porder(pool.affine_select(out=view, in_=view, compare_op=ALU.is_equal, fill=0.0, base=-1,
                               pattern=[[-2, 64], [0, 2]], channel_multiplier=1))
            for n in range(6):
                w = 1 << n
                view = maskT[n][:].rearrange("p (b w c) -> p b w c", w=2, c=w)
                porder(pool.memset(maskT[n][:], 0.0))
                porder(pool.memset(view[:, :, 1:2, :], 1.0))
                porder(pool.affine_select(out=view, in_=view, compare_op=ALU.is_ge, fill=0.0, base=0,
                                          pattern=[[-2 * w, 64 // w], [0, 2], [0, w]], channel_multiplier=1))
                porder(pool.affine_select(out=view, in_=view, compare_op=ALU.is_ge, fill=0.0, base=w - 1,
                                   pattern=[[2 * w, 64 // w], [0, 2], [0, w]], channel_multiplier=-1))
            pool.memset(onec[:], 1.0).then_inc(s("consts"), 1)
            for r, ap in ((C_A, a["a_norm_g"][0]), (C_KV, a["kv_norm_g"]), (C_B, a["b_norm_g"][0]),
                          (C_F, a["f_norm_g"].rearrange("l d -> (l d)")), (C_FIN, a["final_norm_g"]),
                          (C_N1, a["norm1_g_2"][0]), (C_N2, a["norm2_g_2"][0]), (C_FIN2, a["final_g_2"]),
                          (C_ADAB, a["ada_b_2"][0]), (C_VN, a["a_v_norm_g"][0])):
                row_load(0, r, ap)
            for l in range(2):
                row_load(1 + 2 * l, 0, a["f_conv_w"][l, 0:2].rearrange("k c -> (k c)"))
                row_load(2 + 2 * l, 0, a["f_conv_w"][l, 2])
                row_load(2 + 2 * l, 44, a["f_conv_b"][l])
            mu = a["rw_mu_2"][0]
            for c, ap in ((C_C, a["c_2"][0]), (C_QN, a["fox_qn_g_2"][0].rearrange("h d -> (h d)")),
                          (C_KN, a["fox_kn_g_2"][0].rearrange("h d -> (h d)")),
                          (C_ON, a["fox_on_g_2"][0].rearrange("h d -> (h d)")), (C_W0, a["rw_w0_2"][0]),
                          (C_A0, a["rw_a0_2"][0]), (C_KK, a["rw_k_k_2"][0]), (C_KA, a["rw_k_a_2"][0]),
                          (C_RK, a["rw_r_k_2"][0].rearrange("h d -> (h d)")), (C_LG, a["rw_lnx_g_2"][0]),
                          (C_LB, a["rw_lnx_b_2"][0]), (C_MU, mu[0:14 * P])):
                row_load(5, c - C5, ap)
            pool.dma_start(prow[62:63, 5, 0:32], mu[14 * P:14 * P + 32].rearrange("(r c) -> r c", r=1))\
                .then_inc(s("params_loaded"), 16)
            nload += 1
            assert nload == NPARAM, nload
            pool.dma_start(favw[:], wcols(a["w_in_2"][0], 2048, 24)).then_inc(s("fav_loaded"), 16)
            pool.dma_start(fbias[:], a["fox_forget_b_2"][0].rearrange("(h o) -> h o", o=1)).then_inc(s("fav_loaded"), 16)
            pool.dma_start(rwt[:], a["router_w_2"][0].rearrange("(k p) n -> p k n", p=P)).then_inc(s("rt_loaded"), 16)
            pool.dma_start(rbias[:], a["router_bias_2"][0].partition_broadcast(P)).then_inc(s("rt_loaded"), 16)
            pool.dma_start(wsraw, a["a_w_s"][0].rearrange("g i j -> i g j")).then_inc(s("ws_loaded"), 16)
            pool.dma_start(bsb, a["a_b_s"][0].rearrange("g i -> (g i)").partition_broadcast(P)
                           .rearrange("p (g i) -> p g i", g=8)).then_inc(s("bsb_loaded"), 16)
            pool.dma_start(relE[:, 0:REL], a["b_rel_bias"][0]).then_inc(s("rel_loaded"), 16)
            pool.wait_ge(s("rel_ext"), 2)
            pool.dma_start(rel_dram[:, :, 0:RELW], relR[:].unsqueeze(1).to_broadcast([16, P, RELW]))\
                .then_inc(s("rel_stored"), 16)
            pool.wait_ge(s("rel_stored"), 16)
            pool.dma_start(biasT, bass.AP(rel_dram.tensor, 127, [[RELW, P], [P * (RELW + 1), 16], [1, 256]]))\
                .then_inc(s("bias_loaded"), 16)
            pool.wait_ge(s("bias_loaded"), 16)
            pool.memset(biasT[0:64, :, 192:256], NEG).then_inc(s("consts"), 1)
            pool.wait_ge(s("fav_sig"), 1)
            pool.dma_start(sig_dram, sig24[8:24, :]).then_inc(s("sig_stored"), 16)
            pool.wait_ge(s("cum_ready"), 1)
            pool.dma_start(cum_dram, fx8[3]).then_inc(s("sig_stored"), 16)
            pool.wait_ge(s("sig_stored"), 32)

            def fox_rows(i, first):
                if not first:
                    settle(pool, s("fx_mixed"), 2 * i)
                    settle(pool, s("att_sc_added"), 64 + 8 * i)
                for h in range(2):
                    for n, dst in enumerate((akb, avb)):
                        pool.dma_start(dst[64 * h:64 * h + 64, :],
                                       sig_dram[bass.ds(8 * n + 2 * i + h, 1), :].rearrange("o t -> (o t)")
                                       .partition_broadcast(64)).then_inc(s("fx_rows"), 16)
                pool.dma_start(ckb, cum_dram[bass.ds(2 * i, 2), :].partition_broadcast(P)).then_inc(s("fx_rows"), 16)
            looped(pool, 4, fox_rows)

            def level_masks(i, first):
                for n in range(1, 6):
                    for h in range(2):
                        k = 2 * (n - 1) + h
                        if n == 1:
                            settle(pool, s("rw_smt"), 10 * i + 5 * h + 5)
                        else:
                            settle(pool, s("rw_x"), 10 * i + k - 1)
                        nc.gpsimd.tensor_tensor(Am[h], ABT[h][:, :, 0:P], bc4(maskT[n][:]), ALU.mult)\
                            .then_inc(s("rw_am"), 1)
            looped(pool, 4, level_masks)

            pool.wait_ge(s("wT_ready"), 1)
            pool.dma_start(w_dram, wT).then_inc(s("w_stored"), 16)
            pool.wait_ge(s("w_stored"), 16)

            def weight_rows(i, first):
                for par in range(2):
                    if not first:
                        settle(pool, s("exp_act"), 4 * i + 2 * par - 2)
                    pool.dma_start(wbc[par], w_dram[bass.ds(2 * i + par, 1), :].rearrange("o t -> (o t)")
                                   .partition_broadcast(P)).then_inc(s(f"wbc{par}_loaded"), 16)
            looped(pool, 32, weight_rows)

        @block.tensor
        def _(pe):
            def mean_squares(n):
                pe.wait_ge(s("norm_sq_ready"), nth(n))
                for b in range(KB):
                    mm = pe.matmul(ps[7][:], mean[:], sq[:, b, :], start=(b == 0), stop=(b == KB - 1))
                mm.then_inc(s("norm_ss_ready"), 1)

            def linear(stage, rhs, kb, banks):
                units, _, _, used, per, _, base = plan[stage]
                for u in range(units):
                    ring_ready(pe, stage, u // 2, u % 2)
                    w = slot(u % 2, kb, per * P)
                    for b in range(per):
                        n = per * u + b
                        if n >= banks:
                            pe.wait_ge(s("lin_added"), base + n - banks + 1)
                        for k in range(kb):
                            mm = pe.matmul(ps[n % banks][:], w[:, k, b * P:(b + 1) * P], rhs[:, k, :],
                                           start=(k == 0), stop=(k == kb - 1))
                        mm.then_inc(S[used], 1)

            def feed_forward(l):
                stage = f"f{l}in"
                pe.wait_ge(s("norm_h_ready"), nth(f"f{l}", True))

                def body(i, first):
                    for j in range(2):
                        ring_ready(pe, stage, i, j)
                        w = slot(j, 8, 256)
                        for b in range(2):
                            if not first:
                                pe.wait_ge(s("ff_tap0"), 44 * l + 4 * i + 2 * j + b - 3)
                            for k in range(KB):
                                mm = pe.matmul(ps[2 * j + b][:], w[:, k, b * P:(b + 1) * P], hT[:, k, :],
                                               start=(k == 0), stop=(k == KB - 1))
                            mm.then_inc(s("ff_prod"), 1)
                looped(pe, FB // 2, body)
                pe.wait_ge(s("ff_act"), (l + 1) * FB)
                linear(f"f{l}dn", act, FB, 4)

            pe.wait_ge(s("consts"), 3)
            pe.wait_ge(s("x_loaded"), 16)
            for b in range(KB):
                for t in range(TT):
                    tr = pe.transpose(ps[b][:, t * P:(t + 1) * P], x_tok[:, t, b * P:(b + 1) * P], ident[:])
                tr.then_inc(s("x_turned"), 1)
            pe.wait_ge(s("params_loaded"), 16 * NPARAM)
            for t, rows in enumerate(PARAM_ROWS):
                wait(pe, s("x_ready"), t + 1)
                pe.transpose(ps[t][:, 0:rows], prow[0:rows, t, :], ident[0:rows, 0:rows])\
                    .then_inc(s("params_turned"), 1)
            pe.wait_ge(s("x_ready"), KB)
            pe.wait_ge(s("ws_masked"), 1)
            for g in range(8):
                tr = pe.transpose(ps[6 + g // 4][:, (g % 4) * P:(g % 4 + 1) * P], wsraw[:, g, :], ident[:])
            tr.then_inc(s("ws_turned"), 1)

            pe.wait_ge(s("c_silu"), 1)

            def ada(i, first):
                for j in range(2):
                    ring_ready(pe, "ada", i, j)
                    if not first:
                        pe.wait_ge(s("mod_ready"), 2 * i + j - 1)
                    for b in range(2):
                        for k in range(KB):
                            mm = pe.matmul(ps[j][:, b:b + 1], slot(j, 8, 256)[:, k, b * P:(b + 1) * P],
                                           csil[:, k:k + 1], start=(k == 0), stop=(k == KB - 1))
                    mm.then_inc(s("mod_prod"), 1)
            looped(pe, 12, ada)

            mean_squares("a")
            pe.wait_ge(s("norm_h_ready"), nth("a", True))
            pe.wait_ge(s("mod_ready"), 24)
            pe.wait_ge(s("ws_ready"), 1)
            for u in range(4):
                ring_ready(pe, "gv", u // 2, u % 2)
                for t in range(TT):
                    wait(pe, s("gv_taken"), 4 * (u - 2) + t + 1)
                    if u == 1 and t == 3:
                        pe.wait_ge(s("norm_rms_ready"), nth("a"))
                    for k in range(KB):
                        mm = pe.matmul(ps[4 * (u % 2) + t][:, 0:256], hT[:, k, t * P:(t + 1) * P],
                                       slot(u % 2, 8, 256)[:, k, :], start=(k == 0), stop=(k == KB - 1))
                    mm.then_inc(s("gv_prod"), 1)
            pe.wait_ge(s("gv_taken"), 16)
            for u in range(4):
                ring_ready(pe, "gu", u // 2, u % 2)
                for b in range(2):
                    n = 2 * u + b
                    wait(pe, s("gu_taken"), n - 3)
                    for k in range(KB):
                        mm = pe.matmul(ps[n % 4][:], slot(u % 2, 8, 256)[:, k, b * P:(b + 1) * P], hT[:, k, :],
                                       start=(k == 0), stop=(k == KB - 1))
                    mm.then_inc(s("gu_prod"), 1)
            pe.wait_ge(s("vn_ready"), 4)
            for g in range(8):
                if g < 4:
                    bank = 4 + g
                else:
                    bank = g - 4
                    pe.wait_ge(s("gu_taken"), 8)
                for n in range(TT):
                    mm = pe.matmul(ps[bank][:, n * P:(n + 1) * P], vtok[:, n, g * P:(g + 1) * P], wsT[:, g, :],
                                   start=True, stop=True)
                mm.then_inc(s("sp_prod"), 1)
            pe.wait_ge(s("gated"), 8)
            linear("go", gT, KB, 4)
            mean_squares("f0")
            feed_forward(0)

            mean_squares("att")
            pe.wait_ge(s("norm_h_ready"), nth("att", True))

            def pair(i, first):
                attention_projections(i, first)
                pe.wait_ge(s("qk_taken"), 2 * i + 2)
                attention_core(i, first)

            def attention_projections(i, first):
                ring_ready(pe, "att", i, 0)
                for b in range(2):
                    src = (hT, gT)[b]
                    for k in range(KB):
                        mm = pe.matmul(ps[b][:], slot(0, 8, 256)[:, k, b * P:(b + 1) * P], src[:, k, :],
                                       start=(k == 0), stop=(k == KB - 1))
                    mm.then_inc(s("qkv_prod"), 1)
                ring_ready(pe, "att", i, 1)
                if not first:
                    pe.wait_ge(s("o_ready"), i)
                for t in range(TT):
                    for k in range(KB):
                        mm = pe.matmul(ps[2][:, t * P:(t + 1) * P], gT[:, k, t * P:(t + 1) * P],
                                       slot(1, 8, P)[:, k, :], start=(k == 0), stop=(k == KB - 1))
                mm.then_inc(s("qkv_prod"), 1)

            def attention_core(i, first):

                def scores(u):
                    h, qt = u // TT, u % TT
                    if not (first and u < 2):
                        pe.wait_ge(s("att_sc_added"), 8 * i + u - 1)
                    pe.matmul(ps[3 + u % 2][:, 0:(qt + 1) * P], qT[64 * h:64 * h + 64, qt * P:(qt + 1) * P],
                              kT[64 * h:64 * h + 64, 0:(qt + 1) * P], start=True, stop=True).then_inc(s("att_sc_prod"), 1)

                def turn(u):
                    pe.wait_ge(s("att_p_ready"), 8 * i + u + 1)
                    if not (first and u < 2):
                        pe.wait_ge(s("att_pt_taken"), 8 * i + u - 1)
                    for b in range(u % TT + 1):
                        tr = pe.transpose(ps[5 + u % 2][:, b * P:(b + 1) * P],
                                          p_sb[:, u % 2, b * P:(b + 1) * P], ident[:])
                    tr.then_inc(s("att_pt_prod"), 1)

                def values(u):
                    h, qt = u // TT, u % TT
                    pe.wait_ge(s("att_pt_taken"), 8 * i + u + 1)
                    if u == 0:
                        pe.wait_ge(s("v_taken"), i + 1)
                        if not first:
                            pe.wait_ge(s("att_o_norm"), i)
                    for b in range(qt + 1):
                        mm = pe.matmul(ps[7][:, qt * P + 64 * h:qt * P + 64 * h + 64],
                                       pT[:, u % 2, b * P:(b + 1) * P], vt[:, b, 64 * h:64 * h + 64],
                                       start=(b == 0), stop=(b == qt))
                    mm.then_inc(s("att_av_prod"), 1)

                scores(0)
                scores(1)
                for u in range(8):
                    turn(u)
                    if u + 2 < 8:
                        scores(u + 2)
                    if u >= 1:
                        values(u - 1)
                values(7)
                pe.wait_ge(s("att_o_norm"), i + 1)
                for t in range(TT):
                    tr = pe.transpose(ps[2][:, t * P:(t + 1) * P], o_sb[:, t * P:(t + 1) * P], ident[:])
                tr.then_inc(s("att_ot_prod"), 1)

            looped(pe, PAIRS, pair)
            pe.wait_ge(s("o_ready"), PAIRS)
            linear("wo", yT, KB, 2)
            mean_squares("f1")
            feed_forward(1)
            mean_squares("fin")
            mean_squares("n1")
            pe.wait_ge(s("norm_h_ready"), nth("n1", True))
            pe.wait_ge(s("fav_loaded"), 32)
            for k in range(KB):
                mm = pe.matmul(ps[0][0:24, :], favw[:, k, :], hT[:, k, :], start=(k == 0), stop=(k == KB - 1))
            mm.then_inc(s("fav_prod"), 1)
            pe.wait_ge(s("cum_ready"), 1)
            for t in range(TT):
                tr = pe.transpose(ps[1][:, 8 * t:8 * t + 8], fx8[3][:, t * P:(t + 1) * P], ident[0:8, 0:8])
            tr.then_inc(s("cq_turned"), 1)
            pe.wait_ge(s("cq_ready"), 1)

            def fox_pair(i, first):
                for j in range(2):
                    ring_ready(pe, "fx", i, j)
                    for b in range(2):
                        n = 2 * j + b
                        if not first:
                            if n == 0:
                                pe.wait_ge(s("fx_rms"), 3 * i)
                            if n == 2:
                                pe.wait_ge(s("fx_o_taken"), i)
                            if n == 3:
                                pe.wait_ge(s("att_sc_added"), 64 + 8 * i)
                        for k in range(KB):
                            mm = pe.matmul(ps[n][:], slot(j, 8, 256)[:, k, b * P:(b + 1) * P], hT[:, k, :],
                                           start=(k == 0), stop=(k == KB - 1))
                        mm.then_inc(s("fx_prod"), 1)
                for n, src in enumerate((sqq, sqk)):
                    pe.wait_ge(s("fx_sq"), 3 * i + n + 1)
                    pe.matmul(ps[n][:], halfm[:], src, start=True, stop=True).then_inc(s("fx_ms"), 1)
                pe.wait_ge(s("fx_mixed"), 2 * i + 2)
                for t in range(TT):
                    tr = pe.transpose(ps[2][:, t * P:(t + 1) * P], vmix[:, t * P:(t + 1) * P], ident[:])
                tr.then_inc(s("fx_vturned"), 1)
                pe.wait_ge(s("fx_taken"), 4 * i + 4)
                pe.wait_ge(s("fx_qk"), 2 * i + 2)
                attention_core(PAIRS + i, first)
                pe.wait_ge(s("fx_sq"), 3 * i + 3)
                pe.matmul(ps[0][:], halfm[:], sqq, start=True, stop=True).then_inc(s("fx_ms"), 1)
            looped(pe, 4, fox_pair)

            ring_ready(pe, "lora", 0, 0)
            pe.wait_ge(s("fx_rms"), 12)
            for k in range(KB):
                mm = pe.matmul(ps[0][:], slot(0, 8, P)[:, k, :], hT[:, k, :], start=(k == 0), stop=(k == KB - 1))
            mm.then_inc(s("lora_prod"), 1)
            ring_ready(pe, "lora", 0, 1)
            pe.wait_ge(s("fx_o_taken"), 4)
            for n, (c, m) in enumerate(((0, P), (P, 32))):
                for k in range(KB):
                    mm = pe.matmul(ps[1 + n][0:m, :], slot(1, 8, 160)[:, k, c:c + m], hT[:, k, :],
                                   start=(k == 0), stop=(k == KB - 1))
                mm.then_inc(s("lora_prod"), 1)
            pe.wait_ge(s("lora_ready"), 4)

            def rw_pair(i, first):
                if not first:
                    pe.wait_ge(s("rw_y_ready"), i)
                ring_ready(pe, "rw", i, 0)
                for b in range(2):
                    for k in range(KB):
                        mm = pe.matmul(ps[b][:], slot(0, 8, 256)[:, k, b * P:(b + 1) * P], hT[:, k, :],
                                       start=(k == 0), stop=(k == KB - 1))
                    mm.then_inc(s("rw_prod"), 1)
                ring_ready(pe, "rw", i, 1)
                for k in range(KB):
                    mm = pe.matmul(ps[2][:], slot(1, 8, P)[:, k, :], hT[:, k, :], start=(k == 0), stop=(k == KB - 1))
                mm.then_inc(s("rw_prod"), 1)
                for h in range(2):
                    pe.matmul(ps[3 + h][:], ring[64 * h:64 * h + 64, 1, 1024:1152], lwa[64 * h:64 * h + 64, :],
                              start=True, stop=True).then_inc(s("rw_prod"), 1)
                pe.matmul(ps[5][:], ring[:, 1, 1152:1280], lg0, start=True, stop=False)
                pe.matmul(ps[5][:], ring[0:32, 1, 1280:1408], lg1, start=False, stop=True).then_inc(s("rw_prod"), 1)
                for n in range(2):
                    pe.wait_ge(s("rw_sq"), 2 * i + n + 1)
                    pe.matmul(ps[6 + n][:], halfm[:], sqr, start=True, stop=True).then_inc(s("rw_ms"), 1)
                for n, src in enumerate((None, BT, KT, vv)):
                    if n == 0:
                        pe.wait_ge(s("rw_ops"), 4 * i + 4)
                        pe.wait_ge(s("rw_taken"), 6 * i + 6)
                    for t in range(TT):
                        tr = pe.transpose(ps[n][:, t * P:(t + 1) * P],
                                          AR[:, t, 0, :] if n == 0 else src[:, t * P:(t + 1) * P], ident[:])
                    tr.then_inc(s("rw_turned"), 1)
                for h in range(2):
                    own = slice(64 * h, 64 * h + 64)
                    for m, lhs in enumerate((BT, KT)):
                        for half in range(2):
                            n = 4 + 2 * m + half
                            if h == 1:
                                pe.wait_ge(s("rw_smt"), 10 * i + 2 * m + half + 1)
                            elif n == 6:
                                pe.wait_ge(s("rw_nrm"), i + 1)
                            elif n == 7:
                                pe.wait_ge(s("rw_bonus"), i + 1)
                            for t in range(2 * half, 2 * half + 2):
                                mm = pe.matmul(ps[n][:, (t % 2) * 256:(t % 2) * 256 + 256],
                                               lhs[own, t * P:(t + 1) * P], AR[own, t, :, :], start=True, stop=True)
                            mm.then_inc(s("rw_sm"), 1)
                    pe.wait_ge(s("rw_tok"), 4 * i + 4)
                    for t in range(TT):
                        mm = pe.matmul(ps[h][:, t * P:(t + 1) * P], AR[own, t, 0, :], BT[own, t * P:(t + 1) * P],
                                       start=True, stop=True)
                    mm.then_inc(s("rw_sm"), 1)
                for n in range(1, 6):
                    for h in range(2):
                        k = 2 * (n - 1) + h
                        pe.wait_ge(s("rw_am"), 10 * i + k + 1)
                        if n == 1:
                            pe.wait_ge(s("rw_d0"), 4 * i + 2 * h + 2)
                        else:
                            pe.wait_ge(s("rw_dt"), 20 * i + 2 * k - 2)
                        for t in range(TT):
                            mm = pe.matmul(ps[h][:, t * P:(t + 1) * P], Am[h][:, t, :], Dm[h][:, t, :],
                                           start=True, stop=True)
                        mm.then_inc(s("rw_x"), 1)
                    for h in range(2):
                        k = 2 * (n - 1) + h
                        pe.wait_ge(s("rw_xt"), 10 * i + k + 1)
                        if n == 1 and h == 0:
                            pe.wait_ge(s("rw_smt"), 10 * i + 10)
                        for w in range(2):
                            for t in range(TT):
                                mm = pe.matmul(ps[2 + 2 * w + h][:, t * P:(t + 1) * P], (DT, Xm)[w][h][:, t, :],
                                               (Xm, DT)[w][h][:, t, :], start=True, stop=True)
                            mm.then_inc(s("rw_dd"), 1)
                for t in range(TT):
                    for h in range(2):
                        mm = pe.matmul(ps[6][:, t * P + 64 * h:t * P + 64 * h + 64], AKT[h][:, t, 0:P],
                                       tokV[:, t, 64 * h:64 * h + 64], start=True, stop=True)
                mm.then_inc(s("rw_g"), 1)
                pe.wait_ge(s("rw_dt"), 20 * i + 20)
                for h in range(2):
                    for t in range(TT):
                        mm = pe.matmul(ps[0][64 * h:64 * h + 64, t * P:(t + 1) * P], tokA[:, t, 64 * h:64 * h + 64],
                                       DT[h][:, t, :], start=True, stop=True)
                mm.then_inc(s("rw_g"), 1)
                pe.wait_ge(s("rw_gt"), 3 * i + 1)
                for t in range(TT):
                    for h in range(2):
                        mm = pe.matmul(ps[7][:, t * P + 64 * h:t * P + 64 * h + 64], DT[h][:, t, :],
                                       Gm[:, t, 64 * h:64 * h + 64], start=True, stop=True)
                mm.then_inc(s("rw_g"), 1)
                pe.wait_ge(s("rw_gt"), 3 * i + 3)
                for c in range(8):
                    t, e = c // 2, c % 2
                    own = slice(64 * e, 64 * e + 64)
                    pe.wait_ge(s("rw_zt"), 8 * i + c + 1)
                    pe.matmul(ps[1 + e][own, 0:P], ApT[:, c * 64:c * 64 + 64], Zs[:, c, :], start=True, stop=True)\
                        .then_inc(s("rw_u"), 1)
                    if c < 7:
                        pe.matmul(ps[3 + e][:, 0:P], tokK[own, t, :], tokV[own, t, :], start=True, stop=False)
                        pe.wait_ge(s("rw_ut"), 8 * i + c + 1)
                        pe.matmul(ps[3 + e][:, 0:P], tokB[own, t, :], Usb[own, t, :], start=False, stop=True)\
                            .then_inc(s("rw_z"), 1)
                pe.wait_ge(s("rw_ut"), 8 * i + 8)
                for t in range(TT):
                    for e in range(2):
                        pe.matmul(ps[5][64 * e:64 * e + 64, t * P:(t + 1) * P], AR[:, t, 1, 64 * e:64 * e + 64],
                                  Zs[:, 2 * t + e, :], start=True, stop=False, skip_group_check=True)
                    for h in range(2):
                        cols = slice(64 * h, 64 * h + 64)
                        for m, (lhs, rhs) in enumerate(((ABT, Usb), (AKT, tokV))):
                            mm = pe.matmul(ps[5][:, t * P + 64 * h:t * P + 64 * h + 64], lhs[h][:, t, P:256],
                                           rhs[:, t, cols], start=False, stop=(m == 1), skip_group_check=True)
                mm.then_inc(s("rw_yprod"), 1)
                pe.wait_ge(s("rw_yn"), i + 1)
                for t in range(TT):
                    tr = pe.transpose(ps[6][:, t * P:(t + 1) * P], y_sb[:, t * P:(t + 1) * P], ident[:])
                tr.then_inc(s("rw_yturned"), 1)
            looped(pe, 4, rw_pair)
            pe.wait_ge(s("rw_y_ready"), 4)
            linear("w_out", yT, KB, 4)

            mean_squares("n2")
            pe.wait_ge(s("norm_h_ready"), nth("n2", True))
            pe.wait_ge(s("rt_loaded"), 32)
            for t in range(TT):
                for k in range(KB):
                    mm = pe.matmul(ps[0][:, t * 64:t * 64 + 64], hT[:, k, t * P:(t + 1) * P], rwt[:, k, :],
                                   start=(k == 0), stop=(k == KB - 1))
            mm.then_inc(s("rt_prod"), 1)
            pe.wait_ge(s("w_ready"), 1)
            for t in range(TT):
                tr = pe.transpose(ps[1][0:64, t * P:(t + 1) * P], wtok[:, t, :], ident[:])
            tr.then_inc(s("w_turned"), 1)
            pe.wait_ge(s("wT_ready"), 1)

            def experts(i, first):
                for par in range(2):
                    one_expert(i, par, first)

            def one_expert(i, par, first):
                w = exw[par]
                w8 = w[:, 0:4096].rearrange("p (m k n) -> p m k n", m=2, k=KB)
                wd = w[:, 4096:6144].rearrange("p (k n) -> p k n", k=2)
                pe.wait_ge(s(f"exp{par}_loaded"), 48 * i + 48)
                for m in range(2):
                    for b in range(2):
                        if not (first and par == 0):
                            pe.wait_ge(s("exp_act"), 4 * i + 2 * par + b - 1)
                        for k in range(KB):
                            mm = pe.matmul(ps[2 * m + b][:], w8[:, m, k, b * P:(b + 1) * P], hT[:, k, :],
                                           start=(k == 0), stop=(k == KB - 1))
                        mm.then_inc(s("exp_gu"), 1)
                pe.wait_ge(s("exp_act"), 4 * i + 2 * par + 2)
                for b in range(KB):
                    if not (first and par == 0 and b < 4):
                        pe.wait_ge(s("exp_added"), 16 * i + 8 * par + b - 3)
                    for k in range(2):
                        mm = pe.matmul(ps[4 + b % 4][:], wd[:, k, b * P:(b + 1) * P], xact[par][:, k, :],
                                       start=(k == 0), stop=(k == 1))
                    mm.then_inc(s("exp_down"), 1)
            looped(pe, 32, experts)
            one_expert(32, 0, False)
            mean_squares("fin2")
            pe.wait_ge(s("norm_h_ready"), nth("fin2", True))
            for t in range(TT):
                for half in range(2):
                    n = 2 * t + half
                    if n == 7:
                        pe.wait_ge(s("norm_rms_ready"), nth("fin2"))
                    for b in range(4):
                        tr = pe.transpose(ps[n][:, b * P:(b + 1) * P], hT[:, 4 * half + b, t * P:(t + 1) * P], ident[:])
                    tr.then_inc(s("out_turned"), 1)

        @block.scalar
        def _(act_e):
            order = Order(act_e, s("act_order"))

            def squares(n, ready, count):
                act_e.wait_ge(S[ready], count)
                nc.scalar.activation(sq[:], xT[:], ACT.Square).then_inc(s("norm_sq_ready"), 1)
                act_e.wait_ge(s("norm_ss_ready"), nth(n))
                nc.scalar.activation(rms[:], ps[7][:], ACT.Sqrt, bias=epsc[:]).then_inc(s("norm_rms_ready"), 1)

            def feed_forward(l):
                c0 = C_CONV + 256 * l

                def body(i, first):
                    for j in range(2):
                        for b in range(2):
                            blk = 2 * i + j + 22 * b
                            settle(act_e, s("ff_prod"), 44 * l + 4 * i + 2 * j + b + 1)
                            if not first:
                                settle(act_e, s("ff_act"), 22 * l + 2 * i + j - 1)
                            nc.scalar.activation(conv[j][b], ps[2 * j + b][:], ACT.Identity,
                                                 scale=col[:, bass.ds(c0 + P + blk, 1)],
                                                 bias=col[:, bass.ds(c0 + P + 44 + blk, 1)])\
                                .then_inc(s("ff_tap2"), 1)
                    for j in range(2):
                        settle(act_e, s("ff_tap0"), 44 * l + 4 * i + 2 * j + 2)
                        nc.scalar.activation(sil[j], conv[j][1], ACT.Silu).then_inc(s("ff_silu"), 1)
                looped(act_e, FB // 2, body)

            for b in range(0, KB, 2):
                act_e.wait_ge(s("x_turned"), b + 1)
                act_e.wait_ge(s("x_ready"), b) if b else None
                nc.scalar.copy(xT[:, b, :], ps[b][:]).then_inc(s("x_ready"), 1)
            act_e.wait_ge(s("col_ready"), 6)
            nc.scalar.activation(csil[:], col[:, C_C:C_C + 8], ACT.Silu).then_inc(s("c_silu"), 1)
            squares("a", "x_ready", KB)
            act_e.wait_ge(s("consts"), NCONST)
            for u in range(4):
                for t in range(TT):
                    act_e.wait_ge(s("gv_prod"), 4 * u + t + 1)
                    nc.scalar.activation(vtok[:, t, u * 256:(u + 1) * 256], ps[4 * (u % 2) + t][:, 0:256],
                                         ACT.Gelu_apprx_tanh).then_inc(s("gv_taken"), 1)
            act_e.wait_ge(s("gv_taken"), 16)
            for t in range(TT):
                order(nc.scalar.activation(sq[:, 0:2, :], vtok[:, t, :].rearrange("p (a b) -> p a b", a=2), ACT.Square,
                                           accum_out=ss4[:, t:t + 1]))
            nc.scalar.activation(ss4[:, 4:8], ss4[:, 0:4], ACT.Sqrt, scale=1.0 / D, bias=epsc[:])\
                .then_inc(s("vrms_ready"), 1)
            for n in range(8):
                act_e.wait_ge(s("gu_prod"), n + 1)
                nc.scalar.activation(gT[:, n, :], ps[n % 4][:], ACT.Gelu_apprx_tanh).then_inc(s("gu_taken"), 1)
            squares("f0", "lin_added", KB)
            feed_forward(0)
            squares("att", "lin_added", 2 * KB)

            def pair(i, first):
                for b in range(2):
                    settle(act_e, s("qkv_prod"), 3 * i + b + 1)
                    if b == 0 and not first:
                        settle(act_e, s("att_sc_prod"), 8 * i)
                    nc.scalar.activation((qT, kT)[b], ps[b][:], ACT.Copy, scale=(HD ** -0.5, 1.0)[b])\
                        .then_inc(s("qk_taken"), 1)
                attention_core(i, first)
                settle(act_e, s("att_ot_prod"), i + 1)
                nc.scalar.copy(yT[:, bass.ds(i, 1), :], ps[2][:].rearrange("p (a b) -> p a b", a=1))\
                    .then_inc(s("o_ready"), 1)

            def attention_core(i, first):
                def exps(u):
                    n = (u % TT + 1) * P
                    settle(act_e, s("att_negm_ready"), 8 * i + u + 1)
                    if not (first and u < 2):
                        settle(act_e, s("att_pt_prod"), 8 * i + u - 1)
                    nc.scalar.activation(p_sb[:, u % 2, 0:n], s_sb[:, u % 2, 0:n], ACT.Exp, bias=negm[:, u:u + 1],
                                         accum_out=rsum[:, u:u + 1]).then_inc(s("att_p_ready"), 1)

                exps(0)
                for u in range(8):
                    if u < 7:
                        exps(u + 1)
                    n = (u % TT + 1) * P
                    settle(act_e, s("att_pt_prod"), 8 * i + u + 1)
                    if not (first and u < 2):
                        settle(act_e, s("att_av_prod"), 8 * i + u - 1)
                    nc.scalar.copy(pT[:, u % 2, 0:n], ps[5 + u % 2][:, 0:n]).then_inc(s("att_pt_taken"), 1)
            looped(act_e, PAIRS, pair)
            squares("f1", "lin_added", 3 * KB)
            feed_forward(1)
            squares("fin", "lin_added", 4 * KB)
            squares("n1", "norm_h_ready", nth("fin", True))
            act_e.wait_ge(s("fav_prod"), 1)
            nc.scalar.activation(sig24, ps[0][0:24, :], ACT.Sigmoid).then_inc(s("fav_sig"), 1)
            act_e.wait_ge(s("f_abs"), 1)
            order(nc.scalar.activation(fx8[2], fx8[1], ACT.Exp, scale=-1.0))
            nc.scalar.activation(fx8[2], fx8[2], ACT.Ln, bias=onec[0:8, :]).then_inc(s("f_log"), 1)

            def fox_pair(i, first):
                for n, (dst, fn) in enumerate(((qraw, ACT.Copy), (kpad[:, 1:T + 1], ACT.Copy),
                                               (vpad[:, 1:T + 1], ACT.Copy), (gsig, ACT.Sigmoid))):
                    settle(act_e, s("fx_prod"), 4 * i + n + 1)
                    if n == 0 and not first:
                        settle(act_e, s("fx_y_ready"), i)
                    nc.scalar.activation(dst, ps[n][:], fn).then_inc(s("fx_taken"), 1)
                settle(act_e, s("fx_taken"), 4 * i + 1)
                nc.scalar.activation(sqq, qraw, ACT.Square).then_inc(s("fx_sq"), 1)
                settle(act_e, s("fx_mixed"), 2 * i + 1)
                nc.scalar.activation(sqk, kmix, ACT.Square).then_inc(s("fx_sq"), 1)
                for n, dst in enumerate((rq, rk)):
                    settle(act_e, s("fx_ms"), 3 * i + n + 1)
                    nc.scalar.activation(dst, ps[n][:], ACT.Sqrt, bias=epsc[:]).then_inc(s("fx_rms"), 1)
                attention_core(PAIRS + i, first)
                settle(act_e, s("att_ot_prod"), PAIRS + i + 1)
                nc.scalar.copy(oraw, ps[2][:]).then_inc(s("fx_o_taken"), 1)
                settle(act_e, s("fx_o_taken"), i + 1)
                nc.scalar.activation(sqq, oraw, ACT.Square).then_inc(s("fx_sq"), 1)
                settle(act_e, s("fx_ms"), 3 * i + 3)
                nc.scalar.activation(rq, ps[0][:], ACT.Sqrt, bias=epsc[:]).then_inc(s("fx_rms"), 1)
            looped(act_e, 4, fox_pair)

            act_e.wait_ge(s("fx_y_ready"), 4)
            for n, (dst, m) in enumerate(((rp, P), (kp, P), (vp, 32))):
                act_e.wait_ge(s("lora_prod"), n + 1)
                act_e.wait_ge(s("pads"), 2)
                nc.scalar.copy(dst[0:m, 1:T + 1], ps[n][0:m, :]).then_inc(s("lora_taken"), 1)
            act_e.wait_ge(s("lora_mixed"), 3)
            nc.scalar.activation(lwa[0:64, :], rr[0:64, :], ACT.Tanh).then_inc(s("lora_ready"), 1)
            nc.scalar.copy(lwa[64:128, :], rr[64:128, :]).then_inc(s("lora_ready"), 1)
            nc.scalar.activation(lg0, k0, ACT.Sigmoid).then_inc(s("lora_ready"), 1)
            nc.scalar.activation(lg1, vv[0:32, :], ACT.Sigmoid).then_inc(s("lora_ready"), 1)

            def rw_pair(i, first):
                w0, a0 = col[:, bass.ds(C_W0 + i, 1)], col[:, bass.ds(C_A0 + i, 1)]
                for n, dst in enumerate((rp, kp, vp)):
                    settle(act_e, s("rw_prod"), 6 * i + n + 1)
                    if n == 0 and not first:
                        settle(act_e, s("rw_y_ready"), i)
                    if n == 0 and first:
                        act_e.wait_ge(s("lora_ready"), 4)
                    nc.scalar.copy(dst[:, 1:T + 1], ps[n][:]).then_inc(s("rw_taken"), 1)
                for n, (dst, b) in enumerate(((ld, w0), (aa, a0))):
                    settle(act_e, s("rw_prod"), 6 * i + n + 4)
                    nc.scalar.activation(dst, ps[3 + n][:], ACT.Sigmoid, bias=b).then_inc(s("rw_taken"), 1)
                settle(act_e, s("rw_prod"), 6 * i + 6)
                nc.scalar.copy(gg, ps[5][:]).then_inc(s("rw_taken"), 1)
                settle(act_e, s("rw_kk"), i + 1)
                nc.scalar.activation(sqr, kkn, ACT.Square).then_inc(s("rw_sq"), 1)
                settle(act_e, s("rw_ms"), 2 * i + 1)
                nc.scalar.activation(nrm, ps[6][:], ACT.Sqrt, scale=float(HD)).then_inc(s("rw_nrm"), 1)
                settle(act_e, s("rw_L"), 2 * i + 2)
                for dst, src, sc in ((Pt, Lc, 1.0), (Pinv, Lc, -1.0), (Pprev, Pprev, 1.0)):
                    nc.scalar.activation(dst, src, ACT.Exp, scale=sc).then_inc(s("rw_P"), 1)
                for n, dst in enumerate((tokA, tokB, tokK, tokV)):
                    settle(act_e, s("rw_turned"), 4 * i + n + 1)
                    nc.scalar.copy(dst, tiles4(ps[n][:])).then_inc(s("rw_tok"), 1)
                for n in range(1, 6):
                    for h in range(2):
                        k = 2 * (n - 1) + h
                        settle(act_e, s("rw_x"), 10 * i + k + 1)
                        if n > 1:
                            settle(act_e, s("rw_dd"), 20 * i + 2 * k - 2)
                        nc.scalar.copy(Xm[h], tiles4(ps[h][:])).then_inc(s("rw_xt"), 1)
                settle(act_e, s("rw_g"), 3 * i + 1)
                nc.scalar.copy(Gm, tiles4(ps[6][:])).then_inc(s("rw_gt"), 1)
                settle(act_e, s("rw_g"), 3 * i + 2)
                nc.scalar.copy(ApT, ps[0][:]).then_inc(s("rw_gt"), 1)
                settle(act_e, s("rw_g"), 3 * i + 3)
                nc.scalar.copy(Wm, tiles4(ps[7][:])).then_inc(s("rw_gt"), 1)
                settle(act_e, s("rw_yprod"), i + 1)
                nc.scalar.copy(y_sb, ps[5][:]).then_inc(s("rw_yt"), 1)
                settle(act_e, s("rw_yc"), i + 1)
                nc.scalar.activation(y_sq, y_sb, ACT.Square).then_inc(s("rw_ysq"), 1)
                settle(act_e, s("rw_yvar"), i + 1)
                nc.scalar.activation(st8[:, 0:8], st8[:, 8:16], ACT.Sqrt, scale=1.0 / HD, bias=lnxe[:])\
                    .then_inc(s("rw_ystd"), 1)
            looped(act_e, 4, rw_pair)

            squares("n2", "lin_added", 5 * KB)
            act_e.wait_ge(s("rt_prod"), 1)
            nc.scalar.activation(sco, ps[0][:, 0:256].rearrange("p (t e) -> p t e", t=TT), ACT.Sigmoid)\
                .then_inc(s("rt_sig"), 1)

            def one_expert(i, par, first):
                for b in range(2):
                    settle(act_e, s("exp_gu"), 8 * i + 4 * par + b + 1)
                    if not (first and par == 0):
                        settle(act_e, s("exp_act"), 4 * i + 2 * par + b - 1)
                    nc.scalar.activation(xsil[:, b, :], ps[b][:], ACT.Silu).then_inc(s("exp_sil"), 1)

            def experts(i, first):
                for par in range(2):
                    one_expert(i, par, first)
            looped(act_e, 32, experts)
            one_expert(32, 0, False)
            squares("fin2", "moe_added", KB)
            for n in range(0, 8, 2):
                act_e.wait_ge(s("out_turned"), n + 1)
                nc.scalar.copy(out_tok[:, n // 2, 0:512], ps[n][:]).then_inc(s("out_ready"), 1)

        @block.vector
        def _(dve):
            order = Order(dve, s("dve_order"))

            def normalise(n, outs):
                dve.wait_ge(s("norm_rms_ready"), nth(n))
                order(nc.vector.reciprocal(rstd[:], rms[:]))
                for dst, gain in outs:
                    for b in range(KB):
                        ins = nc.vector.scalar_tensor_tensor(out=dst[:, b, :], in0=xT[:, b, :],
                                                             scalar=col[:, gain + b:gain + b + 1], in1=rstd[:],
                                                             op0=ALU.mult, op1=ALU.mult)
                    ins.then_inc(s("norm_h_ready"), 1)

            def add_linear(stage, banks):
                base = plan[stage][6]
                for n in range(KB):
                    dve.wait_ge(s("lin_prod"), base + n + 1)
                    nc.vector.tensor_tensor(xT[:, n, :], ps[n % banks][:], xT[:, n, :], ALU.add)\
                        .then_inc(s("lin_added"), 1)

            def feed_forward(l):
                c0 = C_CONV + 256 * l

                def body(i, first):
                    for j in range(2):
                        for b in range(2):
                            blk = 2 * i + j + 22 * b
                            c = conv[j][b]
                            n = 44 * l + 4 * i + 2 * j + b + 1
                            settle(dve, s("ff_tap2"), n)
                            nc.vector.scalar_tensor_tensor(
                                out=c[:, 1:T], in0=ps[2 * j + b][:, 0:T - 1],
                                scalar=col[:, bass.ds(c0 + 44 + blk, 1)], in1=c[:, 1:T],
                                op0=ALU.mult, op1=ALU.add).then_inc(s("ff_tap1"), 1)
                            settle(dve, s("ff_tap1"), n)
                            nc.vector.scalar_tensor_tensor(
                                out=c[:, 2:T], in0=ps[2 * j + b][:, 0:T - 2],
                                scalar=col[:, bass.ds(c0 + blk, 1)], in1=c[:, 2:T],
                                op0=ALU.mult, op1=ALU.add).then_inc(s("ff_tap0"), 1)
                    for j in range(2):
                        settle(dve, s("ff_silu"), 22 * l + 2 * i + j + 1)
                        nc.vector.tensor_tensor(act[:, bass.ds(2 * i + j, 1), :],
                                                sil[j].rearrange("p (a b) -> p a b", a=1),
                                                conv[j][0].rearrange("p (a b) -> p a b", a=1), ALU.mult)\
                            .then_inc(s("ff_act"), 1)
                looped(dve, FB // 2, body)
                add_linear(f"f{l}dn", 4)

            for b in range(1, KB, 2):
                dve.wait_ge(s("x_turned"), b + 1)
                dve.wait_ge(s("x_ready"), b)
                nc.vector.tensor_copy(xT[:, b, :], ps[b][:]).then_inc(s("x_ready"), 1)
            for t, rows in enumerate(PARAM_ROWS):
                dve.wait_ge(s("params_turned"), t + 1)
                nc.vector.tensor_copy(col[:, t * P:t * P + rows], ps[t][:, 0:rows]).then_inc(s("col_ready"), 1)
            dve.wait_ge(s("rel_loaded"), 16)
            nc.vector.tensor_copy(relE[:, REL:RELW], relE[:, REL - 1:REL].to_broadcast([16, RELW - REL]))\
                .then_inc(s("rel_ext"), 1)
            dve.wait_ge(s("rel_ext"), 1)
            nc.vector.tensor_copy(relR[:], relE[:, ::-1]).then_inc(s("rel_ext"), 1)
            dve.wait_ge(s("ws_loaded"), 16)
            nc.vector.memset(wsraw[0:64, :, 64:128], 0.0).then_inc(s("ws_masked"), 1)
            dve.wait_ge(s("ws_turned"), 1)
            order(nc.vector.tensor_copy(wsT[:, 0:4, :], ps[6][:].rearrange("p (g j) -> p g j", g=4)))
            nc.vector.tensor_copy(wsT[:, 4:8, :], ps[7][:].rearrange("p (g j) -> p g j", g=4)).then_inc(s("ws_ready"), 1)

            def ada(i, first):
                for j in range(2):
                    dve.wait_ge(s("mod_prod"), 2 * i + j + 1)
                    nc.vector.tensor_tensor(mod[:, bass.ds(4 * i + 2 * j, 2)], ps[j][:, 0:2],
                                            col[:, bass.ds(C_ADAB + 4 * i + 2 * j, 2)], ALU.add)\
                        .then_inc(s("mod_ready"), 1)
            looped(dve, 12, ada)
            normalise("a", [(hT, C_A)])
            dve.wait_ge(s("vrms_ready"), 1)
            order(nc.vector.reciprocal(ss4[:, 8:12], ss4[:, 4:8]))
            for t in range(TT):
                nc.vector.tensor_scalar(vtok[:, t, :], vtok[:, t, :], ss4[:, 8 + t:9 + t], None, ALU.mult)\
                    .then_inc(s("vn_ready"), 1)
            dve.wait_ge(s("bsb_loaded"), 16)
            dve.wait_ge(s("gu_taken"), 8)
            for g in range(8):
                dve.wait_ge(s("sp_prod"), g + 1)
                bank = 4 + g if g < 4 else g - 4
                order(nc.vector.scalar_tensor_tensor(
                    out=sptmp.rearrange("p (n i) -> p n i", n=TT), in0=ps[bank][:].rearrange("p (n i) -> p n i", n=TT),
                    scalar=col[:, C_VN + g:C_VN + g + 1],
                    in1=bsb[:, g, :].unsqueeze(1).to_broadcast([P, TT, P]), op0=ALU.mult, op1=ALU.add))
                nc.vector.tensor_tensor(gT[:, g, :], gT[:, g, :], sptmp, ALU.mult).then_inc(s("gated"), 1)
                dve.wait_ge(s("gated"), g + 1)
            add_linear("go", 4)
            normalise("f0", [(hT, C_F)])
            feed_forward(0)
            normalise("att", [(hT, C_B), (gT, C_KV)])
            dve.wait_ge(s("consts"), NCONST)
            dve.wait_ge(s("bias_loaded"), 16)

            def pair(i, first):
                dve.wait_ge(s("qkv_prod"), 3 * i + 3)
                if not first:
                    dve.wait_ge(s("att_av_prod"), 8 * i)
                nc.vector.tensor_copy(vt, ps[2][:].rearrange("p (t c) -> p t c", t=TT)).then_inc(s("v_taken"), 1)
                for u in range(8):
                    h, qt = u // TT, u % TT
                    n, far = (qt + 1) * P, max(qt - 1, 0) * P
                    sc = ps[3 + u % 2]
                    settle(dve, s("att_sc_prod"), 8 * i + u + 1)
                    if not (first and u < 2):
                        settle(dve, s("att_p_ready"), 8 * i + u - 1)
                    if far:
                        nc.vector.tensor_scalar(s_sb[:, u % 2, 0:far], sc[:, 0:far],
                                                biasT[:, bass.ds(2 * i + h, 1), 0:1].rearrange("p a b -> p (a b)"), None, ALU.add)
                    nc.vector.tensor_tensor(s_sb[:, u % 2, far:n].unsqueeze(1), sc[:, far:n].unsqueeze(1),
                                            biasT[:, bass.ds(2 * i + h, 1), 256 - (n - far):256],
                                            ALU.add).then_inc(s("att_sc_added"), 1)
                    row_max(i, u, n)
                attention_out(i, first)

            def row_max(i, u, n):
                dve.wait_ge(s("att_sc_added"), 8 * i + u + 1)
                nc.vector.tensor_reduce(mx[:, u:u + 1], s_sb[:, u % 2, 0:n], AX.X, ALU.max).then_inc(s("att_sc_max"), 1)
                settle(dve, s("att_sc_max"), 8 * i + u + 1)
                nc.vector.tensor_scalar(negm[:, u:u + 1], mx[:, u:u + 1], -1.0, None, ALU.mult)\
                    .then_inc(s("att_negm_ready"), 1)

            def attention_out(i, first):
                settle(dve, s("att_p_ready"), 8 * i + 8)
                nc.vector.reciprocal(rinv, rsum).then_inc(s("att_r_inv"), 1)
                settle(dve, s("att_r_inv"), i + 1)
                dve.wait_ge(s("att_av_prod"), 8 * i + 8)
                if not first:
                    dve.wait_ge(s("att_ot_prod"), i)
                nc.vector.tensor_tensor(o_sb.rearrange("p (t h d) -> p h t d", t=TT, h=2),
                                        ps[7][:].rearrange("p (t h d) -> p h t d", t=TT, h=2),
                                        rinv.rearrange("p (h t) -> p h t", h=2).unsqueeze(3)
                                        .to_broadcast([P, 2, TT, HD]), ALU.mult).then_inc(s("att_o_norm"), 1)
            looped(dve, PAIRS, pair)
            add_linear("wo", 2)
            normalise("f1", [(hT, C_F + 8)])
            feed_forward(1)
            normalise("fin", [(xT, C_FIN)])

            def normalise_mod(n, gain, shift):
                dve.wait_ge(s("norm_rms_ready"), nth(n))
                order(nc.vector.reciprocal(rstd[:], rms[:]))
                for b in range(KB):
                    ins = nc.vector.scalar_tensor_tensor(out=hT[:, b, :], in0=xT[:, b, :], scalar=gmod[:, gain + b:gain + b + 1],
                                                         in1=rstd[:], op0=ALU.mult, op1=ALU.mult)
                order(ins)
                for b in range(KB):
                    ins = nc.vector.tensor_scalar(hT[:, b, :], hT[:, b, :], mod[:, shift + b:shift + b + 1], None, ALU.add)
                ins.then_inc(s("norm_h_ready"), 1)

            nc.vector.scalar_tensor_tensor(out=gmod[:, 0:8], in0=mod[:, 8:16], scalar=1.0, in1=col[:, C_N1:C_N1 + 8],
                                           op0=ALU.add, op1=ALU.mult)
            nc.vector.scalar_tensor_tensor(out=gmod[:, 8:16], in0=mod[:, 32:40], scalar=1.0, in1=col[:, C_N2:C_N2 + 8],
                                           op0=ALU.add, op1=ALU.mult)
            order(nc.vector.tensor_scalar(qn8, col[:, C_QN:C_QN + 4], HD ** -0.5, None, ALU.mult))
            normalise_mod("n1", 0, 0)
            nc.vector.memset(kpad[:, 0:1], 0.0)
            nc.vector.memset(vpad[:, 0:1], 0.0).then_inc(s("pads"), 1)
            dve.wait_ge(s("fav_loaded"), 32)
            dve.wait_ge(s("fav_sig"), 1)
            order(nc.vector.tensor_scalar(fx8[0], ps[0][0:8, :], fbias[:], None, ALU.add))
            nc.vector.scalar_tensor_tensor(out=fx8[1], in0=fx8[0], scalar=-1.0, in1=fx8[0], op0=ALU.mult, op1=ALU.max)\
                .then_inc(s("f_abs"), 1)
            dve.wait_ge(s("f_log"), 1)
            order(nc.vector.scalar_tensor_tensor(out=fx8[1], in0=fx8[0], scalar=0.0, in1=fx8[2], op0=ALU.min,
                                                 op1=ALU.subtract))
            nc.vector.tensor_tensor_scan(fx8[3], ones8[:], fx8[1], 0.0, ALU.mult, ALU.add).then_inc(s("cum_ready"), 1)
            dve.wait_ge(s("cq_turned"), 1)
            nc.vector.tensor_copy(cq, ps[1][:, 0:32].rearrange("p (t h) -> p t h", t=TT)).then_inc(s("cq_ready"), 1)
            dve.wait_ge(s("cq_ready"), 1)
            dve.wait_ge(s("pads"), 1)
            steps = Order(dve, s("fx_order"), (s("consts"), NCONST))

            def token_shift(dst, pad, gate):
                steps(nc.vector.tensor_tensor(dst, pad[:, 0:T], pad[:, 1:T + 1], ALU.subtract))
                steps(nc.vector.tensor_tensor(dst, dst, gate, ALU.mult))
                nc.vector.tensor_tensor(dst, dst, pad[:, 1:T + 1], ALU.add).then_inc(s("fx_mixed"), 1)

            def fox_pair(i, first):
                steps.round(i, 16)
                settle(dve, s("fx_rows"), 80 * i + 80)
                settle(dve, s("fx_taken"), 4 * i + 2)
                token_shift(kmix, kpad, akb)
                settle(dve, s("fx_taken"), 4 * i + 3)
                token_shift(vmix, vpad, avb)
                settle(dve, s("fx_mixed"), 2 * i + 2)
                for n, (dst, src, r, gain) in enumerate(((qT, qraw, rq, small[:, bass.ds(48 + i, 1)]),
                                                         (kT, kmix, rk, col[:, bass.ds(C_KN + i, 1)]))):
                    settle(dve, s("fx_rms"), 3 * i + n + 1)
                    steps(nc.vector.reciprocal(r, r))
                    nc.vector.scalar_tensor_tensor(out=dst, in0=src, scalar=gain, in1=r, op0=ALU.mult, op1=ALU.mult)\
                        .then_inc(s("fx_qk"), 1)
                settle(dve, s("fx_vturned"), i + 1)
                nc.vector.tensor_copy(vt, ps[2][:].rearrange("p (t c) -> p t c", t=TT)).then_inc(s("v_taken"), 1)
                for u in range(8):
                    h, qt = u // TT, u % TT
                    n = (qt + 1) * P
                    settle(dve, s("att_sc_prod"), 64 + 8 * i + u + 1)
                    if not (first and u < 2):
                        settle(dve, s("att_p_ready"), 64 + 8 * i + u - 1)
                    row = s_sb[:, u % 2, :]
                    steps(nc.vector.scalar_tensor_tensor(out=row[:, 0:n], in0=ps[3 + u % 2][:, 0:n],
                                                         scalar=cq[:, qt, bass.ds(2 * i + h, 1)], in1=ckb[:, h, 0:n],
                                                         op0=ALU.add, op1=ALU.subtract))
                    nc.vector.tensor_tensor(row[:, n - P:n], row[:, n - P:n], tri[:], ALU.add)\
                        .then_inc(s("att_sc_added"), 1)
                    row_max(PAIRS + i, u, n)
                attention_out(PAIRS + i, first)
                settle(dve, s("fx_rms"), 3 * i + 3)
                steps(nc.vector.reciprocal(rq, rq))
                steps(nc.vector.scalar_tensor_tensor(out=kmix, in0=oraw, scalar=col[:, bass.ds(C_ON + i, 1)], in1=rq,
                                                     op0=ALU.mult, op1=ALU.mult))
                one = lambda x: x.rearrange("p (a b) -> p a b", a=1)
                nc.vector.tensor_tensor(yT[:, bass.ds(i, 1), :], one(kmix), one(gsig), ALU.mult)\
                    .then_inc(s("fx_y_ready"), 1)
            looped(dve, 4, fox_pair)

            dve.wait_ge(s("fx_y_ready"), 4)
            dve.wait_ge(s("att_av_prod"), 96)
            nc.vector.memset(rp[:, 0:1], 0.0)
            nc.vector.memset(kp[:, 0:1], 0.0)
            nc.vector.memset(vp[:, 0:1], 0.0).then_inc(s("pads"), 1)
            dve.wait_ge(s("pads"), 2)

            def shifted(step, dst, pad, mu, m=P):
                step(nc.vector.tensor_tensor(dd[0:m, :], pad[0:m, 0:T], pad[0:m, 1:T + 1], ALU.subtract))
                return nc.vector.scalar_tensor_tensor(out=dst[0:m, :], in0=dd[0:m, :], scalar=mu, in1=pad[0:m, 1:T + 1],
                                                      op0=ALU.mult, op1=ALU.add)

            for n, (dst, pad, m) in enumerate(((rr, rp, P), (k0, kp, P), (vv, vp, 32))):
                dve.wait_ge(s("lora_taken"), n + 1)
                shifted(order, dst, pad, col[0:m, C_MU + 12 + n:C_MU + 13 + n], m).then_inc(s("lora_mixed"), 1)
                dve.wait_ge(s("lora_mixed"), n + 1)
            dve.wait_ge(s("lora_ready"), 4)
            rsteps = Order(dve, s("rw_order"), (s("consts"), NCONST))
            ar4 = lambda x: x.rearrange("p (t c) -> p t c", t=TT)

            def rw_pair(i, first):
                rsteps.round(i, 27)
                for n, (dst, pad) in enumerate(((rr, rp), (k0, kp), (vv, vp))):
                    settle(dve, s("rw_taken"), 6 * i + n + 1)
                    rsteps(shifted(rsteps, dst, pad, col[:, bass.ds(C_MU + 4 * n + i, 1)]))
                nc.vector.tensor_scalar(kkn, k0, col[:, bass.ds(C_KK + i, 1)], None, ALU.mult).then_inc(s("rw_kk"), 1)
                settle(dve, s("rw_taken"), 6 * i + 4)
                rsteps(nc.vector.tensor_scalar(ld, ld, -E_DECAY, None, ALU.mult))
                nc.vector.tensor_tensor_scan(Lc, cmask[:], ld, 0.0, ALU.mult, ALU.add).then_inc(s("rw_L"), 1)
                settle(dve, s("rw_L"), 2 * i + 1)
                nc.vector.tensor_tensor(Pprev, Lc, ld, ALU.subtract).then_inc(s("rw_L"), 1)
                settle(dve, s("rw_nrm"), i + 1)
                rsteps(nc.vector.tensor_scalar(nrm, nrm, 1e-12, None, ALU.max))
                rsteps(nc.vector.reciprocal(nrm, nrm))
                rsteps(nc.vector.tensor_tensor(kkn, kkn, nrm, ALU.mult))
                settle(dve, s("rw_taken"), 6 * i + 5)
                rsteps(nc.vector.tensor_scalar(dd, aa, 1.0, col[:, bass.ds(C_KA + i, 1)], ALU.subtract, ALU.mult))
                rsteps(nc.vector.scalar_tensor_tensor(out=k0, in0=dd, scalar=1.0, in1=k0, op0=ALU.add, op1=ALU.mult))
                settle(dve, s("rw_ms"), 2 * i + 1)
                nc.vector.scalar_tensor_tensor(out=sqr, in0=rr, scalar=col[:, bass.ds(C_RK + i, 1)], in1=k0,
                                               op0=ALU.mult, op1=ALU.mult).then_inc(s("rw_sq"), 1)
                rsteps(nc.vector.tensor_tensor(dd, kkn, aa, ALU.mult))
                settle(dve, s("rw_P"), 3 * i + 3)
                nc.vector.scalar_tensor_tensor(out=AR[:, :, 0, :], in0=ar4(kkn), scalar=-1.0, in1=ar4(Pprev),
                                               op0=ALU.mult, op1=ALU.mult).then_inc(s("rw_ops"), 1)
                nc.vector.tensor_tensor(AR[:, :, 1, :], ar4(rr), ar4(Pt), ALU.mult).then_inc(s("rw_ops"), 1)
                nc.vector.tensor_tensor(BT, dd, Pinv, ALU.mult).then_inc(s("rw_ops"), 1)
                nc.vector.tensor_tensor(KT, k0, Pinv, ALU.mult).then_inc(s("rw_ops"), 1)
                settle(dve, s("rw_ms"), 2 * i + 2)
                nc.vector.scalar_tensor_tensor(out=nrm, in0=ps[7][:], scalar=float(HD), in1=vv, op0=ALU.mult,
                                               op1=ALU.mult).then_inc(s("rw_bonus"), 1)
                nc.vector.memset(Zs[:, 0, :], 0.0).then_inc(s("rw_zt"), 1)
                for h in range(2):
                    for n in range(4):
                        settle(dve, s("rw_sm"), 10 * i + 5 * h + n + 1)
                        half = n % 2
                        dst = (ABT, AKT)[n // 2][h][:, 2 * half:2 * half + 2, :]
                        nc.vector.tensor_tensor(dst, ps[4 + n][:].rearrange("p (t c) -> p t c", t=2),
                                                maskAR[:].unsqueeze(1).to_broadcast([P, 2, 256]), ALU.mult)\
                            .then_inc(s("rw_smt"), 1)
                    settle(dve, s("rw_sm"), 10 * i + 5 * h + 5)
                    nc.vector.tensor_tensor(Dm[h], tiles4(ps[h][:]), bc4(mask1[:]), ALU.mult).then_inc(s("rw_smt"), 1)
                    settle(dve, s("rw_smt"), 10 * i + 5 * h + 5)
                    rsteps(nc.vector.tensor_tensor(DT[h], ABT[h][:, :, 0:P], bc4(maskT[0][:]), ALU.mult))
                    nc.vector.tensor_tensor(Dm[h], Dm[h], bc4(ident[:]), ALU.add).then_inc(s("rw_d0"), 1)
                    nc.vector.tensor_tensor(DT[h], DT[h], bc4(ident[:]), ALU.add).then_inc(s("rw_d0"), 1)
                settle(dve, s("rw_d0"), 4 * i + 4)
                for n in range(1, 6):
                    for h in range(2):
                        for w in range(2):
                            k = 4 * (n - 1) + 2 * h + w
                            settle(dve, s("rw_dd"), 20 * i + 4 * (n - 1) + 2 * h + 2)
                            m = (Dm, DT)[w][h]
                            nc.vector.tensor_tensor(m, tiles4(ps[2 + 2 * w + h][:]), m, ALU.add).then_inc(s("rw_dt"), 1)
                    settle(dve, s("rw_dt"), 20 * i + 4 * n)
                settle(dve, s("rw_gt"), 3 * i + 3)
                for c in range(8):
                    t, e = c // 2, c % 2
                    own = slice(64 * e, 64 * e + 64)
                    settle(dve, s("rw_u"), 8 * i + c + 1)
                    nc.vector.tensor_tensor(Usb[own, t, :], ps[1 + e][own, 0:P], Wm[own, t, :], ALU.add)\
                        .then_inc(s("rw_ut"), 1)
                    if c < 7:
                        last = Pt[:, 64 * c + 63:64 * c + 64]
                        settle(dve, s("rw_z"), 7 * i + c + 1)
                        rsteps(nc.vector.scalar_tensor_tensor(out=ztmp, in0=ps[3 + e][:, 0:P], scalar=last, in1=bdiag[:],
                                                              op0=ALU.mult, op1=ALU.mult))
                        nc.vector.scalar_tensor_tensor(out=Zs[:, c + 1, :], in0=Zs[:, c, :], scalar=last, in1=ztmp,
                                                       op0=ALU.mult, op1=ALU.add).then_inc(s("rw_zt"), 1)
                        settle(dve, s("rw_zt"), 8 * i + c + 2)
                y8 = y_sb.rearrange("p (u d) -> p u d", d=HD)
                bc8 = lambda x: x.unsqueeze(2).to_broadcast([P, 8, HD])
                settle(dve, s("rw_yt"), i + 1)
                rsteps(nc.vector.tensor_reduce(st8[:, 0:8], y8, AX.X, ALU.add))
                rsteps(nc.vector.tensor_scalar(st8[:, 0:8], st8[:, 0:8], 1.0 / HD, None, ALU.mult))
                nc.vector.tensor_tensor(y8, y8, bc8(st8[:, 0:8]), ALU.subtract).then_inc(s("rw_yc"), 1)
                settle(dve, s("rw_ysq"), i + 1)
                nc.vector.tensor_reduce(st8[:, 8:16], y_sq.rearrange("p (u d) -> p u d", d=HD), AX.X, ALU.add)\
                    .then_inc(s("rw_yvar"), 1)
                settle(dve, s("rw_ystd"), i + 1)
                rsteps(nc.vector.reciprocal(st8[:, 0:8], st8[:, 0:8]))
                settle(dve, s("rw_yc"), i + 1)
                nc.vector.tensor_tensor(y8, y8, bc8(st8[:, 0:8]), ALU.mult).then_inc(s("rw_yn"), 1)
                settle(dve, s("rw_yturned"), i + 1)
                rsteps(nc.vector.tensor_scalar(dd, ps[6][:], col[:, bass.ds(C_LG + i, 1)],
                                               col[:, bass.ds(C_LB + i, 1)], ALU.mult, ALU.add))
                rsteps(nc.vector.tensor_tensor(dd, dd, nrm, ALU.add))
                one = lambda x: x.rearrange("p (a b) -> p a b", a=1)
                settle(dve, s("rw_taken"), 6 * i + 6)
                nc.vector.tensor_tensor(yT[:, bass.ds(4 + i, 1), :], one(dd), one(gg), ALU.mult)\
                    .then_inc(s("rw_y_ready"), 1)
            looped(dve, 4, rw_pair)

            for n in range(KB):
                dve.wait_ge(s("lin_prod"), 4 * KB + n + 1)
                nc.vector.scalar_tensor_tensor(out=xT[:, n, :], in0=ps[n % 4][:], scalar=mod[:, 16 + n:17 + n],
                                               in1=xT[:, n, :], op0=ALU.mult, op1=ALU.add)\
                    .then_inc(s("lin_added"), 1)

            normalise_mod("n2", 8, 24)
            dve.wait_ge(s("rt_loaded"), 32)
            dve.wait_ge(s("rt_sig"), 1)

            def top(vals, kth, k, mask, eq, at, starts, n):
                kb = kth.to_broadcast([P, TT, n])
                flat = lambda x: x.rearrange("p t e -> p (t e)")
                order(nc.vector.tensor_tensor(mask, vals, kb, ALU.is_gt))
                order(nc.vector.tensor_tensor(eq, vals, kb, ALU.is_equal))
                order(nc.vector.tensor_reduce(room, mask, AX.X, ALU.add))
                order(nc.vector.tensor_scalar(room, room, -1.0, float(k), ALU.mult, ALU.add))
                order(nc.vector.tensor_tensor_scan(flat(at), starts, flat(eq), 0.0, ALU.mult, ALU.add))
                order(nc.vector.tensor_tensor(at, at, room.to_broadcast([P, TT, n]), ALU.is_le))
                order(nc.vector.tensor_tensor(eq, eq, at, ALU.mult))
                order(nc.vector.tensor_tensor(mask, mask, eq, ALU.add))

            u8 = lambda x: x.rearrange("p t (g e) -> p (t g) e", e=8)
            order(nc.vector.tensor_tensor(sel, sco, rbias[:].unsqueeze(1).to_broadcast([P, TT, 64]), ALU.add))
            for u in range(32):
                mxi = nc.vector.max(srt[:, u, :], u8(sel)[:, u, :])
            order(mxi)
            order(nc.vector.tensor_tensor(gsc.rearrange("p t (g o) -> p (t g) o", o=1), srt[:, :, 0:1], srt[:, :, 1:2], ALU.add))
            for t in range(TT):
                mxi = nc.vector.max(gsrt[:, t, :], gsc[:, t, :])
            order(mxi)
            top(gsc, gsrt[:, :, 3:4], 4, gmask, geq, gpos, cm8[:], 8)
            order(nc.vector.tensor_scalar(gmask, gmask, 1.0, 1e30, ALU.subtract, ALU.mult))
            order(nc.vector.tensor_tensor(u8(sel), u8(sel), gmask.rearrange("p t (g o) -> p (t g) o", o=1)
                                          .to_broadcast([P, 32, 8]), ALU.add))
            for t in range(TT):
                mxi = nc.vector.max(esrt[:, t, :], sel[:, t, :])
            order(mxi)
            top(sel, esrt[:, :, 5:6], 6, wtok, eqm, pos, cmask[:, 0:256], 64)
            order(nc.vector.tensor_tensor(wtok, wtok, sco, ALU.mult))
            order(nc.vector.tensor_reduce(wsum, wtok, AX.X, ALU.add))
            order(nc.vector.reciprocal(wsum, wsum))
            order(nc.vector.tensor_scalar(wsum, wsum, 2.5, None, ALU.mult))
            nc.vector.tensor_tensor(wtok, wtok, wsum.to_broadcast([P, TT, 64]), ALU.mult).then_inc(s("w_ready"), 1)
            dve.wait_ge(s("w_turned"), 1)
            nc.vector.tensor_copy(wT, ps[1][0:64, :]).then_inc(s("wT_ready"), 1)
            order(nc.vector.memset(yT[:], 0.0))

            def one_expert(i, par, first, shared=False):
                for b in range(2):
                    n = 4 * i + 2 * par + b + 1
                    settle(dve, s("exp_gu"), 8 * i + 4 * par + b + 3)
                    settle(dve, s("exp_sil"), n)
                    if not first:
                        settle(dve, s("exp_down"), 16 * i + 8 * par - 8)
                    nc.vector.tensor_tensor(xact[par][:, b, :], ps[2 + b][:], xsil[:, b, :], ALU.mult)\
                        .then_inc(s("exp_act" if shared else "exp_raw"), 1)
                    if not shared:
                        settle(dve, s("exp_raw"), n)
                        if b == 0:
                            settle(dve, s(f"wbc{par}_loaded"), 16 * i + 16)
                        nc.vector.tensor_tensor(xact[par][:, b, :], xact[par][:, b, :], wbc[par], ALU.mult)\
                            .then_inc(s("exp_act"), 1)
                for b in range(KB):
                    settle(dve, s("exp_down"), 16 * i + 8 * par + b + 1)
                    if b == 0 and not (first and par == 0):
                        settle(dve, s("exp_added"), 16 * i + 8 * par)
                    nc.vector.tensor_tensor(yT[:, b, :], ps[4 + b % 4][:], yT[:, b, :], ALU.add)\
                        .then_inc(s("exp_added"), 1)

            def experts(i, first):
                for par in range(2):
                    one_expert(i, par, first)
            looped(dve, 32, experts)
            one_expert(32, 0, False, True)
            dve.wait_ge(s("exp_added"), 520)
            for b in range(KB):
                nc.vector.scalar_tensor_tensor(out=xT[:, b, :], in0=yT[:, b, :], scalar=mod[:, 40 + b:41 + b],
                                               in1=xT[:, b, :], op0=ALU.mult, op1=ALU.add).then_inc(s("moe_added"), 1)
            normalise("fin2", [(hT, C_FIN2)])
            for n in range(1, 8, 2):
                dve.wait_ge(s("out_turned"), n + 1)
                nc.vector.tensor_copy(out_tok[:, n // 2, 512:1024], ps[n][:]).then_inc(s("out_ready"), 1)


def kernel(**inputs):
    import numpy as np
    import concourse.bacc as bacc
    from concourse.bass_utils import run_bass_kernel_spmd

    nc = bacc.Bacc("TRN2", target_bir_lowering=False, num_devices=1)
    arrays = {name: np.ascontiguousarray(value) for name, value in inputs.items()}
    a = {name: nc.dram_tensor(name, v.shape, mybir.dt.from_np(v.dtype), kind="ExternalInput").ap()
         for name, v in arrays.items()}
    out = nc.dram_tensor("out", [1, T, D], F32, kind="ExternalOutput").ap()
    program(nc, a, out)
    return run_bass_kernel_spmd(nc, [arrays], core_ids=[0]).results[0]["out"]
```

```python
from contextlib import ExitStack

import concourse.bass as bass
from concourse import mybir

ALU = mybir.AluOpType
ACT = mybir.ActivationFunctionType
AX = mybir.AxisListType
F32 = mybir.dt.float32
U32 = mybir.dt.uint32

P = 128
D = 1024
KB = D // P
T = 512
TT = T // P
FF = 2816
FB = FF // P
PAIRS = 8
HD = 64
EPS = 1e-6
NEG = -1e30
REL = 257
RELW = 384
EXPERTS = 64
ROUNDS = T // P
PL = ROUNDS * EXPERTS + 4
RW = 2072
E_DECAY = 0.6065306597126334

C_A, C_KV, C_B, C_F, C_FIN, C_N1, C_N2, C_FIN2, C_ADAB, C_VN = 0, 8, 16, 24, 40, 48, 56, 64, 72, 120
C_CONV = 128
C5 = 640
C_C, C_QN, C_KN, C_ON, C_W0, C_A0, C_KK, C_KA, C_RK, C_LG, C_LB, C_MU = [
    C5 + n for n in (0, 8, 12, 16, 20, 24, 28, 32, 36, 40, 44, 48)]
PARAM_ROWS = (128, 88, 88, 88, 88, 63)


def wait(eng, sem, count):
    if not isinstance(count, int) or count > 0:
        eng.wait_ge(sem, count)


class Order:

    def __init__(self, eng, sem, consts=None):
        self.eng, self.sem, self.n, self.off, self.consts = eng, sem, 0, 0, consts

    def __call__(self, ins):
        self.n += 1
        ins.then_inc(self.sem, 1)
        self.eng.wait_ge(self.sem, self.n + self.off)
        if not isinstance(self.off, int):
            self.eng.wait_ge(*self.consts)

    def round(self, i, steps):
        assert self.n in (0, steps), self.n
        self.n, self.off = 0, i * steps


def looped(eng, n, body):
    body(0, True)
    if n == 2:
        body(1, False)
    elif n > 2:
        with eng.Fori(1, n) as i:
            body(i, False)


def program(nc, a, out):
    with ExitStack() as ctx:
        def sb(name, *shape, dt=F32):
            return ctx.enter_context(nc.sbuf_tensor(name, list(shape), dt))

        def sem(name):
            return ctx.enter_context(nc.semaphore(name))

        def scratch(name, *shape):
            return nc.dram_tensor(name, list(shape), F32, kind="Internal").ap()

        ps = [ctx.enter_context(nc.psum_tensor(f"bank{i}", [P, 512], F32)) for i in range(8)]

        xT = sb("xT", P, KB, T)
        hT = sb("hT", P, KB, T)
        two = sb("two", P, 2 * KB * T)
        gT = two[:, 0:KB * T].rearrange("p (b t) -> p b t", b=KB)
        yT = sb("yT", P, KB, T)
        sq = sb("sq", P, KB, T)
        big = sb("big", P, FB * T)
        ring = sb("ring", P, 2, FB * P)
        prow = sb("prow", P, 6, P)
        col = sb("col", P, 6 * P)
        ident = sb("ident", P, P)
        mean = sb("mean", P, P)
        rstd = sb("rstd", P, T)
        rms = sb("rms", P, T)
        epsc = sb("epsc", P, 1)
        mod = sb("mod", P, 48)
        csil = sb("csil", P, 8)
        ss4 = sb("ss4", P, 16)
        biasT = two[:, KB * T:].rearrange("p (h k) -> p h k", h=16)
        small = sb("small", P, 64)
        relE, relR = sb("relE", 16, RELW), sb("relR", 16, RELW)
        rel_dram = scratch("rel_dram", 16, P, RELW + 1)

        x_tok = sq[:].rearrange("p b t -> p (b t)").rearrange("p (t d) -> p t d", t=TT)
        act = big[:].rearrange("p (b t) -> p b t", b=FB)
        vtok = big[:, 0:4096].rearrange("p (t d) -> p t d", t=TT)
        wsraw = big[:, 4096:5120].rearrange("p (g j) -> p g j", g=8)
        wsT = big[:, 5120:6144].rearrange("p (g j) -> p g j", g=8)
        bsb = big[:, 6144:7168].rearrange("p (g j) -> p g j", g=8)
        sptmp = big[:, 7168:7680]
        ffw = sb("ffw", P, 6 * T)
        conv = [[ffw[:, (2 * j + b) * T:(2 * j + b + 1) * T] for b in range(2)] for j in range(2)]
        sil = [ffw[:, (4 + j) * T:(5 + j) * T] for j in range(2)]

        def carve(start, *shapes):
            got, at = [], start
            for s in shapes:
                n = s if isinstance(s, int) else s[0] * s[1]
                t = big[:, at:at + n]
                got.append(t if isinstance(s, int) else t.rearrange("p (a b) -> p a b", a=s[0]))
                at += n
            assert at <= FB * T, at
            return got

        qT, kT, vt, s_sb, p_sb, pT, o_sb, negm, rsum, mx, rinv = carve(
            0, 512, 512, (4, 128), (2, 512), (2, 512), (2, 512), 512, 8, 8, 8, 8)

        kpad, vpad, qraw, akb, avb, sqq, sqk, gsig = carve_from = carve(
            5696, 520, 520, 512, 512, 512, 512, 512, 512)
        ckb = two[:, 0:1024].rearrange("p (h t) -> p h t", h=2)
        sig24 = two[0:24, 1024:1536]
        fx8 = [two[0:8, 2048 + 512 * n:2560 + 512 * n] for n in range(4)]
        rq, rk, oraw, kmix, vmix = [two[:, 4096 + 512 * n:4608 + 512 * n] for n in range(5)]
        cq = small[:, 0:32].rearrange("p (t h) -> p t h", t=TT)
        gmod = small[:, 32:48]
        qn8 = small[:, 48:52]
        favw = sb("favw", P, KB, 24)
        fbias = sb("fbias", 8, 1)
        ones8 = sb("ones8", 8, T)
        tri = sb("tri", P, P)
        bdiag = sb("bdiag", P, P)
        halfm = sb("halfm", P, P)
        maskAR = sb("maskAR", P, 256)
        mask1 = sb("mask1", P, P)
        maskT = [sb(f"maskT{n}", P, P) for n in range(6)]
        cmask = sb("cmask", P, T)
        onec = sb("onec", P, 1)
        lnxe = sb("lnxe", P, 1)
        sig_dram, cum_dram = scratch("sig_dram", 16, T), scratch("cum_dram", 8, T)

        rp, kp, vp, dd, rr, k0, vv, ld, aa, gg, Lc, Pt, Pinv, Pprev, kkn, sqr, nrm, BT, KT, AR_ = carve(
            0, *[520] * 3, *[512] * 16, 1024)
        AR = AR_.rearrange("p (t w c) -> p t w c", t=TT, w=2)
        tokA, tokB, tokK, tokV, Gm, ApT, Wm, Usb = [two[:, 512 * n:512 * n + 512] for n in range(8)]
        tiles4 = lambda x: x.rearrange("p (t c) -> p t c", t=TT)
        tokA, tokB, tokK, tokV, Gm, Wm, Usb = map(tiles4, (tokA, tokB, tokK, tokV, Gm, Wm, Usb))
        ABT = [two[:, 4096 + 1024 * h:5120 + 1024 * h].rearrange("p (t c) -> p t c", t=TT) for h in range(2)]
        AKT = [two[:, 6144 + 1024 * h:7168 + 1024 * h].rearrange("p (t c) -> p t c", t=TT) for h in range(2)]
        sqf = sq[:].rearrange("p b t -> p (b t)")
        Dm, DT, Xm = [[tiles4(sqf[:, 1024 * n + 512 * h:1024 * n + 512 * h + 512]) for h in range(2)] for n in range(3)]
        Zs = sqf[:, 3072:4096].rearrange("p (c n) -> p c n", c=8)
        Am = [tiles4(ffw[:, 512 * h:512 * h + 512]) for h in range(2)]
        ztmp = ffw[:, 1024:1152]
        y_sb, y_sq = ffw[:, 2048:2560], ffw[:, 2560:3072]
        st8 = ss4
        lwa, lg0 = rms[:], rstd[:]
        lg1 = prow[0:32, 0:4, :].rearrange("p a b -> p (a b)")

        rwt = sb("rwt", P, KB, 64)
        rbias = sb("rbias", P, 64)
        cm8 = sb("cm8", P, 32)
        exw = [big[:, 0:6144], two[:, 0:6144]]
        flat_ring = ring[:].rearrange("p j n -> p (j n)")
        sh_gu, sh_dn = flat_ring[:, 0:4096], big[:, 6144:8192]
        hrow = [flat_ring[:, D * n:D * n + D] for n in range(2)]
        hgT = [flat_ring[:, 2048 + D * n:2048 + D * n + D].rearrange("p (b c) -> p b c", b=KB) for n in range(2)]
        yrow = [big[:, 6144 + D * n:6144 + D * n + D] for n in range(2)]
        onehot = [tiles4(big[:, 8192 + T * n:8192 + T * n + T]) for n in range(2)]
        eact = [big[:, 9216 + 256 * n:9472 + 256 * n] for n in range(2)]
        esil = [big[:, 9728 + 256 * n:9984 + 256 * n] for n in range(2)]
        place = ffw[:, 0:TT * PL].rearrange("p (t e) -> p t e", t=TT)
        count1 = ffw[:, 1152:1280]
        tokid = ffw[:, 1280:1284]
        etop = ffw[:, 1344:1408]
        wj, yposf = [ffw[:, 1408 + 32 * n:1432 + 32 * n].rearrange("p (t j) -> p t j", t=TT) for n in range(2)]
        nth_sel, ypos, over, pick = [tiles4(ffw[:, 1536 + 256 * n:1792 + 256 * n]) for n in range(4)]
        earlier, ones = maskT[0], maskT[1]
        slot_token = sb("slot_token", P, 2, dt=U32)
        yidx = sb("yidx", P, 24, dt=U32)
        overflow = sb("overflow", P, 1, dt=U32)
        h_dram, y_dram = scratch("h_dram", T, D), scratch("y_dram", ROUNDS * EXPERTS * P, D)
        htok = yT[:].rearrange("p b t -> p (b t)").rearrange("p (t d) -> p t d", t=TT)
        moe = hT[:].rearrange("p b t -> p (b t)").rearrange("p (t d) -> p t d", t=TT)
        yg = [sqf[:, D * n:D * n + D] for n in range(4)] + [htok[:, n, :] for n in range(4)]
        rt = two[:, 6144:8192]
        r4 = lambda n, w: rt[:, n:n + 4 * w].rearrange("p (t e) -> p t e", t=TT)
        sco, sel, eqm, pos, wtok = [r4(256 * n, 64) for n in range(5)]
        srt = rt[:, 1280:1536].rearrange("p (u e) -> p u e", e=8)
        gsc, gsrt, gmask, geq, gpos, esrt = [r4(1536 + 32 * n, 8) for n in range(6)]
        room, wsum = r4(1728, 1), r4(1732, 1)
        xact = sqf[:, 1024:2048].rearrange("p (b t) -> p b t", b=2)
        xsil = sqf[:, 3072:4096].rearrange("p (b t) -> p b t", b=2)
        out_tok = sqf.rearrange("p (t d) -> p t d", t=TT)

        S = {}
        bc4 = lambda m: m.unsqueeze(1).to_broadcast([P, TT, P])

        def s(name):
            if name not in S:
                S[name] = sem(name)
            return S[name]

        for n in ("ring0_loaded", "ring1_loaded", "ff_prod", "ada0_loaded", "ada1_loaded", "expgu0_loaded",
                  "expgu1_loaded", "expdn0_loaded", "expdn1_loaded", "hrow0_loaded", "hrow1_loaded",
                  "y0_stored", "y1_stored", "yg0_loaded", "yg1_loaded", "exp_sil", "exp_act", "y_act", "y_dve",
                  "overflow_known", "lin_prod", "mod_prod", "x_loaded", "sh_loaded", "exp_gu", "exp_down",
                  "out_ready", "pool_order", "consts", "side_loaded", "ws_loaded", "rel_loaded", "pool_consts",
                  "rel_ext", "rel_stored", "norm_sq_ready", "norm_sum", "ada_summed", "col_ready", "fav_sig",
                  "sig_stored", "cum_ready", "fx_mixed", "att_sc_added", "fx_rows", "rw_smt", "rw_x", "rw_am",
                  "rw_y_ready", "moe_consts", "h_stored", "slot_ready", "hrow_turned", "yidx_ready",
                  "sh_added", "y_summed", "norm_ss_ready", "mod_ready", "lin_added", "ff_tap0", "norm_h_ready",
                  "ff_act", "x_turned", "params_loaded", "x_ready", "params_turned", "ws_step", "gv_taken",
                  "norm_rms_ready", "gv_prod", "gu_taken", "gu_prod", "vn_ready", "sp_prod", "gated",
                  "qk_taken", "qkv_prod", "o_ready", "att_sc_prod", "att_p_ready", "att_pt_taken",
                  "att_pt_prod", "v_taken", "att_o_norm", "att_av_prod", "att_ot_prod", "fav_prod", "cq_step",
                  "fx_rms", "fx_o_taken", "fx_prod", "fx_sq", "fx_ms", "fx_vturned", "fx_taken", "fx_qk",
                  "lora_prod", "lora_ready", "rw_prod", "rw_sq", "rw_ms", "rw_ops", "rw_taken", "rw_turned",
                  "rw_nrm", "rw_bonus", "rw_sm", "rw_tok", "rw_d0", "rw_dt", "rw_xt", "rw_dd", "rw_g", "rw_gt",
                  "rw_zt", "rw_u", "rw_ut", "rw_z", "rw_out_step", "rt_prod", "htok_taken", "htok_turned",
                  "sh_gu_prod", "rt_masked", "places_prod", "onehot_ready", "slot_prod", "hgt_act", "hgt_dve",
                  "sh_act", "sh_prod", "moe_turned", "out_turned", "act_order", "h_scaled", "ff_tap2",
                  "ff_silu", "vrms_ready", "att_negm_ready", "f_abs", "f_log", "fx_y_ready", "pads",
                  "lora_taken", "lora_mixed", "rw_kk", "rw_L", "rw_P", "rt_sig", "sh_sil", "dve_order",
                  "ff_tap1", "att_sc_max", "att_r_inv", "fx_order", "rw_order", "moe_added"):
            s(n)
        NORMS = ["a", "f0", "att", "f1", "fin", "n1", "n2", "fin2"]
        nth = lambda n: NORMS.index(n) + 1

        def h_count(n, b, out=0):
            k = NORMS.index(n)
            return KB * (k + out + (k > NORMS.index("att"))) + b + 1

        LINEARS = ["go", "f0dn", "wo", "f1dn", "w_out"]

        plan, steps, loads, before = {}, {}, [0, 0], None
        STAGES = [("gv", 4, 1, 1, "gv_prod", 4), ("gu", 4, 1, 1, "gu_prod", 2),
                  ("go", 4, 1, 1, "lin_prod", 2), ("f0in", 22, 2, 2, "ff_prod", 2), ("f0dn", 8, 1, 1, "lin_prod", 1),
                  ("att", 16, 2, 1, "qkv_prod", (2, 3)), ("wo", 4, 1, 1, "lin_prod", 2),
                  ("f1in", 22, 2, 2, "ff_prod", 2), ("f1dn", 8, 1, 1, "lin_prod", 1),
                  ("fx", 8, 2, 2, "fx_prod", 2), ("lora", 2, 1, 1, "lora_prod", (1, 3)),
                  ("rw", 8, 2, 5, "rw_prod", (2, 6)), ("w_out", 4, 1, 1, "lin_prod", 2)]
        for name, units, d0, d1, used, per in STAGES:
            plan[name] = (units, list(loads), (d0, d1), used, per, before, steps.get(used, 0))
            steps[used] = steps.get(used, 0) + (units // 2 * per[1] if isinstance(per, tuple) else units * per)
            loads[0] += 16 * d0 * units // 2
            loads[1] += 16 * d1 * units // 2
            before = name

        def steps_of(stage):
            per = plan[stage][4]
            return per if isinstance(per, tuple) else (per, 2 * per)

        def used_count(stage, m):
            odd, both = steps_of(stage)
            return plan[stage][6] + both * (m // 2) + odd * (m % 2)

        def ring_ready(eng, stage, i, j):
            _, base, d, *_ = plan[stage]
            wait(eng, (S["ring0_loaded"], S["ring1_loaded"])[j], base[j] + 16 * d[j] * (i + 1))

        adaw = [two[:, 2048 * j:2048 * j + 2048].rearrange("p (k n) -> p k n", k=KB) for j in range(2)]
        ADA = FB
        ADA_UNITS = 6 * D // 256

        def slot(j, k, n):
            return ring[:, j, 0:k * n].rearrange("p (k n) -> p k n", k=k)

        def wcols(w, c0, n):
            return w.rearrange("(k p) n -> p k n", p=P)[:, :, bass.ds(c0, n)]

        w_in, w_kv, w_q = a["a_w_in"][0], a["w_kv"], a["b_w_q"][0]

        def unit_loads(stage, i, j):
            u = 2 * i + j
            if stage == "gv":
                return [(slot(j, 8, 256), wcols(w_in, D + u * 256, 256))]
            if stage == "gu":
                return [(slot(j, 8, 256), wcols(w_in, u * 256, 256))]
            if stage in ("go", "wo", "w_out"):
                w = {"go": a["a_w_out"][0], "wo": a["b_w_o"][0], "w_out": a["w_out_2"][0]}[stage]
                return [(slot(j, 8, 256), wcols(w, u * 256, 256))]
            if stage in ("f0in", "f1in"):
                w = a["f_w_in"][int(stage[1])]
                return [(slot(j, 8, 256)[:, :, b * P:(b + 1) * P], wcols(w, b * FF + u * P, P)) for b in range(2)]
            if stage in ("f0dn", "f1dn"):
                return [(slot(j, FB, P), wcols(a["f_w_down"][int(stage[1])], u * P, P))]
            if stage == "att":
                if j == 0:
                    return [(slot(0, 8, 256)[:, :, 0:P], wcols(w_q, i * P, P)),
                            (slot(0, 8, 256)[:, :, P:256], wcols(w_kv, i * P, P))]
                return [(slot(1, 8, P), wcols(w_kv, D + i * P, P))]
            w2 = a["w_in_2"][0]
            if stage == "fx":
                return [(slot(j, 8, 256)[:, :, b * P:(b + 1) * P], wcols(w2, (2 * j + b) * 512 + i * P, P))
                        for b in range(2)]
            if stage == "lora":
                return [(slot(j, 8, (P, 160)[j]), wcols(w2, (RW + 1536, RW + 1664)[j], (P, 160)[j]))]
            if stage == "rw":
                if j == 0:
                    return [(slot(0, 8, 256)[:, :, b * P:(b + 1) * P], wcols(w2, RW + b * 512 + i * P, P))
                            for b in range(2)]
                own = bass.ds(i * P, P)
                return [(slot(1, 8, P), wcols(w2, RW + 1024 + i * P, P)),
                        (ring[0:64, 1, 1024:1152], a["rw_decay_up_2"][0][:, own]),
                        (ring[64:128, 1, 1024:1152], a["rw_iclr_up_2"][0][:, own]),
                        (ring[:, 1, 1152:1280], a["rw_gate_up_2"][0][0:P, own]),
                        (ring[0:32, 1, 1280:1408], a["rw_gate_up_2"][0][P:160, own])]
            raise AssertionError(stage)

        block = ctx.enter_context(nc.Block())
        NCONST = 5
        NPARAM = 10 + 6 + 13

        def settle(eng, sem, count):
            wait(eng, sem, count)
            if not isinstance(count, int):
                eng.wait_ge(S["consts"], NCONST)

        def all_experts(eng, body, after=None):
            looped(eng, EXPERTS // 2, body)
            eng.wait_ge(s("overflow_known"), 1)
            with eng.If(eng.value_load(overflow[0:1, 0:1], min_val=0, max_val=1) > 0):
                with eng.Fori(EXPERTS // 2, ROUNDS * EXPERTS // 2) as i:
                    body(i, False)
                if after:
                    after(ROUNDS * EXPERTS)
            if after:
                with eng.Else():
                    after(EXPERTS)

        @block.sync
        def _(sp):
            def stage_loads(stage):
                units, _, _, used, per, before, base = plan[stage]

                def load(i, first):
                    for j in range(2):
                        if first and before is not None:
                            sp.wait_ge(S[plan[before][3]], used_count(before, plan[before][0] - 1 + j))
                        elif not first:
                            even, both = steps_of(stage)
                            sp.wait_ge(S[used], both * i + base - (both - even if j == 0 else 0))
                        for dst, src in unit_loads(stage, i, j):
                            sp.dma_start(dst, src).then_inc(S[f"ring{j}_loaded"], 16)
                        if stage == "f0in":
                            ada_load(2 * i + j, j)
                looped(sp, units // 2, load)
                if stage == "f0in":
                    for u in range(ADA, ADA_UNITS):
                        ada_load(u, u % 2)

            def ada_load(u, j):
                if isinstance(u, int) and u < 2:
                    sp.wait_ge(s("lin_prod"), KB)
                else:
                    sp.wait_ge(s("mod_prod"), u - 1)
                sp.dma_start(adaw[j], wcols(a["ada_w_2"][0], u * 256, 256)).then_inc(s(f"ada{j}_loaded"), 16)

            sp.dma_start(x_tok, a["x"][0].rearrange("(t p) d -> p t d", p=P)).then_inc(s("x_loaded"), 16)
            for name, *_ in STAGES:
                stage_loads(name)

            sp.wait_ge(s("lin_prod"), 5 * KB)
            for k, n in ((0, "sh_w_gate_2"), (2048, "sh_w_up_2")):
                sp.dma_start(sh_gu[:, k:k + 2048].rearrange("p (k n) -> p k n", k=KB),
                             a[n][0].rearrange("(k p) n -> p k n", p=P)).then_inc(s("sh_loaded"), 16)
            sp.dma_start(sh_dn.rearrange("p (k n) -> p k n", k=2),
                         a["sh_w_down_2"][0].rearrange("(k p) n -> p k n", p=P)).then_inc(s("sh_loaded"), 16)

            def expert_loads(i, first, r=0):
                for par in range(2):
                    w = exw[par]
                    e = bass.ds(2 * i + par - EXPERTS * r, 1)
                    one = lambda n: a[n][0][e].rearrange("o r c -> (o r) c")
                    wait(sp, s("exp_gu"), 4 * i + 2 * par - 2)
                    for k, n in ((0, "exp_w_gate_2"), (2048, "exp_w_up_2")):
                        sp.dma_start(w[:, k:k + 2048].rearrange("p (k n) -> p k n", k=KB),
                                     one(n).rearrange("(k p) n -> p k n", p=P)).then_inc(s(f"expgu{par}_loaded"), 16)
                    wait(sp, s("exp_down"), 4 * i + 2 * par - 2)
                    sp.dma_start(w[:, 4096:6144].rearrange("p (k n) -> p k n", k=2),
                                 one("exp_w_down_2").rearrange("(k p) n -> p k n", p=P))\
                        .then_inc(s(f"expdn{par}_loaded"), 16)

            looped(sp, EXPERTS // 2, expert_loads)
            sp.wait_ge(s("overflow_known"), 1)
            with sp.If(sp.value_load(overflow[0:1, 0:1], min_val=0, max_val=1) > 0):
                for r in range(1, ROUNDS):
                    with sp.Fori(r * EXPERTS // 2, (r + 1) * EXPERTS // 2) as i:
                        expert_loads(i, False, r)
            sp.wait_ge(s("out_ready"), TT)
            sp.dma_start(out[0, :, 512:].rearrange("(t p) d -> p t d", p=P), out_tok[:, :, 512:]).then_inc(s("x_loaded"), 16)
            sp.wait_ge(s("x_loaded"), 48)

        @block.gpsimd
        def _(pool):
            pool.memset(prow[:, 5, :], 0.0).then_inc(s("pool_order"), 1)
            pool.memset(ident[:], 0.0).then_inc(s("pool_order"), 1)
            pool.memset(mean[:], 1.0 / D).then_inc(s("consts"), 1)
            pool.memset(epsc[:], EPS).then_inc(s("consts"), 1)
            pool.wait_ge(s("pool_order"), 2)
            pool.affine_select(out=ident[:], in_=ident[:], compare_op=ALU.not_equal, fill=1.0, base=0,
                               pattern=[[-1, P]], channel_multiplier=1).then_inc(s("consts"), 1)
            pool.dma_start(favw[:], wcols(a["w_in_2"][0], 2048, 24)).then_inc(s("side_loaded"), 16)
            pool.dma_start(fbias[:], a["fox_forget_b_2"][0].rearrange("(h o) -> h o", o=1)).then_inc(s("side_loaded"), 16)
            pool.dma_start(rwt[:], a["router_w_2"][0].rearrange("(k p) n -> p k n", p=P)).then_inc(s("side_loaded"), 16)
            pool.dma_start(rbias[:], a["router_bias_2"][0].partition_broadcast(P)).then_inc(s("side_loaded"), 16)
            pool.dma_start(wsraw, a["a_w_s"][0].rearrange("g i j -> i g j")).then_inc(s("ws_loaded"), 16)
            pool.dma_start(bsb, a["a_b_s"][0].rearrange("g i -> (g i)").partition_broadcast(P)
                           .rearrange("p (g i) -> p g i", g=8)).then_inc(s("ws_loaded"), 16)
            pool.dma_start(relE[:, 0:REL], a["b_rel_bias"][0]).then_inc(s("rel_loaded"), 16)
            porder = Order(pool, s("pool_consts"))
            porder(pool.memset(lnxe[:], 64e-5))
            porder(pool.memset(ones8[:], 1.0))
            porder(pool.memset(cmask[:], 1.0))
            porder(pool.memset(cmask[:].rearrange("p (c n) -> p c n", n=64)[:, :, 0:1], 0.0))
            porder(pool.memset(cm8[:], 1.0))
            porder(pool.memset(cm8[:].rearrange("p (c n) -> p c n", n=8)[:, :, 0:1], 0.0))
            porder(pool.memset(tri[:], 0.0))
            porder(pool.affine_select(out=tri[:], in_=tri[:], compare_op=ALU.is_ge, fill=NEG, base=0,
                               pattern=[[-1, P]], channel_multiplier=1))
            for tile, v in ((bdiag, 1.0), (halfm, 1.0 / HD)):
                porder(pool.memset(tile[:], v))
                porder(pool.memset(tile[0:64, 64:128], 0.0))
                porder(pool.memset(tile[64:128, 0:64], 0.0))
            porder(pool.memset(maskAR[:], 1.0))
            for w, op in ((0, ALU.is_gt), (1, ALU.is_ge)):
                half = maskAR[:, w * P:(w + 1) * P]
                porder(pool.affine_select(out=half, in_=half, compare_op=op, fill=0.0, base=0,
                                          pattern=[[1, P]], channel_multiplier=-1))
                porder(pool.memset(maskAR[0:64, w * P + 64:(w + 1) * P], 0.0))
            porder(pool.memset(mask1[:], 0.0))
            view = mask1[:].rearrange("p (b w) -> p b w", w=2)
            porder(pool.memset(view[:, :, 0:1], 1.0))
            porder(pool.affine_select(out=view, in_=view, compare_op=ALU.is_equal, fill=0.0, base=-1,
                               pattern=[[-2, 64], [0, 2]], channel_multiplier=1))
            for n in range(6):
                w = 1 << n
                view = maskT[n][:].rearrange("p (b w c) -> p b w c", w=2, c=w)
                porder(pool.memset(maskT[n][:], 0.0))
                porder(pool.memset(view[:, :, 1:2, :], 1.0))
                porder(pool.affine_select(out=view, in_=view, compare_op=ALU.is_ge, fill=0.0, base=0,
                                          pattern=[[-2 * w, 64 // w], [0, 2], [0, w]], channel_multiplier=1))
                porder(pool.affine_select(out=view, in_=view, compare_op=ALU.is_ge, fill=0.0, base=w - 1,
                                   pattern=[[2 * w, 64 // w], [0, 2], [0, w]], channel_multiplier=-1))
            pool.memset(onec[:], 1.0).then_inc(s("consts"), 1)
            pool.wait_ge(s("rel_ext"), 2)
            pool.dma_start(rel_dram[:, :, 0:RELW], relR[:].unsqueeze(1).to_broadcast([16, P, RELW]))\
                .then_inc(s("rel_stored"), 16)
            pool.wait_ge(s("rel_stored"), 16)
            pool.dma_start(biasT, bass.AP(rel_dram.tensor, 127, [[RELW, P], [P * (RELW + 1), 16], [1, 256]]))\
                .then_inc(s("rel_stored"), 16)
            pool.wait_ge(s("rel_stored"), 32)
            pool.memset(biasT[0:64, :, 192:256], NEG).then_inc(s("consts"), 1)

            def square_sums(n):
                for b in range(1, KB - 1):
                    pool.wait_ge(s("norm_sq_ready"), KB * (nth(n) - 1) + b + 1)
                    if b > 1:
                        pool.wait_ge(s("norm_sum"), 6 * (nth(n) - 2) + b - 1)
                    nc.gpsimd.tensor_tensor(sq[:, 0, :], sq[:, 0, :], sq[:, b, :], ALU.add).then_inc(s("norm_sum"), 1)

            def ada(i, first):
                for j in range(2):
                    ada_unit(2 * i + j, j)

            def ada_unit(u, j):
                def step(k, ins):
                    ins.then_inc(s("ada_summed"), 1)
                    if k < 4:
                        settle(pool, s("ada_summed"), 4 * u + k)

                w = adaw[j]
                settle(pool, s(f"ada{j}_loaded"), 16 * (u // 2) + 16 if isinstance(u, int) else 8 * (u - j) + 16)
                step(1, nc.gpsimd.tensor_tensor(w, w, csil[:].unsqueeze(2).to_broadcast([P, KB, 256]), ALU.mult))
                for k, n in ((2, 4), (3, 2), (4, 1)):
                    step(k, nc.gpsimd.tensor_tensor(w[:, 0:n, :], w[:, 0:n, :], w[:, n:2 * n, :], ALU.add))

            square_sums("f0")
            pool.wait_ge(s("col_ready"), len(PARAM_ROWS) + 1)
            looped(pool, ADA // 2, ada)
            for u in range(ADA, ADA_UNITS):
                ada_unit(u, u % 2)
            for n in ("att", "f1", "fin", "n1"):
                square_sums(n)
            pool.wait_ge(s("fav_sig"), 1)
            pool.dma_start(sig_dram, sig24[8:24, :]).then_inc(s("sig_stored"), 16)
            pool.wait_ge(s("cum_ready"), 1)
            pool.dma_start(cum_dram, fx8[3]).then_inc(s("sig_stored"), 16)
            pool.wait_ge(s("sig_stored"), 32)

            def fox_rows(i, first):
                if not first:
                    settle(pool, s("fx_mixed"), 2 * i)
                    settle(pool, s("att_sc_added"), 64 + 8 * i)
                for h in range(2):
                    for n, dst in enumerate((akb, avb)):
                        pool.dma_start(dst[64 * h:64 * h + 64, :],
                                       sig_dram[bass.ds(8 * n + 2 * i + h, 1), :].rearrange("o t -> (o t)")
                                       .partition_broadcast(64)).then_inc(s("fx_rows"), 16)
                pool.dma_start(ckb, cum_dram[bass.ds(2 * i, 2), :].partition_broadcast(P)).then_inc(s("fx_rows"), 16)
            looped(pool, 4, fox_rows)

            def level_masks(i, first):
                for n in range(1, 6):
                    for h in range(2):
                        k = 2 * (n - 1) + h
                        if n == 1:
                            settle(pool, s("rw_smt"), 10 * i + 5 * h + 5)
                        else:
                            settle(pool, s("rw_x"), 10 * i + k - 1)
                        nc.gpsimd.tensor_tensor(Am[h], ABT[h][:, :, 0:P], bc4(maskT[n][:]), ALU.mult)\
                            .then_inc(s("rw_am"), 1)
            looped(pool, 4, level_masks)

            square_sums("n2")
            pool.wait_ge(s("rw_y_ready"), 4)
            pool.memset(ones[:], 1.0).then_inc(s("moe_consts"), 1)
            pool.wait_ge(s("moe_consts"), 1)
            pool.affine_select(out=earlier[:], in_=ones[:], compare_op=ALU.is_gt, fill=0.0, base=0,
                               pattern=[[1, P]], channel_multiplier=-1).then_inc(s("moe_consts"), 1)
            for dst, step, n, base, ch in ((count1, 1, P, 1, 0), (tokid, P, TT, 0, 1), (etop, P, EXPERTS, -1, 0)):
                pool.iota(dst, [[step, n]], base=base, channel_multiplier=ch,
                          allow_small_or_imprecise_dtypes=True).then_inc(s("moe_consts"), 1)
            pool.wait_ge(s("h_stored"), 32)

            def gather(n, par):
                ready, turned = n + 1, 2 * n - 2
                if not isinstance(n, int):
                    ready, turned = pool.to_reg(ready), pool.to_reg(turned)
                    pool.wait_ge(s("consts"), NCONST)
                wait(pool, s("slot_ready"), ready)
                wait(pool, s("hrow_turned"), turned)
                pool.indirect_dma_start(hrow[par], None, h_dram, bass.IndirectOffsetOnAxis(slot_token[:, par:par + 1], 0))\
                    .then_inc(s(f"hrow{par}_loaded"), 16)

            gather(0, 0)
            gather(1, 1)

            def experts(i, first):
                for par in range(2):
                    gather(2 * i + par + 2, par)

            def token_results(n):
                for par in range(2):
                    pool.wait_ge(s(f"y{par}_stored"), 8 * n)
                pool.wait_ge(s("yidx_ready"), 1)
                pool.wait_ge(s("sh_added"), KB)
                for k in range(6 * TT):
                    if k % 4 == 0 and k >= 8:
                        pool.wait_ge(s("y_summed"), k - 4)
                    pool.indirect_dma_start(yg[k % 8], None, y_dram[0:n * P, :], bass.IndirectOffsetOnAxis(yidx[:, k:k + 1], 0))\
                        .then_inc(s(f"yg{k // 4 % 2}_loaded"), 16)

            all_experts(pool, experts, token_results)
            square_sums("fin2")

        @block.tensor
        def _(pe):
            def mean_squares(n):
                if n == "a":
                    blocks = range(KB)
                else:
                    blocks = (0, KB - 1)
                    pe.wait_ge(s("norm_sum"), 6 * (nth(n) - 1))
                pe.wait_ge(s("norm_sq_ready"), KB * nth(n))
                for b in blocks:
                    mm = pe.matmul(ps[7][:], mean[:], sq[:, b, :], start=(b == 0), stop=(b == KB - 1))
                mm.then_inc(s("norm_ss_ready"), 1)

            def ada_unit(u, j):
                pe.wait_ge(s("ada_summed"), 4 * u + 4)
                wait(pe, s("mod_ready"), u - 1)
                for b in range(2):
                    mm = pe.matmul(ps[4 + j][:, b:b + 1], adaw[j][:, 0, b * P:(b + 1) * P], onec[:],
                                   start=True, stop=True)
                mm.then_inc(s("mod_prod"), 1)

            def linear(stage, rhs, kb, banks):
                units, _, _, used, per, _, base = plan[stage]
                for u in range(units):
                    ring_ready(pe, stage, u // 2, u % 2)
                    w = slot(u % 2, kb, per * P)
                    for b in range(per):
                        n = per * u + b
                        if n >= banks:
                            pe.wait_ge(s("lin_added"), base + n - banks + 1)
                        for k in range(kb):
                            mm = pe.matmul(ps[n % banks][:], w[:, k, b * P:(b + 1) * P], rhs[:, k, :],
                                           start=(k == 0), stop=(k == kb - 1))
                        mm.then_inc(S[used], 1)

            def feed_forward(l):
                stage = f"f{l}in"

                def body(i, first):
                    for j in range(2):
                        ring_ready(pe, stage, i, j)
                        w = slot(j, 8, 256)
                        for b in range(2):
                            if not first:
                                pe.wait_ge(s("ff_tap0"), 44 * l + 4 * i + 2 * j + b - 3)
                            for k in range(KB):
                                if first and j == 0 and b == 0:
                                    pe.wait_ge(s("norm_h_ready"), h_count(f"f{l}", k))
                                mm = pe.matmul(ps[2 * j + b][:], w[:, k, b * P:(b + 1) * P], hT[:, k, :],
                                               start=(k == 0), stop=(k == KB - 1))
                            mm.then_inc(s("ff_prod"), 1)
                        if l == 0:
                            ada_unit(2 * i + j, j)
                looped(pe, FB // 2, body)
                if l == 0:
                    for u in range(ADA, ADA_UNITS):
                        ada_unit(u, u % 2)
                pe.wait_ge(s("ff_act"), (l + 1) * FB)
                linear(f"f{l}dn", act, FB, 4)

            pe.wait_ge(s("consts"), 3)
            pe.wait_ge(s("x_loaded"), 16)
            for b in range(KB):
                for t in range(TT):
                    tr = pe.transpose(ps[b][:, t * P:(t + 1) * P], x_tok[:, t, b * P:(b + 1) * P], ident[:])
                tr.then_inc(s("x_turned"), 1)
            pe.wait_ge(s("params_loaded"), 16 * NPARAM)
            for t, rows in enumerate(PARAM_ROWS):
                wait(pe, s("x_ready"), t + 1)
                pe.transpose(ps[t][:, 0:rows], prow[0:rows, t, :], ident[0:rows, 0:rows])\
                    .then_inc(s("params_turned"), 1)
            pe.wait_ge(s("x_ready"), KB)
            pe.wait_ge(s("ws_step"), 1)
            for g in range(8):
                tr = pe.transpose(ps[6 + g // 4][:, (g % 4) * P:(g % 4 + 1) * P], wsraw[:, g, :], ident[:])
            tr.then_inc(s("ws_step"), 1)


            pe.wait_ge(s("ws_step"), 3)
            mean_squares("a")
            for u in range(4):
                ring_ready(pe, "gv", u // 2, u % 2)
                for t in range(TT):
                    wait(pe, s("gv_taken"), 4 * (u - 2) + t + 1)
                    if u == 1 and t == 3:
                        pe.wait_ge(s("norm_rms_ready"), nth("a"))
                    for k in range(KB):
                        if u == 0 and t == 0:
                            pe.wait_ge(s("norm_h_ready"), h_count("a", k))
                        mm = pe.matmul(ps[4 * (u % 2) + t][:, 0:256], hT[:, k, t * P:(t + 1) * P],
                                       slot(u % 2, 8, 256)[:, k, :], start=(k == 0), stop=(k == KB - 1))
                    mm.then_inc(s("gv_prod"), 1)
            pe.wait_ge(s("gv_taken"), 16)
            for u in range(4):
                ring_ready(pe, "gu", u // 2, u % 2)
                for b in range(2):
                    n = 2 * u + b
                    wait(pe, s("gu_taken"), n - 3)
                    for k in range(KB):
                        mm = pe.matmul(ps[n % 4][:], slot(u % 2, 8, 256)[:, k, b * P:(b + 1) * P], hT[:, k, :],
                                       start=(k == 0), stop=(k == KB - 1))
                    mm.then_inc(s("gu_prod"), 1)
            pe.wait_ge(s("vn_ready"), 4)
            for g in range(8):
                if g < 4:
                    bank = 4 + g
                else:
                    bank = g - 4
                    pe.wait_ge(s("gu_taken"), 8)
                for n in range(TT):
                    mm = pe.matmul(ps[bank][:, n * P:(n + 1) * P], vtok[:, n, g * P:(g + 1) * P], wsT[:, g, :],
                                   start=True, stop=True)
                mm.then_inc(s("sp_prod"), 1)
            pe.wait_ge(s("gated"), 8)
            linear("go", gT, KB, 4)
            mean_squares("f0")
            feed_forward(0)

            mean_squares("att")

            def pair(i, first):
                attention_projections(i, first)
                pe.wait_ge(s("qk_taken"), 2 * i + 2)
                attention_core(i, first)

            def attention_projections(i, first):
                ring_ready(pe, "att", i, 0)
                for b in range(2):
                    src = (hT, gT)[b]
                    for k in range(KB):
                        if first:
                            pe.wait_ge(s("norm_h_ready"), h_count("att", k, b))
                        mm = pe.matmul(ps[b][:], slot(0, 8, 256)[:, k, b * P:(b + 1) * P], src[:, k, :],
                                       start=(k == 0), stop=(k == KB - 1))
                    mm.then_inc(s("qkv_prod"), 1)
                ring_ready(pe, "att", i, 1)
                if not first:
                    pe.wait_ge(s("o_ready"), i)
                for t in range(TT):
                    for k in range(KB):
                        mm = pe.matmul(ps[2][:, t * P:(t + 1) * P], gT[:, k, t * P:(t + 1) * P],
                                       slot(1, 8, P)[:, k, :], start=(k == 0), stop=(k == KB - 1))
                mm.then_inc(s("qkv_prod"), 1)

            def attention_core(i, first):

                def scores(u):
                    h, qt = u // TT, u % TT
                    if not (first and u < 2):
                        pe.wait_ge(s("att_sc_added"), 8 * i + u - 1)
                    pe.matmul(ps[3 + u % 2][:, 0:(qt + 1) * P], qT[64 * h:64 * h + 64, qt * P:(qt + 1) * P],
                              kT[64 * h:64 * h + 64, 0:(qt + 1) * P], start=True, stop=True).then_inc(s("att_sc_prod"), 1)

                def turn(u):
                    pe.wait_ge(s("att_p_ready"), 8 * i + u + 1)
                    if not (first and u < 2):
                        pe.wait_ge(s("att_pt_taken"), 8 * i + u - 1)
                    for b in range(u % TT + 1):
                        tr = pe.transpose(ps[5 + u % 2][:, b * P:(b + 1) * P],
                                          p_sb[:, u % 2, b * P:(b + 1) * P], ident[:])
                    tr.then_inc(s("att_pt_prod"), 1)

                def values(u):
                    h, qt = u // TT, u % TT
                    pe.wait_ge(s("att_pt_taken"), 8 * i + u + 1)
                    if u == 0:
                        pe.wait_ge(s("v_taken"), i + 1)
                        if not first:
                            pe.wait_ge(s("att_o_norm"), i)
                    for b in range(qt + 1):
                        mm = pe.matmul(ps[7][:, qt * P + 64 * h:qt * P + 64 * h + 64],
                                       pT[:, u % 2, b * P:(b + 1) * P], vt[:, b, 64 * h:64 * h + 64],
                                       start=(b == 0), stop=(b == qt))
                    mm.then_inc(s("att_av_prod"), 1)

                scores(0)
                scores(1)
                for u in range(8):
                    turn(u)
                    if u + 2 < 8:
                        scores(u + 2)
                    if u >= 1:
                        values(u - 1)
                values(7)
                pe.wait_ge(s("att_o_norm"), i + 1)
                for t in range(TT):
                    tr = pe.transpose(ps[2][:, t * P:(t + 1) * P], o_sb[:, t * P:(t + 1) * P], ident[:])
                tr.then_inc(s("att_ot_prod"), 1)

            looped(pe, PAIRS, pair)
            pe.wait_ge(s("o_ready"), PAIRS)
            linear("wo", yT, KB, 2)
            mean_squares("f1")
            feed_forward(1)
            mean_squares("fin")
            mean_squares("n1")
            pe.wait_ge(s("side_loaded"), 64)
            for k in range(KB):
                pe.wait_ge(s("norm_h_ready"), h_count("n1", k))
                mm = pe.matmul(ps[0][0:24, :], favw[:, k, :], hT[:, k, :], start=(k == 0), stop=(k == KB - 1))
            mm.then_inc(s("fav_prod"), 1)
            pe.wait_ge(s("cum_ready"), 1)
            for t in range(TT):
                tr = pe.transpose(ps[1][:, 8 * t:8 * t + 8], fx8[3][:, t * P:(t + 1) * P], ident[0:8, 0:8])
            tr.then_inc(s("cq_step"), 1)
            pe.wait_ge(s("cq_step"), 2)

            def fox_pair(i, first):
                for j in range(2):
                    ring_ready(pe, "fx", i, j)
                    for b in range(2):
                        n = 2 * j + b
                        if not first:
                            if n == 0:
                                pe.wait_ge(s("fx_rms"), 3 * i)
                            if n == 2:
                                pe.wait_ge(s("fx_o_taken"), i)
                            if n == 3:
                                pe.wait_ge(s("att_sc_added"), 64 + 8 * i)
                        for k in range(KB):
                            mm = pe.matmul(ps[n][:], slot(j, 8, 256)[:, k, b * P:(b + 1) * P], hT[:, k, :],
                                           start=(k == 0), stop=(k == KB - 1))
                        mm.then_inc(s("fx_prod"), 1)
                for n, src in enumerate((sqq, sqk)):
                    pe.wait_ge(s("fx_sq"), 3 * i + n + 1)
                    pe.matmul(ps[n][:], halfm[:], src, start=True, stop=True).then_inc(s("fx_ms"), 1)
                pe.wait_ge(s("fx_mixed"), 2 * i + 2)
                for t in range(TT):
                    tr = pe.transpose(ps[2][:, t * P:(t + 1) * P], vmix[:, t * P:(t + 1) * P], ident[:])
                tr.then_inc(s("fx_vturned"), 1)
                pe.wait_ge(s("fx_taken"), 4 * i + 4)
                pe.wait_ge(s("fx_qk"), 2 * i + 2)
                attention_core(PAIRS + i, first)
                pe.wait_ge(s("fx_sq"), 3 * i + 3)
                pe.matmul(ps[0][:], halfm[:], sqq, start=True, stop=True).then_inc(s("fx_ms"), 1)
            looped(pe, 4, fox_pair)

            ring_ready(pe, "lora", 0, 0)
            pe.wait_ge(s("fx_rms"), 12)
            for k in range(KB):
                mm = pe.matmul(ps[0][:], slot(0, 8, P)[:, k, :], hT[:, k, :], start=(k == 0), stop=(k == KB - 1))
            mm.then_inc(s("lora_prod"), 1)
            ring_ready(pe, "lora", 0, 1)
            pe.wait_ge(s("fx_o_taken"), 4)
            for n, (c, m) in enumerate(((0, P), (P, 32))):
                for k in range(KB):
                    mm = pe.matmul(ps[1 + n][0:m, :], slot(1, 8, 160)[:, k, c:c + m], hT[:, k, :],
                                   start=(k == 0), stop=(k == KB - 1))
                mm.then_inc(s("lora_prod"), 1)
            pe.wait_ge(s("lora_ready"), 4)

            def rw_pair(i, first):
                if not first:
                    pe.wait_ge(s("rw_y_ready"), i)
                ring_ready(pe, "rw", i, 0)
                for b in range(2):
                    for k in range(KB):
                        mm = pe.matmul(ps[b][:], slot(0, 8, 256)[:, k, b * P:(b + 1) * P], hT[:, k, :],
                                       start=(k == 0), stop=(k == KB - 1))
                    mm.then_inc(s("rw_prod"), 1)
                ring_ready(pe, "rw", i, 1)
                for k in range(KB):
                    mm = pe.matmul(ps[2][:], slot(1, 8, P)[:, k, :], hT[:, k, :], start=(k == 0), stop=(k == KB - 1))
                mm.then_inc(s("rw_prod"), 1)
                for h in range(2):
                    pe.matmul(ps[3 + h][:], ring[64 * h:64 * h + 64, 1, 1024:1152], lwa[64 * h:64 * h + 64, :],
                              start=True, stop=True).then_inc(s("rw_prod"), 1)
                pe.matmul(ps[5][:], ring[:, 1, 1152:1280], lg0, start=True, stop=False)
                pe.matmul(ps[5][:], ring[0:32, 1, 1280:1408], lg1, start=False, stop=True).then_inc(s("rw_prod"), 1)
                for n in range(2):
                    pe.wait_ge(s("rw_sq"), 2 * i + n + 1)
                    pe.matmul(ps[6 + n][:], halfm[:], sqr, start=True, stop=True).then_inc(s("rw_ms"), 1)
                for n, src in enumerate((None, BT, KT, vv)):
                    if n == 0:
                        pe.wait_ge(s("rw_ops"), 4 * i + 4)
                        pe.wait_ge(s("rw_taken"), 6 * i + 6)
                    for t in range(TT):
                        tr = pe.transpose(ps[n][:, t * P:(t + 1) * P],
                                          AR[:, t, 0, :] if n == 0 else src[:, t * P:(t + 1) * P], ident[:])
                    tr.then_inc(s("rw_turned"), 1)
                for h in range(2):
                    own = slice(64 * h, 64 * h + 64)
                    for m, lhs in enumerate((BT, KT)):
                        for half in range(2):
                            n = 4 + 2 * m + half
                            if h == 1:
                                pe.wait_ge(s("rw_smt"), 10 * i + 2 * m + half + 1)
                            elif n == 6:
                                pe.wait_ge(s("rw_nrm"), i + 1)
                            elif n == 7:
                                pe.wait_ge(s("rw_bonus"), i + 1)
                            for t in range(2 * half, 2 * half + 2):
                                mm = pe.matmul(ps[n][:, (t % 2) * 256:(t % 2) * 256 + 256],
                                               lhs[own, t * P:(t + 1) * P], AR[own, t, :, :], start=True, stop=True)
                            mm.then_inc(s("rw_sm"), 1)
                    pe.wait_ge(s("rw_tok"), 4 * i + 4)
                    for t in range(TT):
                        mm = pe.matmul(ps[h][:, t * P:(t + 1) * P], AR[own, t, 0, :], BT[own, t * P:(t + 1) * P],
                                       start=True, stop=True)
                    mm.then_inc(s("rw_sm"), 1)
                for n in range(1, 6):
                    for h in range(2):
                        k = 2 * (n - 1) + h
                        pe.wait_ge(s("rw_am"), 10 * i + k + 1)
                        if n == 1:
                            pe.wait_ge(s("rw_d0"), 4 * i + 2 * h + 2)
                        else:
                            pe.wait_ge(s("rw_dt"), 20 * i + 2 * k - 2)
                        for t in range(TT):
                            mm = pe.matmul(ps[h][:, t * P:(t + 1) * P], Am[h][:, t, :], Dm[h][:, t, :],
                                           start=True, stop=True)
                        mm.then_inc(s("rw_x"), 1)
                    for h in range(2):
                        k = 2 * (n - 1) + h
                        pe.wait_ge(s("rw_xt"), 10 * i + k + 1)
                        if n == 1 and h == 0:
                            pe.wait_ge(s("rw_smt"), 10 * i + 10)
                        for w in range(2):
                            for t in range(TT):
                                mm = pe.matmul(ps[2 + 2 * w + h][:, t * P:(t + 1) * P], (DT, Xm)[w][h][:, t, :],
                                               (Xm, DT)[w][h][:, t, :], start=True, stop=True)
                            mm.then_inc(s("rw_dd"), 1)
                for t in range(TT):
                    for h in range(2):
                        mm = pe.matmul(ps[6][:, t * P + 64 * h:t * P + 64 * h + 64], AKT[h][:, t, 0:P],
                                       tokV[:, t, 64 * h:64 * h + 64], start=True, stop=True)
                mm.then_inc(s("rw_g"), 1)
                pe.wait_ge(s("rw_dt"), 20 * i + 20)
                for h in range(2):
                    for t in range(TT):
                        mm = pe.matmul(ps[0][64 * h:64 * h + 64, t * P:(t + 1) * P], tokA[:, t, 64 * h:64 * h + 64],
                                       DT[h][:, t, :], start=True, stop=True)
                mm.then_inc(s("rw_g"), 1)
                pe.wait_ge(s("rw_gt"), 3 * i + 1)
                for t in range(TT):
                    for h in range(2):
                        mm = pe.matmul(ps[7][:, t * P + 64 * h:t * P + 64 * h + 64], DT[h][:, t, :],
                                       Gm[:, t, 64 * h:64 * h + 64], start=True, stop=True)
                mm.then_inc(s("rw_g"), 1)
                pe.wait_ge(s("rw_gt"), 3 * i + 3)
                for c in range(8):
                    t, e = c // 2, c % 2
                    own = slice(64 * e, 64 * e + 64)
                    pe.wait_ge(s("rw_zt"), 8 * i + c + 1)
                    pe.matmul(ps[1 + e][own, 0:P], ApT[:, c * 64:c * 64 + 64], Zs[:, c, :], start=True, stop=True)\
                        .then_inc(s("rw_u"), 1)
                    if c < 7:
                        pe.matmul(ps[3 + e][:, 0:P], tokK[own, t, :], tokV[own, t, :], start=True, stop=False)
                        pe.wait_ge(s("rw_ut"), 8 * i + c + 1)
                        pe.matmul(ps[3 + e][:, 0:P], tokB[own, t, :], Usb[own, t, :], start=False, stop=True)\
                            .then_inc(s("rw_z"), 1)
                pe.wait_ge(s("rw_ut"), 8 * i + 8)
                for t in range(TT):
                    for e in range(2):
                        pe.matmul(ps[5][64 * e:64 * e + 64, t * P:(t + 1) * P], AR[:, t, 1, 64 * e:64 * e + 64],
                                  Zs[:, 2 * t + e, :], start=True, stop=False, skip_group_check=True)
                    for h in range(2):
                        cols = slice(64 * h, 64 * h + 64)
                        for m, (lhs, rhs) in enumerate(((ABT, Usb), (AKT, tokV))):
                            mm = pe.matmul(ps[5][:, t * P + 64 * h:t * P + 64 * h + 64], lhs[h][:, t, P:256],
                                           rhs[:, t, cols], start=False, stop=(m == 1), skip_group_check=True)
                mm.then_inc(s("rw_out_step"), 1)
                pe.wait_ge(s("rw_out_step"), 8 * i + 7)
                for t in range(TT):
                    tr = pe.transpose(ps[6][:, t * P:(t + 1) * P], y_sb[:, t * P:(t + 1) * P], ident[:])
                tr.then_inc(s("rw_out_step"), 1)
            looped(pe, 4, rw_pair)
            pe.wait_ge(s("rw_y_ready"), 4)
            linear("w_out", yT, KB, 4)

            mean_squares("n2")
            pe.wait_ge(s("side_loaded"), 64)
            for t in range(TT):
                for k in range(KB):
                    if t == 0:
                        pe.wait_ge(s("norm_h_ready"), h_count("n2", k))
                    mm = pe.matmul(ps[0][:, t * 64:t * 64 + 64], hT[:, k, t * P:(t + 1) * P], rwt[:, k, :],
                                   start=(k == 0), stop=(k == KB - 1))
            mm.then_inc(s("rt_prod"), 1)
            for t in range(TT):
                for half in range(2):
                    wait(pe, s("htok_taken"), 2 * (t - 1) + half + 1)
                    for b in range(4):
                        tr = pe.transpose(ps[2 + half][:, b * P:(b + 1) * P], hT[:, 4 * half + b, t * P:(t + 1) * P], ident[:])
                    tr.then_inc(s("htok_turned"), 1)
            pe.wait_ge(s("sh_loaded"), 48)
            w8 = sh_gu.rearrange("p (m k n) -> p m k n", m=2, k=KB)
            for m in range(2):
                for b in range(2):
                    for k in range(KB):
                        mm = pe.matmul(ps[4 + 2 * m + b][:], w8[:, m, k, b * P:(b + 1) * P], hT[:, k, :],
                                       start=(k == 0), stop=(k == KB - 1))
                    mm.then_inc(s("sh_gu_prod"), 1)
            pe.wait_ge(s("rt_masked"), 1)
            pe.wait_ge(s("moe_consts"), 5)
            for t in range(TT):
                for u in range(t + 1):
                    mm = pe.matmul(ps[0][:, t * 64:t * 64 + 64], (earlier if u == t else ones)[:], wtok[:, u, :],
                                   start=(u == 0), stop=(u == t))
            for t in range(TT):
                mm = pe.matmul(ps[1][:, 0:64], ones[:], wtok[:, t, :], start=(t == 0), stop=(t == TT - 1))
            mm.then_inc(s("places_prod"), 1)

            def places_tokens(n, par):
                pe.wait_ge(s("onehot_ready"), n + 1)
                wait(pe, s("slot_ready"), n)
                for t in range(TT):
                    mm = pe.matmul(ps[0][:, 0:1], onehot[par][:, t, :], tokid[:, t:t + 1],
                                   start=(t == 0), stop=(t == TT - 1))
                mm.then_inc(s("slot_prod"), 1)

            def turn_rows(n, par):
                pe.wait_ge(s(f"hrow{par}_loaded"), 8 * (n - par) + 16)
                wait(pe, s("hgt_act"), n)
                wait(pe, s("hgt_dve"), n)
                for half in range(2):
                    for b in range(4):
                        tr = pe.transpose(ps[1 + half][:, b * P:(b + 1) * P],
                                          hrow[par][:, (4 * half + b) * P:(4 * half + b + 1) * P], ident[:])
                    tr.then_inc(s("hrow_turned"), 1)

            places_tokens(0, 0)
            places_tokens(1, 1)
            wd = sh_dn.rearrange("p (k n) -> p k n", k=2)
            pe.wait_ge(s("sh_act"), 2)
            for b in range(KB):
                wait(pe, s("sh_added"), b - 3)
                for k in range(2):
                    mm = pe.matmul(ps[4 + b % 4][:], wd[:, k, b * P:(b + 1) * P], xact[:, k, :],
                                   start=(k == 0), stop=(k == 1))
                mm.then_inc(s("sh_prod"), 1)
            turn_rows(0, 0)
            pe.wait_ge(s("sh_added"), KB)

            def expert(n, par):
                w = exw[par]
                w8 = w[:, 0:4096].rearrange("p (m k n) -> p m k n", m=2, k=KB)
                wd = w[:, 4096:6144].rearrange("p (k n) -> p k n", k=2)
                pe.wait_ge(s(f"expgu{par}_loaded"), 16 * (n - par) + 32)
                pe.wait_ge(s("hgt_act"), n + 1)
                pe.wait_ge(s("hgt_dve"), n + 1)
                for m in range(2):
                    wait(pe, s(("exp_sil", "exp_act")[m]), n)
                    for b in range(2):
                        for k in range(KB):
                            mm = pe.matmul(ps[3 + m][:, b * P:(b + 1) * P], w8[:, m, k, b * P:(b + 1) * P],
                                           hgT[par][:, k, :], start=(k == 0), stop=(k == KB - 1))
                    mm.then_inc(s("exp_gu"), 1)
                turn_rows(n + 1, 1 - par)
                places_tokens(n + 2, par)
                pe.wait_ge(s("exp_act"), n + 1)
                pe.wait_ge(s(f"expdn{par}_loaded"), 8 * (n - par) + 16)
                for half in range(2):
                    wait(pe, s(("y_act", "y_dve")[half]), n)
                    for k in range(2):
                        mm = pe.matmul(ps[5 + half][:], eact[par][:, k * P:(k + 1) * P],
                                       wd[:, k, half * 512:(half + 1) * 512], start=(k == 0), stop=(k == 1))
                    mm.then_inc(s("exp_down"), 1)

            def experts(i, first):
                for par in range(2):
                    expert(2 * i + par, par)
            all_experts(pe, experts)
            for t in range(TT):
                pe.wait_ge(s("y_summed"), 6 * t + 6)
                for b in range(KB):
                    tr = pe.transpose(ps[b][:, t * P:(t + 1) * P], moe[:, t, b * P:(b + 1) * P], ident[:])
            tr.then_inc(s("moe_turned"), 1)
            mean_squares("fin2")
            for half in range(2):
                for t in range(TT):
                    n = TT * half + t
                    if n == 7:
                        pe.wait_ge(s("norm_rms_ready"), nth("fin2"))
                    for b in range(4 * half, 4 * half + 4):
                        if t == 0:
                            pe.wait_ge(s("norm_h_ready"), h_count("fin2", b))
                        tr = pe.transpose(ps[n][:, b % 4 * P:(b % 4 + 1) * P], hT[:, b, t * P:(t + 1) * P], ident[:])
                    tr.then_inc(s("out_turned"), 1)

        @block.scalar
        def _(act_e):
            order = Order(act_e, s("act_order"))

            def squares(n, ready, count):
                for b in range(KB):
                    act_e.wait_ge(S[ready], count if n == "a" else count - KB + b + 1)
                    nc.scalar.activation(sq[:, b, :], xT[:, b, :], ACT.Square).then_inc(s("norm_sq_ready"), 1)
                act_e.wait_ge(s("norm_ss_ready"), nth(n))
                nc.scalar.activation(rms[:], ps[7][:], ACT.Sqrt, bias=epsc[:]).then_inc(s("norm_rms_ready"), 1)

            def shift(n, c):
                for b in range(KB):
                    act_e.wait_ge(s("h_scaled"), KB * (n == "n2") + b + 1)
                    nc.scalar.activation(hT[:, b, :], hT[:, b, :], ACT.Identity, bias=mod[:, c + b:c + b + 1])\
                        .then_inc(s("norm_h_ready"), 1)

            def feed_forward(l):
                c0 = C_CONV + 256 * l

                def body(i, first):
                    for j in range(2):
                        for b in range(2):
                            blk = 2 * i + j + 22 * b
                            settle(act_e, s("ff_prod"), 44 * l + 4 * i + 2 * j + b + 1)
                            if not first:
                                settle(act_e, s("ff_act"), 22 * l + 2 * i + j - 1)
                            nc.scalar.activation(conv[j][b], ps[2 * j + b][:], ACT.Identity,
                                                 scale=col[:, bass.ds(c0 + P + blk, 1)],
                                                 bias=col[:, bass.ds(c0 + P + 44 + blk, 1)])\
                                .then_inc(s("ff_tap2"), 1)
                    for j in range(2):
                        settle(act_e, s("ff_tap0"), 44 * l + 4 * i + 2 * j + 2)
                        nc.scalar.activation(sil[j], conv[j][1], ACT.Silu).then_inc(s("ff_silu"), 1)
                looped(act_e, FB // 2, body)

            rows = lambda ap: ap.rearrange("(r c) -> r c", c=P)
            nload = 0

            def row_load(tile, r0, flat, n=None):
                nonlocal nload
                src = rows(flat)
                act_e.dma_start(prow[r0:r0 + src.shape[0], tile, 0:P], src).then_inc(s("params_loaded"), 16)
                nload += 1

            act_e.wait_ge(s("pool_order"), 2)
            for r, ap in ((C_A, a["a_norm_g"][0]), (C_KV, a["kv_norm_g"]), (C_B, a["b_norm_g"][0]),
                          (C_F, a["f_norm_g"].rearrange("l d -> (l d)")), (C_FIN, a["final_norm_g"]),
                          (C_N1, a["norm1_g_2"][0]), (C_N2, a["norm2_g_2"][0]), (C_FIN2, a["final_g_2"]),
                          (C_ADAB, a["ada_b_2"][0]), (C_VN, a["a_v_norm_g"][0])):
                row_load(0, r, ap)
            for l in range(2):
                row_load(1 + 2 * l, 0, a["f_conv_w"][l, 0:2].rearrange("k c -> (k c)"))
                row_load(2 + 2 * l, 0, a["f_conv_w"][l, 2])
                row_load(2 + 2 * l, 44, a["f_conv_b"][l])
            mu = a["rw_mu_2"][0]
            for c, ap in ((C_C, a["c_2"][0]), (C_QN, a["fox_qn_g_2"][0].rearrange("h d -> (h d)")),
                          (C_KN, a["fox_kn_g_2"][0].rearrange("h d -> (h d)")),
                          (C_ON, a["fox_on_g_2"][0].rearrange("h d -> (h d)")), (C_W0, a["rw_w0_2"][0]),
                          (C_A0, a["rw_a0_2"][0]), (C_KK, a["rw_k_k_2"][0]), (C_KA, a["rw_k_a_2"][0]),
                          (C_RK, a["rw_r_k_2"][0].rearrange("h d -> (h d)")), (C_LG, a["rw_lnx_g_2"][0]),
                          (C_LB, a["rw_lnx_b_2"][0]), (C_MU, mu[0:14 * P])):
                row_load(5, c - C5, ap)
            act_e.dma_start(prow[62:63, 5, 0:32], mu[14 * P:14 * P + 32].rearrange("(r c) -> r c", r=1))\
                .then_inc(s("params_loaded"), 16)
            nload += 1
            assert nload == NPARAM, nload

            for b in range(0, KB, 2):
                act_e.wait_ge(s("x_turned"), b + 1)
                act_e.wait_ge(s("x_ready"), b) if b else None
                nc.scalar.copy(xT[:, b, :], ps[b][:]).then_inc(s("x_ready"), 1)
            act_e.wait_ge(s("col_ready"), 6)
            nc.scalar.activation(csil[:], col[:, C_C:C_C + 8], ACT.Silu).then_inc(s("col_ready"), 1)
            squares("a", "x_ready", KB)
            act_e.wait_ge(s("consts"), NCONST)
            for u in range(4):
                for t in range(TT):
                    act_e.wait_ge(s("gv_prod"), 4 * u + t + 1)
                    nc.scalar.activation(vtok[:, t, u * 256:(u + 1) * 256], ps[4 * (u % 2) + t][:, 0:256],
                                         ACT.Gelu_apprx_tanh).then_inc(s("gv_taken"), 1)
            act_e.wait_ge(s("gv_taken"), 16)
            for t in range(TT):
                order(nc.scalar.activation(sq[:, 0:2, :], vtok[:, t, :].rearrange("p (a b) -> p a b", a=2), ACT.Square,
                                           accum_out=ss4[:, t:t + 1]))
            nc.scalar.activation(ss4[:, 4:8], ss4[:, 0:4], ACT.Sqrt, scale=1.0 / D, bias=epsc[:])\
                .then_inc(s("vrms_ready"), 1)
            for n in range(8):
                act_e.wait_ge(s("gu_prod"), n + 1)
                nc.scalar.activation(gT[:, n, :], ps[n % 4][:], ACT.Gelu_apprx_tanh).then_inc(s("gu_taken"), 1)
            squares("f0", "lin_added", KB)
            feed_forward(0)
            squares("att", "lin_added", 2 * KB)

            def pair(i, first):
                for b in range(2):
                    settle(act_e, s("qkv_prod"), 3 * i + b + 1)
                    if b == 0 and not first:
                        settle(act_e, s("att_sc_prod"), 8 * i)
                    nc.scalar.activation((qT, kT)[b], ps[b][:], ACT.Copy, scale=(HD ** -0.5, 1.0)[b])\
                        .then_inc(s("qk_taken"), 1)
                attention_core(i, first)
                settle(act_e, s("att_ot_prod"), i + 1)
                nc.scalar.copy(yT[:, bass.ds(i, 1), :], ps[2][:].rearrange("p (a b) -> p a b", a=1))\
                    .then_inc(s("o_ready"), 1)

            def attention_core(i, first):
                def exps(u):
                    n = (u % TT + 1) * P
                    settle(act_e, s("att_negm_ready"), 8 * i + u + 1)
                    if not (first and u < 2):
                        settle(act_e, s("att_pt_prod"), 8 * i + u - 1)
                    nc.scalar.activation(p_sb[:, u % 2, 0:n], s_sb[:, u % 2, 0:n], ACT.Exp, bias=negm[:, u:u + 1],
                                         accum_out=rsum[:, u:u + 1]).then_inc(s("att_p_ready"), 1)

                exps(0)
                for u in range(8):
                    if u < 7:
                        exps(u + 1)
                    n = (u % TT + 1) * P
                    settle(act_e, s("att_pt_prod"), 8 * i + u + 1)
                    if not (first and u < 2):
                        settle(act_e, s("att_av_prod"), 8 * i + u - 1)
                    nc.scalar.copy(pT[:, u % 2, 0:n], ps[5 + u % 2][:, 0:n]).then_inc(s("att_pt_taken"), 1)
            looped(act_e, PAIRS, pair)
            squares("f1", "lin_added", 3 * KB)
            feed_forward(1)
            squares("fin", "lin_added", 4 * KB)
            squares("n1", "norm_h_ready", h_count("fin", KB - 1))
            shift("n1", 0)
            act_e.wait_ge(s("fav_prod"), 1)
            nc.scalar.activation(sig24, ps[0][0:24, :], ACT.Sigmoid).then_inc(s("fav_sig"), 1)
            act_e.wait_ge(s("f_abs"), 1)
            order(nc.scalar.activation(fx8[2], fx8[1], ACT.Exp, scale=-1.0))
            nc.scalar.activation(fx8[2], fx8[2], ACT.Ln, bias=onec[0:8, :]).then_inc(s("f_log"), 1)

            def fox_pair(i, first):
                for n, (dst, fn) in enumerate(((qraw, ACT.Copy), (kpad[:, 1:T + 1], ACT.Copy),
                                               (vpad[:, 1:T + 1], ACT.Copy), (gsig, ACT.Sigmoid))):
                    settle(act_e, s("fx_prod"), 4 * i + n + 1)
                    if n == 0 and not first:
                        settle(act_e, s("fx_y_ready"), i)
                    nc.scalar.activation(dst, ps[n][:], fn).then_inc(s("fx_taken"), 1)
                settle(act_e, s("fx_taken"), 4 * i + 1)
                nc.scalar.activation(sqq, qraw, ACT.Square).then_inc(s("fx_sq"), 1)
                settle(act_e, s("fx_mixed"), 2 * i + 1)
                nc.scalar.activation(sqk, kmix, ACT.Square).then_inc(s("fx_sq"), 1)
                for n, dst in enumerate((rq, rk)):
                    settle(act_e, s("fx_ms"), 3 * i + n + 1)
                    nc.scalar.activation(dst, ps[n][:], ACT.Sqrt, bias=epsc[:]).then_inc(s("fx_rms"), 1)
                attention_core(PAIRS + i, first)
                settle(act_e, s("att_ot_prod"), PAIRS + i + 1)
                nc.scalar.copy(oraw, ps[2][:]).then_inc(s("fx_o_taken"), 1)
                settle(act_e, s("fx_o_taken"), i + 1)
                nc.scalar.activation(sqq, oraw, ACT.Square).then_inc(s("fx_sq"), 1)
                settle(act_e, s("fx_ms"), 3 * i + 3)
                nc.scalar.activation(rq, ps[0][:], ACT.Sqrt, bias=epsc[:]).then_inc(s("fx_rms"), 1)
            looped(act_e, 4, fox_pair)

            act_e.wait_ge(s("fx_y_ready"), 4)
            for n, (dst, m) in enumerate(((rp, P), (kp, P), (vp, 32))):
                act_e.wait_ge(s("lora_prod"), n + 1)
                act_e.wait_ge(s("pads"), 2)
                nc.scalar.copy(dst[0:m, 1:T + 1], ps[n][0:m, :]).then_inc(s("lora_taken"), 1)
            act_e.wait_ge(s("lora_mixed"), 3)
            nc.scalar.activation(lwa[0:64, :], rr[0:64, :], ACT.Tanh).then_inc(s("lora_ready"), 1)
            nc.scalar.copy(lwa[64:128, :], rr[64:128, :]).then_inc(s("lora_ready"), 1)
            nc.scalar.activation(lg0, k0, ACT.Sigmoid).then_inc(s("lora_ready"), 1)
            nc.scalar.activation(lg1, vv[0:32, :], ACT.Sigmoid).then_inc(s("lora_ready"), 1)

            def rw_pair(i, first):
                w0, a0 = col[:, bass.ds(C_W0 + i, 1)], col[:, bass.ds(C_A0 + i, 1)]
                for n, dst in enumerate((rp, kp, vp)):
                    settle(act_e, s("rw_prod"), 6 * i + n + 1)
                    if n == 0 and not first:
                        settle(act_e, s("rw_y_ready"), i)
                    if n == 0 and first:
                        act_e.wait_ge(s("lora_ready"), 4)
                    nc.scalar.copy(dst[:, 1:T + 1], ps[n][:]).then_inc(s("rw_taken"), 1)
                for n, (dst, b) in enumerate(((ld, w0), (aa, a0))):
                    settle(act_e, s("rw_prod"), 6 * i + n + 4)
                    nc.scalar.activation(dst, ps[3 + n][:], ACT.Sigmoid, bias=b).then_inc(s("rw_taken"), 1)
                settle(act_e, s("rw_prod"), 6 * i + 6)
                nc.scalar.copy(gg, ps[5][:]).then_inc(s("rw_taken"), 1)
                settle(act_e, s("rw_kk"), i + 1)
                nc.scalar.activation(sqr, kkn, ACT.Square).then_inc(s("rw_sq"), 1)
                settle(act_e, s("rw_ms"), 2 * i + 1)
                nc.scalar.activation(nrm, ps[6][:], ACT.Sqrt, scale=float(HD)).then_inc(s("rw_nrm"), 1)
                settle(act_e, s("rw_L"), 2 * i + 2)
                for dst, src, sc in ((Pt, Lc, 1.0), (Pinv, Lc, -1.0), (Pprev, Pprev, 1.0)):
                    nc.scalar.activation(dst, src, ACT.Exp, scale=sc).then_inc(s("rw_P"), 1)
                for n, dst in enumerate((tokA, tokB, tokK, tokV)):
                    settle(act_e, s("rw_turned"), 4 * i + n + 1)
                    nc.scalar.copy(dst, tiles4(ps[n][:])).then_inc(s("rw_tok"), 1)
                for n in range(1, 6):
                    for h in range(2):
                        k = 2 * (n - 1) + h
                        settle(act_e, s("rw_x"), 10 * i + k + 1)
                        if n > 1:
                            settle(act_e, s("rw_dd"), 20 * i + 2 * k - 2)
                        nc.scalar.copy(Xm[h], tiles4(ps[h][:])).then_inc(s("rw_xt"), 1)
                settle(act_e, s("rw_g"), 3 * i + 1)
                nc.scalar.copy(Gm, tiles4(ps[6][:])).then_inc(s("rw_gt"), 1)
                settle(act_e, s("rw_g"), 3 * i + 2)
                nc.scalar.copy(ApT, ps[0][:]).then_inc(s("rw_gt"), 1)
                settle(act_e, s("rw_g"), 3 * i + 3)
                nc.scalar.copy(Wm, tiles4(ps[7][:])).then_inc(s("rw_gt"), 1)
                settle(act_e, s("rw_out_step"), 8 * i + 1)
                nc.scalar.copy(y_sb, ps[5][:]).then_inc(s("rw_out_step"), 1)
                settle(act_e, s("rw_out_step"), 8 * i + 3)
                nc.scalar.activation(y_sq, y_sb, ACT.Square).then_inc(s("rw_out_step"), 1)
                settle(act_e, s("rw_out_step"), 8 * i + 5)
                nc.scalar.activation(st8[:, 0:8], st8[:, 8:16], ACT.Sqrt, scale=1.0 / HD, bias=lnxe[:])\
                    .then_inc(s("rw_out_step"), 1)
            looped(act_e, 4, rw_pair)

            squares("n2", "lin_added", 5 * KB)
            shift("n2", 24)
            act_e.wait_ge(s("rt_prod"), 1)
            nc.scalar.activation(sco, ps[0][:, 0:256].rearrange("p (t e) -> p t e", t=TT), ACT.Sigmoid)\
                .then_inc(s("rt_sig"), 1)

            for t in range(TT):
                for half in range(2):
                    act_e.wait_ge(s("htok_turned"), 2 * t + half + 1)
                    nc.scalar.copy(htok[:, t, half * 512:(half + 1) * 512], ps[2 + half][:]).then_inc(s("htok_taken"), 1)
                if t % 2:
                    act_e.wait_ge(s("htok_taken"), 2 * t + 2)
                    act_e.dma_start(h_dram[(t - 1) * P:(t + 1) * P, :].rearrange("(t p) d -> p t d", p=P),
                                    htok[:, t - 1:t + 1, :]).then_inc(s("h_stored"), 16)
            for b in range(2):
                act_e.wait_ge(s("sh_gu_prod"), b + 1)
                nc.scalar.activation(xsil[:, b, :], ps[4 + b][:], ACT.Silu).then_inc(s("sh_sil"), 1)

            def rows_half(n, par):
                settle(act_e, s("hrow_turned"), 2 * n + 1)
                settle(act_e, s("exp_gu"), 2 * n - 2)
                nc.scalar.copy(hgT[par][:, 0:4, :], tiles4(ps[1][:])).then_inc(s("hgt_act"), 1)

            rows_half(0, 0)

            def expert(n, par):
                settle(act_e, s("exp_gu"), 2 * n + 1)
                settle(act_e, s("exp_act"), n - 1)
                nc.scalar.activation(esil[par], ps[3][:, 0:256], ACT.Silu).then_inc(s("exp_sil"), 1)
                rows_half(n + 1, 1 - par)
                settle(act_e, s("exp_down"), 2 * n + 1)
                settle(act_e, s(f"y{par}_stored"), 8 * (n - par))
                nc.scalar.copy(yrow[par][:, 0:512], ps[5][:]).then_inc(s("y_act"), 1)
                settle(act_e, s("y_act"), n + 1)
                settle(act_e, s("y_dve"), n + 1)
                act_e.dma_start(y_dram[bass.ds(n * P, P), :], yrow[par]).then_inc(s(f"y{par}_stored"), 16)

            def experts(i, first):
                for par in range(2):
                    expert(2 * i + par, par)
            all_experts(act_e, experts)
            squares("fin2", "moe_added", KB)
            for t in range(TT):
                act_e.wait_ge(s("out_turned"), t + 1)
                order(nc.scalar.copy(out_tok[:, t, 0:512], ps[t][:]))
            act_e.dma_start(out[0, :, 0:512].rearrange("(t p) d -> p t d", p=P), out_tok[:, :, 0:512])\
                .then_inc(s("x_loaded"), 16)

        @block.vector
        def _(dve):
            order = Order(dve, s("dve_order"))

            def normalise(n, outs):
                dve.wait_ge(s("norm_rms_ready"), nth(n))
                order(nc.vector.reciprocal(rstd[:], rms[:]))
                for dst, gain in outs:
                    for b in range(KB):
                        nc.vector.scalar_tensor_tensor(out=dst[:, b, :], in0=xT[:, b, :],
                                                       scalar=col[:, gain + b:gain + b + 1], in1=rstd[:],
                                                       op0=ALU.mult, op1=ALU.mult).then_inc(s("norm_h_ready"), 1)

            def add_linear(stage, banks):
                base = plan[stage][6]
                for n in range(KB):
                    dve.wait_ge(s("lin_prod"), base + n + 1)
                    nc.vector.tensor_tensor(xT[:, n, :], ps[n % banks][:], xT[:, n, :], ALU.add)\
                        .then_inc(s("lin_added"), 1)

            def feed_forward(l):
                c0 = C_CONV + 256 * l

                def body(i, first):
                    for j in range(2):
                        for b in range(2):
                            blk = 2 * i + j + 22 * b
                            c = conv[j][b]
                            n = 44 * l + 4 * i + 2 * j + b + 1
                            settle(dve, s("ff_tap2"), n)
                            nc.vector.scalar_tensor_tensor(
                                out=c[:, 1:T], in0=ps[2 * j + b][:, 0:T - 1],
                                scalar=col[:, bass.ds(c0 + 44 + blk, 1)], in1=c[:, 1:T],
                                op0=ALU.mult, op1=ALU.add).then_inc(s("ff_tap1"), 1)
                            settle(dve, s("ff_tap1"), n)
                            nc.vector.scalar_tensor_tensor(
                                out=c[:, 2:T], in0=ps[2 * j + b][:, 0:T - 2],
                                scalar=col[:, bass.ds(c0 + blk, 1)], in1=c[:, 2:T],
                                op0=ALU.mult, op1=ALU.add).then_inc(s("ff_tap0"), 1)
                        if l == 0:
                            ada_unit(2 * i + j, j)
                    for j in range(2):
                        settle(dve, s("ff_silu"), 22 * l + 2 * i + j + 1)
                        nc.vector.tensor_tensor(act[:, bass.ds(2 * i + j, 1), :],
                                                sil[j].rearrange("p (a b) -> p a b", a=1),
                                                conv[j][0].rearrange("p (a b) -> p a b", a=1), ALU.mult)\
                            .then_inc(s("ff_act"), 1)
                looped(dve, FB // 2, body)
                if l == 0:
                    for u in range(ADA, ADA_UNITS):
                        ada_unit(u, u % 2)
                add_linear(f"f{l}dn", 4)

            for b in range(1, KB, 2):
                dve.wait_ge(s("x_turned"), b + 1)
                dve.wait_ge(s("x_ready"), b)
                nc.vector.tensor_copy(xT[:, b, :], ps[b][:]).then_inc(s("x_ready"), 1)
            for t, rows in enumerate(PARAM_ROWS):
                dve.wait_ge(s("params_turned"), t + 1)
                nc.vector.tensor_copy(col[:, t * P:t * P + rows], ps[t][:, 0:rows]).then_inc(s("col_ready"), 1)
            dve.wait_ge(s("rel_loaded"), 16)
            nc.vector.tensor_copy(relE[:, REL:RELW], relE[:, REL - 1:REL].to_broadcast([16, RELW - REL]))\
                .then_inc(s("rel_ext"), 1)
            dve.wait_ge(s("rel_ext"), 1)
            nc.vector.tensor_copy(relR[:], relE[:, ::-1]).then_inc(s("rel_ext"), 1)
            dve.wait_ge(s("ws_loaded"), 32)
            nc.vector.memset(wsraw[0:64, :, 64:128], 0.0).then_inc(s("ws_step"), 1)
            dve.wait_ge(s("ws_step"), 2)
            order(nc.vector.tensor_copy(wsT[:, 0:4, :], ps[6][:].rearrange("p (g j) -> p g j", g=4)))
            nc.vector.tensor_copy(wsT[:, 4:8, :], ps[7][:].rearrange("p (g j) -> p g j", g=4)).then_inc(s("ws_step"), 1)

            def ada_unit(u, j):
                settle(dve, s("mod_prod"), u + 1)
                nc.vector.tensor_tensor(mod[:, bass.ds(2 * u, 2)], ps[4 + j][:, 0:2],
                                        col[:, bass.ds(C_ADAB + 2 * u, 2)], ALU.add).then_inc(s("mod_ready"), 1)

            normalise("a", [(hT, C_A)])
            dve.wait_ge(s("vrms_ready"), 1)
            order(nc.vector.reciprocal(ss4[:, 8:12], ss4[:, 4:8]))
            for t in range(TT):
                nc.vector.tensor_scalar(vtok[:, t, :], vtok[:, t, :], ss4[:, 8 + t:9 + t], None, ALU.mult)\
                    .then_inc(s("vn_ready"), 1)
            dve.wait_ge(s("ws_loaded"), 32)
            dve.wait_ge(s("gu_taken"), 8)
            for g in range(8):
                dve.wait_ge(s("sp_prod"), g + 1)
                bank = 4 + g if g < 4 else g - 4
                order(nc.vector.scalar_tensor_tensor(
                    out=sptmp.rearrange("p (n i) -> p n i", n=TT), in0=ps[bank][:].rearrange("p (n i) -> p n i", n=TT),
                    scalar=col[:, C_VN + g:C_VN + g + 1],
                    in1=bsb[:, g, :].unsqueeze(1).to_broadcast([P, TT, P]), op0=ALU.mult, op1=ALU.add))
                nc.vector.tensor_tensor(gT[:, g, :], gT[:, g, :], sptmp, ALU.mult).then_inc(s("gated"), 1)
                dve.wait_ge(s("gated"), g + 1)
            add_linear("go", 4)
            normalise("f0", [(hT, C_F)])
            feed_forward(0)
            normalise("att", [(hT, C_B), (gT, C_KV)])
            dve.wait_ge(s("consts"), NCONST)
            dve.wait_ge(s("rel_stored"), 32)

            def pair(i, first):
                dve.wait_ge(s("qkv_prod"), 3 * i + 3)
                if not first:
                    dve.wait_ge(s("att_av_prod"), 8 * i)
                nc.vector.tensor_copy(vt, ps[2][:].rearrange("p (t c) -> p t c", t=TT)).then_inc(s("v_taken"), 1)
                for u in range(8):
                    h, qt = u // TT, u % TT
                    n, far = (qt + 1) * P, max(qt - 1, 0) * P
                    sc = ps[3 + u % 2]
                    settle(dve, s("att_sc_prod"), 8 * i + u + 1)
                    if not (first and u < 2):
                        settle(dve, s("att_p_ready"), 8 * i + u - 1)
                    if far:
                        nc.vector.tensor_scalar(s_sb[:, u % 2, 0:far], sc[:, 0:far],
                                                biasT[:, bass.ds(2 * i + h, 1), 0:1].rearrange("p a b -> p (a b)"), None, ALU.add)
                    nc.vector.tensor_tensor(s_sb[:, u % 2, far:n].unsqueeze(1), sc[:, far:n].unsqueeze(1),
                                            biasT[:, bass.ds(2 * i + h, 1), 256 - (n - far):256],
                                            ALU.add).then_inc(s("att_sc_added"), 1)
                    row_max(i, u, n)
                attention_out(i, first)

            def row_max(i, u, n):
                dve.wait_ge(s("att_sc_added"), 8 * i + u + 1)
                nc.vector.tensor_reduce(mx[:, u:u + 1], s_sb[:, u % 2, 0:n], AX.X, ALU.max).then_inc(s("att_sc_max"), 1)
                settle(dve, s("att_sc_max"), 8 * i + u + 1)
                nc.vector.tensor_scalar(negm[:, u:u + 1], mx[:, u:u + 1], -1.0, None, ALU.mult)\
                    .then_inc(s("att_negm_ready"), 1)

            def attention_out(i, first):
                settle(dve, s("att_p_ready"), 8 * i + 8)
                nc.vector.reciprocal(rinv, rsum).then_inc(s("att_r_inv"), 1)
                settle(dve, s("att_r_inv"), i + 1)
                dve.wait_ge(s("att_av_prod"), 8 * i + 8)
                if not first:
                    dve.wait_ge(s("att_ot_prod"), i)
                nc.vector.tensor_tensor(o_sb.rearrange("p (t h d) -> p h t d", t=TT, h=2),
                                        ps[7][:].rearrange("p (t h d) -> p h t d", t=TT, h=2),
                                        rinv.rearrange("p (h t) -> p h t", h=2).unsqueeze(3)
                                        .to_broadcast([P, 2, TT, HD]), ALU.mult).then_inc(s("att_o_norm"), 1)
            looped(dve, PAIRS, pair)
            add_linear("wo", 2)
            normalise("f1", [(hT, C_F + 8)])
            feed_forward(1)
            normalise("fin", [(xT, C_FIN)])

            def normalise_mod(n, gain):
                dve.wait_ge(s("norm_rms_ready"), nth(n))
                order(nc.vector.reciprocal(rstd[:], rms[:]))
                for b in range(KB):
                    nc.vector.scalar_tensor_tensor(out=hT[:, b, :], in0=xT[:, b, :], scalar=gmod[:, gain + b:gain + b + 1],
                                                   in1=rstd[:], op0=ALU.mult, op1=ALU.mult).then_inc(s("h_scaled"), 1)

            dve.wait_ge(s("mod_ready"), ADA_UNITS)
            nc.vector.scalar_tensor_tensor(out=gmod[:, 0:8], in0=mod[:, 8:16], scalar=1.0, in1=col[:, C_N1:C_N1 + 8],
                                           op0=ALU.add, op1=ALU.mult)
            nc.vector.scalar_tensor_tensor(out=gmod[:, 8:16], in0=mod[:, 32:40], scalar=1.0, in1=col[:, C_N2:C_N2 + 8],
                                           op0=ALU.add, op1=ALU.mult)
            order(nc.vector.tensor_scalar(qn8, col[:, C_QN:C_QN + 4], HD ** -0.5, None, ALU.mult))
            normalise_mod("n1", 0)
            nc.vector.memset(kpad[:, 0:1], 0.0)
            nc.vector.memset(vpad[:, 0:1], 0.0).then_inc(s("pads"), 1)
            dve.wait_ge(s("side_loaded"), 64)
            dve.wait_ge(s("fav_sig"), 1)
            order(nc.vector.tensor_scalar(fx8[0], ps[0][0:8, :], fbias[:], None, ALU.add))
            nc.vector.scalar_tensor_tensor(out=fx8[1], in0=fx8[0], scalar=-1.0, in1=fx8[0], op0=ALU.mult, op1=ALU.max)\
                .then_inc(s("f_abs"), 1)
            dve.wait_ge(s("f_log"), 1)
            order(nc.vector.scalar_tensor_tensor(out=fx8[1], in0=fx8[0], scalar=0.0, in1=fx8[2], op0=ALU.min,
                                                 op1=ALU.subtract))
            nc.vector.tensor_tensor_scan(fx8[3], ones8[:], fx8[1], 0.0, ALU.mult, ALU.add).then_inc(s("cum_ready"), 1)
            dve.wait_ge(s("cq_step"), 1)
            nc.vector.tensor_copy(cq, ps[1][:, 0:32].rearrange("p (t h) -> p t h", t=TT)).then_inc(s("cq_step"), 1)
            dve.wait_ge(s("cq_step"), 2)
            dve.wait_ge(s("pads"), 1)
            steps = Order(dve, s("fx_order"), (s("consts"), NCONST))

            def token_shift(dst, pad, gate):
                steps(nc.vector.tensor_tensor(dst, pad[:, 0:T], pad[:, 1:T + 1], ALU.subtract))
                steps(nc.vector.tensor_tensor(dst, dst, gate, ALU.mult))
                nc.vector.tensor_tensor(dst, dst, pad[:, 1:T + 1], ALU.add).then_inc(s("fx_mixed"), 1)

            def fox_pair(i, first):
                steps.round(i, 16)
                settle(dve, s("fx_rows"), 80 * i + 80)
                settle(dve, s("fx_taken"), 4 * i + 2)
                token_shift(kmix, kpad, akb)
                settle(dve, s("fx_taken"), 4 * i + 3)
                token_shift(vmix, vpad, avb)
                settle(dve, s("fx_mixed"), 2 * i + 2)
                for n, (dst, src, r, gain) in enumerate(((qT, qraw, rq, small[:, bass.ds(48 + i, 1)]),
                                                         (kT, kmix, rk, col[:, bass.ds(C_KN + i, 1)]))):
                    settle(dve, s("fx_rms"), 3 * i + n + 1)
                    steps(nc.vector.reciprocal(r, r))
                    nc.vector.scalar_tensor_tensor(out=dst, in0=src, scalar=gain, in1=r, op0=ALU.mult, op1=ALU.mult)\
                        .then_inc(s("fx_qk"), 1)
                settle(dve, s("fx_vturned"), i + 1)
                nc.vector.tensor_copy(vt, ps[2][:].rearrange("p (t c) -> p t c", t=TT)).then_inc(s("v_taken"), 1)
                for u in range(8):
                    h, qt = u // TT, u % TT
                    n = (qt + 1) * P
                    settle(dve, s("att_sc_prod"), 64 + 8 * i + u + 1)
                    if not (first and u < 2):
                        settle(dve, s("att_p_ready"), 64 + 8 * i + u - 1)
                    row = s_sb[:, u % 2, :]
                    steps(nc.vector.scalar_tensor_tensor(out=row[:, 0:n], in0=ps[3 + u % 2][:, 0:n],
                                                         scalar=cq[:, qt, bass.ds(2 * i + h, 1)], in1=ckb[:, h, 0:n],
                                                         op0=ALU.add, op1=ALU.subtract))
                    nc.vector.tensor_tensor(row[:, n - P:n], row[:, n - P:n], tri[:], ALU.add)\
                        .then_inc(s("att_sc_added"), 1)
                    row_max(PAIRS + i, u, n)
                attention_out(PAIRS + i, first)
                settle(dve, s("fx_rms"), 3 * i + 3)
                steps(nc.vector.reciprocal(rq, rq))
                steps(nc.vector.scalar_tensor_tensor(out=kmix, in0=oraw, scalar=col[:, bass.ds(C_ON + i, 1)], in1=rq,
                                                     op0=ALU.mult, op1=ALU.mult))
                one = lambda x: x.rearrange("p (a b) -> p a b", a=1)
                nc.vector.tensor_tensor(yT[:, bass.ds(i, 1), :], one(kmix), one(gsig), ALU.mult)\
                    .then_inc(s("fx_y_ready"), 1)
            looped(dve, 4, fox_pair)

            dve.wait_ge(s("fx_y_ready"), 4)
            dve.wait_ge(s("att_av_prod"), 96)
            nc.vector.memset(rp[:, 0:1], 0.0)
            nc.vector.memset(kp[:, 0:1], 0.0)
            nc.vector.memset(vp[:, 0:1], 0.0).then_inc(s("pads"), 1)
            dve.wait_ge(s("pads"), 2)

            def shifted(step, dst, pad, mu, m=P):
                step(nc.vector.tensor_tensor(dd[0:m, :], pad[0:m, 0:T], pad[0:m, 1:T + 1], ALU.subtract))
                return nc.vector.scalar_tensor_tensor(out=dst[0:m, :], in0=dd[0:m, :], scalar=mu, in1=pad[0:m, 1:T + 1],
                                                      op0=ALU.mult, op1=ALU.add)

            for n, (dst, pad, m) in enumerate(((rr, rp, P), (k0, kp, P), (vv, vp, 32))):
                dve.wait_ge(s("lora_taken"), n + 1)
                shifted(order, dst, pad, col[0:m, C_MU + 12 + n:C_MU + 13 + n], m).then_inc(s("lora_mixed"), 1)
                dve.wait_ge(s("lora_mixed"), n + 1)
            dve.wait_ge(s("lora_ready"), 4)
            rsteps = Order(dve, s("rw_order"), (s("consts"), NCONST))
            ar4 = lambda x: x.rearrange("p (t c) -> p t c", t=TT)

            def rw_pair(i, first):
                rsteps.round(i, 27)
                for n, (dst, pad) in enumerate(((rr, rp), (k0, kp), (vv, vp))):
                    settle(dve, s("rw_taken"), 6 * i + n + 1)
                    rsteps(shifted(rsteps, dst, pad, col[:, bass.ds(C_MU + 4 * n + i, 1)]))
                nc.vector.tensor_scalar(kkn, k0, col[:, bass.ds(C_KK + i, 1)], None, ALU.mult).then_inc(s("rw_kk"), 1)
                settle(dve, s("rw_taken"), 6 * i + 4)
                rsteps(nc.vector.tensor_scalar(ld, ld, -E_DECAY, None, ALU.mult))
                nc.vector.tensor_tensor_scan(Lc, cmask[:], ld, 0.0, ALU.mult, ALU.add).then_inc(s("rw_L"), 1)
                settle(dve, s("rw_L"), 2 * i + 1)
                nc.vector.tensor_tensor(Pprev, Lc, ld, ALU.subtract).then_inc(s("rw_L"), 1)
                settle(dve, s("rw_nrm"), i + 1)
                rsteps(nc.vector.tensor_scalar(nrm, nrm, 1e-12, None, ALU.max))
                rsteps(nc.vector.reciprocal(nrm, nrm))
                rsteps(nc.vector.tensor_tensor(kkn, kkn, nrm, ALU.mult))
                settle(dve, s("rw_taken"), 6 * i + 5)
                rsteps(nc.vector.tensor_scalar(dd, aa, 1.0, col[:, bass.ds(C_KA + i, 1)], ALU.subtract, ALU.mult))
                rsteps(nc.vector.scalar_tensor_tensor(out=k0, in0=dd, scalar=1.0, in1=k0, op0=ALU.add, op1=ALU.mult))
                settle(dve, s("rw_ms"), 2 * i + 1)
                nc.vector.scalar_tensor_tensor(out=sqr, in0=rr, scalar=col[:, bass.ds(C_RK + i, 1)], in1=k0,
                                               op0=ALU.mult, op1=ALU.mult).then_inc(s("rw_sq"), 1)
                rsteps(nc.vector.tensor_tensor(dd, kkn, aa, ALU.mult))
                settle(dve, s("rw_P"), 3 * i + 3)
                nc.vector.scalar_tensor_tensor(out=AR[:, :, 0, :], in0=ar4(kkn), scalar=-1.0, in1=ar4(Pprev),
                                               op0=ALU.mult, op1=ALU.mult).then_inc(s("rw_ops"), 1)
                nc.vector.tensor_tensor(AR[:, :, 1, :], ar4(rr), ar4(Pt), ALU.mult).then_inc(s("rw_ops"), 1)
                nc.vector.tensor_tensor(BT, dd, Pinv, ALU.mult).then_inc(s("rw_ops"), 1)
                nc.vector.tensor_tensor(KT, k0, Pinv, ALU.mult).then_inc(s("rw_ops"), 1)
                settle(dve, s("rw_ms"), 2 * i + 2)
                nc.vector.scalar_tensor_tensor(out=nrm, in0=ps[7][:], scalar=float(HD), in1=vv, op0=ALU.mult,
                                               op1=ALU.mult).then_inc(s("rw_bonus"), 1)
                nc.vector.memset(Zs[:, 0, :], 0.0).then_inc(s("rw_zt"), 1)
                for h in range(2):
                    for n in range(4):
                        settle(dve, s("rw_sm"), 10 * i + 5 * h + n + 1)
                        half = n % 2
                        dst = (ABT, AKT)[n // 2][h][:, 2 * half:2 * half + 2, :]
                        nc.vector.tensor_tensor(dst, ps[4 + n][:].rearrange("p (t c) -> p t c", t=2),
                                                maskAR[:].unsqueeze(1).to_broadcast([P, 2, 256]), ALU.mult)\
                            .then_inc(s("rw_smt"), 1)
                    settle(dve, s("rw_sm"), 10 * i + 5 * h + 5)
                    nc.vector.tensor_tensor(Dm[h], tiles4(ps[h][:]), bc4(mask1[:]), ALU.mult).then_inc(s("rw_smt"), 1)
                    settle(dve, s("rw_smt"), 10 * i + 5 * h + 5)
                    rsteps(nc.vector.tensor_tensor(DT[h], ABT[h][:, :, 0:P], bc4(maskT[0][:]), ALU.mult))
                    nc.vector.tensor_tensor(Dm[h], Dm[h], bc4(ident[:]), ALU.add).then_inc(s("rw_d0"), 1)
                    nc.vector.tensor_tensor(DT[h], DT[h], bc4(ident[:]), ALU.add).then_inc(s("rw_d0"), 1)
                settle(dve, s("rw_d0"), 4 * i + 4)
                for n in range(1, 6):
                    for h in range(2):
                        for w in range(2):
                            k = 4 * (n - 1) + 2 * h + w
                            settle(dve, s("rw_dd"), 20 * i + 4 * (n - 1) + 2 * h + 2)
                            m = (Dm, DT)[w][h]
                            nc.vector.tensor_tensor(m, tiles4(ps[2 + 2 * w + h][:]), m, ALU.add).then_inc(s("rw_dt"), 1)
                    settle(dve, s("rw_dt"), 20 * i + 4 * n)
                settle(dve, s("rw_gt"), 3 * i + 3)
                for c in range(8):
                    t, e = c // 2, c % 2
                    own = slice(64 * e, 64 * e + 64)
                    settle(dve, s("rw_u"), 8 * i + c + 1)
                    nc.vector.tensor_tensor(Usb[own, t, :], ps[1 + e][own, 0:P], Wm[own, t, :], ALU.add)\
                        .then_inc(s("rw_ut"), 1)
                    if c < 7:
                        last = Pt[:, 64 * c + 63:64 * c + 64]
                        settle(dve, s("rw_z"), 7 * i + c + 1)
                        rsteps(nc.vector.scalar_tensor_tensor(out=ztmp, in0=ps[3 + e][:, 0:P], scalar=last, in1=bdiag[:],
                                                              op0=ALU.mult, op1=ALU.mult))
                        nc.vector.scalar_tensor_tensor(out=Zs[:, c + 1, :], in0=Zs[:, c, :], scalar=last, in1=ztmp,
                                                       op0=ALU.mult, op1=ALU.add).then_inc(s("rw_zt"), 1)
                        settle(dve, s("rw_zt"), 8 * i + c + 2)
                y8 = y_sb.rearrange("p (u d) -> p u d", d=HD)
                bc8 = lambda x: x.unsqueeze(2).to_broadcast([P, 8, HD])
                settle(dve, s("rw_out_step"), 8 * i + 2)
                rsteps(nc.vector.tensor_reduce(st8[:, 0:8], y8, AX.X, ALU.add))
                rsteps(nc.vector.tensor_scalar(st8[:, 0:8], st8[:, 0:8], 1.0 / HD, None, ALU.mult))
                nc.vector.tensor_tensor(y8, y8, bc8(st8[:, 0:8]), ALU.subtract).then_inc(s("rw_out_step"), 1)
                settle(dve, s("rw_out_step"), 8 * i + 4)
                nc.vector.tensor_reduce(st8[:, 8:16], y_sq.rearrange("p (u d) -> p u d", d=HD), AX.X, ALU.add)\
                    .then_inc(s("rw_out_step"), 1)
                settle(dve, s("rw_out_step"), 8 * i + 6)
                rsteps(nc.vector.reciprocal(st8[:, 0:8], st8[:, 0:8]))
                settle(dve, s("rw_out_step"), 8 * i + 3)
                nc.vector.tensor_tensor(y8, y8, bc8(st8[:, 0:8]), ALU.mult).then_inc(s("rw_out_step"), 1)
                settle(dve, s("rw_out_step"), 8 * i + 8)
                rsteps(nc.vector.tensor_scalar(dd, ps[6][:], col[:, bass.ds(C_LG + i, 1)],
                                               col[:, bass.ds(C_LB + i, 1)], ALU.mult, ALU.add))
                rsteps(nc.vector.tensor_tensor(dd, dd, nrm, ALU.add))
                one = lambda x: x.rearrange("p (a b) -> p a b", a=1)
                settle(dve, s("rw_taken"), 6 * i + 6)
                nc.vector.tensor_tensor(yT[:, bass.ds(4 + i, 1), :], one(dd), one(gg), ALU.mult)\
                    .then_inc(s("rw_y_ready"), 1)
            looped(dve, 4, rw_pair)

            for n in range(KB):
                dve.wait_ge(s("lin_prod"), 4 * KB + n + 1)
                nc.vector.scalar_tensor_tensor(out=xT[:, n, :], in0=ps[n % 4][:], scalar=mod[:, 16 + n:17 + n],
                                               in1=xT[:, n, :], op0=ALU.mult, op1=ALU.add)\
                    .then_inc(s("lin_added"), 1)

            normalise_mod("n2", 8)
            dve.wait_ge(s("side_loaded"), 64)
            dve.wait_ge(s("rt_sig"), 1)

            def top(vals, kth, k, mask, eq, at, starts, n):
                kb = kth.to_broadcast([P, TT, n])
                flat = lambda x: x.rearrange("p t e -> p (t e)")
                order(nc.vector.tensor_tensor(mask, vals, kb, ALU.is_gt))
                order(nc.vector.tensor_tensor(eq, vals, kb, ALU.is_equal))
                order(nc.vector.tensor_reduce(room, mask, AX.X, ALU.add))
                order(nc.vector.tensor_scalar(room, room, -1.0, float(k), ALU.mult, ALU.add))
                order(nc.vector.tensor_tensor_scan(flat(at), starts, flat(eq), 0.0, ALU.mult, ALU.add))
                order(nc.vector.tensor_tensor(at, at, room.to_broadcast([P, TT, n]), ALU.is_le))
                order(nc.vector.tensor_tensor(eq, eq, at, ALU.mult))
                order(nc.vector.tensor_tensor(mask, mask, eq, ALU.add))

            u8 = lambda x: x.rearrange("p t (g e) -> p (t g) e", e=8)
            order(nc.vector.tensor_tensor(sel, sco, rbias[:].unsqueeze(1).to_broadcast([P, TT, 64]), ALU.add))
            for u in range(32):
                mxi = nc.vector.max(srt[:, u, :], u8(sel)[:, u, :])
            order(mxi)
            order(nc.vector.tensor_tensor(gsc.rearrange("p t (g o) -> p (t g) o", o=1), srt[:, :, 0:1], srt[:, :, 1:2], ALU.add))
            for t in range(TT):
                mxi = nc.vector.max(gsrt[:, t, :], gsc[:, t, :])
            order(mxi)
            top(gsc, gsrt[:, :, 3:4], 4, gmask, geq, gpos, cm8[:], 8)
            order(nc.vector.tensor_scalar(gmask, gmask, 1.0, 1e30, ALU.subtract, ALU.mult))
            order(nc.vector.tensor_tensor(u8(sel), u8(sel), gmask.rearrange("p t (g o) -> p (t g) o", o=1)
                                          .to_broadcast([P, 32, 8]), ALU.add))
            for t in range(TT):
                mxi = nc.vector.max(esrt[:, t, :], sel[:, t, :])
            order(mxi)
            top(sel, esrt[:, :, 5:6], 6, wtok, eqm, pos, cmask[:, 0:256], 64)
            nc.vector.tensor_tensor(sco, wtok, sco, ALU.mult).then_inc(s("rt_masked"), 1)
            dve.wait_ge(s("rt_masked"), 1)
            order(nc.vector.tensor_reduce(wsum, sco, AX.X, ALU.add))
            order(nc.vector.reciprocal(wsum, wsum))
            order(nc.vector.tensor_scalar(wsum, wsum, 2.5, None, ALU.mult))
            order(nc.vector.tensor_tensor(sco, sco, wsum.to_broadcast([P, TT, EXPERTS]), ALU.mult))
            order(nc.vector.memset(place[:, :, ROUNDS * EXPERTS:PL], 0.0))
            dve.wait_ge(s("places_prod"), 1)
            order(nc.vector.scalar_tensor_tensor(out=place[:, :, 0:EXPERTS], in0=ps[0][:, 0:256].rearrange("p (t e) -> p t e", t=TT),
                                                 scalar=1.0, in1=wtok, op0=ALU.add, op1=ALU.mult))
            order(nc.vector.tensor_reduce(room[:, 0, :], ps[1][:, 0:EXPERTS], AX.X, ALU.max))
            nc.vector.tensor_scalar(overflow[:], room[:, 0, :], float(P), None, ALU.is_gt).then_inc(s("overflow_known"), 1)

            def onehots(n, par):
                settle(dve, s("slot_prod"), n - 1)
                for t in range(TT):
                    ins = nc.vector.tensor_scalar(onehot[par][:, t, :], count1, place[:, t, bass.ds(n, 1)], None, ALU.is_equal)
                ins.then_inc(s("onehot_ready"), 1)

            def slot_tokens(n, par):
                settle(dve, s("slot_prod"), n + 1)
                settle(dve, s(f"hrow{par}_loaded"), 8 * (n - par))
                nc.vector.tensor_copy(slot_token[:, par:par + 1], ps[0][:, 0:1]).then_inc(s("slot_ready"), 1)

            def rows_half(n, par):
                settle(dve, s("hrow_turned"), 2 * n + 2)
                settle(dve, s("exp_gu"), 2 * n - 2)
                nc.vector.tensor_copy(hgT[par][:, 4:8, :], tiles4(ps[2][:])).then_inc(s("hgt_dve"), 1)

            onehots(0, 0)
            onehots(1, 1)
            for r in range(1, ROUNDS):
                ins = nc.vector.tensor_scalar(place[:, :, r * EXPERTS:(r + 1) * EXPERTS], place[:, :, 0:EXPERTS],
                                              float(-r * P), None, ALU.add)
            order(ins)
            slot_tokens(0, 0)
            onehots(2, 0)
            slot_tokens(1, 1)
            for b in range(2):
                dve.wait_ge(s("sh_gu_prod"), 3 + b)
                dve.wait_ge(s("sh_sil"), b + 1)
                nc.vector.tensor_tensor(xact[:, b, :], ps[6 + b][:], xsil[:, b, :], ALU.mult).then_inc(s("sh_act"), 1)
            flat = lambda x: x.rearrange("p t e -> p (t e)")
            order(nc.vector.tensor_tensor_scan(flat(nth_sel), cmask[:, 0:256], flat(wtok), 0.0, ALU.mult, ALU.add))
            order(nc.vector.tensor_tensor(nth_sel, nth_sel, wtok, ALU.mult))
            order(nc.vector.tensor_tensor(ypos, place[:, :, 0:EXPERTS], etop.unsqueeze(1).to_broadcast([P, TT, EXPERTS]), ALU.add))
            for r in range(1, ROUNDS):
                order(nc.vector.tensor_scalar(over, place[:, :, 0:EXPERTS], r * P + 0.5, float((EXPERTS - 1) * P), ALU.is_gt, ALU.mult))
                order(nc.vector.tensor_tensor(ypos, ypos, over, ALU.add))
            for j in range(6):
                order(nc.vector.tensor_scalar(over, nth_sel, float(j + 1), None, ALU.is_equal))
                for v, dst in ((ypos, yposf), (sco, wj)):
                    order(nc.vector.tensor_tensor(pick, over, v, ALU.mult))
                    order(nc.vector.tensor_reduce(dst[:, :, j:j + 1], pick, AX.X, ALU.add))
            nc.vector.tensor_copy(yidx[:].rearrange("p (t j) -> p t j", t=TT), yposf).then_inc(s("yidx_ready"), 1)
            for b in range(KB):
                dve.wait_ge(s("sh_prod"), b + 1)
                nc.vector.scalar_tensor_tensor(out=xT[:, b, :], in0=ps[4 + b % 4][:], scalar=mod[:, 40 + b:41 + b],
                                               in1=xT[:, b, :], op0=ALU.mult, op1=ALU.add).then_inc(s("sh_added"), 1)
            rows_half(0, 0)

            def expert(n, par):
                onehots(n + 3, 1 - par)
                settle(dve, s("exp_gu"), 2 * n + 2)
                settle(dve, s("exp_sil"), n + 1)
                settle(dve, s("exp_down"), 2 * n - 2)
                nc.vector.tensor_tensor(eact[par], ps[4][:, 0:256], esil[par], ALU.mult).then_inc(s("exp_act"), 1)
                rows_half(n + 1, 1 - par)
                slot_tokens(n + 2, par)
                settle(dve, s("exp_down"), 2 * n + 2)
                settle(dve, s(f"y{par}_stored"), 8 * (n - par))
                nc.vector.tensor_copy(yrow[par][:, 512:1024], ps[6][:]).then_inc(s("y_dve"), 1)

            def experts(i, first):
                for par in range(2):
                    expert(2 * i + par, par)
            all_experts(dve, experts)
            for t in range(TT):
                for j in range(6):
                    k = 6 * t + j
                    if k % 4 == 0:
                        dve.wait_ge(s(f"yg{k // 4 % 2}_loaded"), 64 * (k // 8 + 1))
                    wait(dve, s("y_summed"), k if j else 0)
                    w = wj[:, t, j:j + 1]
                    if j == 0:
                        ins = nc.vector.tensor_scalar(moe[:, t, :], yg[k % 8], w, None, ALU.mult)
                    else:
                        ins = nc.vector.scalar_tensor_tensor(out=moe[:, t, :], in0=yg[k % 8], scalar=w, in1=moe[:, t, :],
                                                             op0=ALU.mult, op1=ALU.add)
                    ins.then_inc(s("y_summed"), 1)
            dve.wait_ge(s("moe_turned"), 1)
            for b in range(KB):
                nc.vector.scalar_tensor_tensor(out=xT[:, b, :], in0=ps[b][:], scalar=mod[:, 40 + b:41 + b],
                                               in1=xT[:, b, :], op0=ALU.mult, op1=ALU.add).then_inc(s("moe_added"), 1)
            normalise("fin2", [(hT, C_FIN2)])
            for t in range(TT):
                dve.wait_ge(s("out_turned"), TT + t + 1)
                nc.vector.tensor_copy(out_tok[:, t, 512:1024], ps[TT + t][:]).then_inc(s("out_ready"), 1)


def kernel(**inputs):
    import numpy as np
    import concourse.bacc as bacc
    from concourse.bass_utils import run_bass_kernel_spmd

    nc = bacc.Bacc("TRN2", target_bir_lowering=False, num_devices=1)
    arrays = {name: np.ascontiguousarray(value) for name, value in inputs.items()}
    a = {name: nc.dram_tensor(name, v.shape, mybir.dt.from_np(v.dtype), kind="ExternalInput").ap()
         for name, v in arrays.items()}
    out = nc.dram_tensor("out", [1, T, D], F32, kind="ExternalOutput").ap()
    program(nc, a, out)
    return run_bass_kernel_spmd(nc, [arrays], core_ids=[0]).results[0]["out"]
```

```python
from contextlib import ExitStack

import concourse.bass as bass
from concourse import mybir

ALU = mybir.AluOpType
ACT = mybir.ActivationFunctionType
AX = mybir.AxisListType
F32 = mybir.dt.float32
U32 = mybir.dt.uint32

P = 128
D = 1024
KB = D // P
T = 512
TT = T // P
FF = 2816
FB = FF // P
PAIRS = 8
HD = 64
EPS = 1e-6
NEG = -1e30
REL = 257
RELW = 384
EXPERTS = 64
ROUNDS = T // P
PL = ROUNDS * EXPERTS + 4
RW = 2072
E_DECAY = 0.6065306597126334

C_A, C_KV, C_B, C_F, C_FIN, C_N1, C_N2, C_FIN2, C_ADAB, C_VN = 0, 8, 16, 24, 40, 48, 56, 64, 72, 120
C_CONV = 128
C5 = 640
C_C, C_QN, C_KN, C_ON, C_W0, C_A0, C_KK, C_KA, C_RK, C_LG, C_LB, C_MU = [
    C5 + n for n in (0, 8, 12, 16, 20, 24, 28, 32, 36, 40, 44, 48)]
PARAM_ROWS = (128, 88, 88, 88, 88, 63)


def wait(eng, sem, count):
    if not isinstance(count, int) or count > 0:
        eng.wait_ge(sem, count)


class Order:

    def __init__(self, eng, sem, consts=None):
        self.eng, self.sem, self.n, self.off, self.consts = eng, sem, 0, 0, consts

    def __call__(self, ins):
        self.n += 1
        ins.then_inc(self.sem, 1)
        self.eng.wait_ge(self.sem, self.n + self.off)
        if not isinstance(self.off, int):
            self.eng.wait_ge(*self.consts)

    def round(self, i, steps, before=0):
        assert self.n in (0, before, steps), self.n
        self.n, self.off = 0, before + i * steps


def looped(eng, n, body):
    body(0, True)
    if n == 2:
        body(1, False)
    elif n > 2:
        with eng.Fori(1, n) as i:
            body(i, False)


def pipelined(eng, n, body):
    body(0, True, False)
    with eng.Fori(1, n - 1) as i:
        body(i, False, False)
    body(n - 1, False, True)


def program(nc, a, out):
    with ExitStack() as ctx:
        def sb(name, *shape, dt=F32):
            return ctx.enter_context(nc.sbuf_tensor(name, list(shape), dt))

        def sem(name):
            return ctx.enter_context(nc.semaphore(name))

        def scratch(name, *shape):
            return nc.dram_tensor(name, list(shape), F32, kind="Internal").ap()

        ps = [ctx.enter_context(nc.psum_tensor(f"bank{i}", [P, 512], F32)) for i in range(8)]

        xT = sb("xT", P, KB, T)
        hT = sb("hT", P, KB, T)
        two = sb("two", P, 2 * KB * T)
        gT = two[:, 0:KB * T].rearrange("p (b t) -> p b t", b=KB)
        yT = sb("yT", P, KB, T)
        sq = sb("sq", P, KB, T)
        big = sb("big", P, FB * T)
        ring = sb("ring", P, 2, FB * P)
        prow = sb("prow", P, 6, P)
        col = sb("col", P, 6 * P)
        ident = sb("ident", P, P)
        mean = sb("mean", P, P)
        rstd = sb("rstd", P, T)
        rms = sb("rms", P, T)
        epsc = sb("epsc", P, 1)
        mod = sb("mod", P, 48)
        csil = sb("csil", P, 8)
        ss4 = sb("ss4", P, 16)
        biasT = two[:, KB * T:].rearrange("p (h k) -> p h k", h=16)
        small = sb("small", P, 64)
        relE, relR = sb("relE", 16, RELW), sb("relR", 16, RELW)
        rel_dram = scratch("rel_dram", 16, P, RELW + 1)

        x_tok = big[:, 0:4096].rearrange("p (t d) -> p t d", t=TT)
        act = big[:].rearrange("p (b t) -> p b t", b=FB)
        vtok = big[:, 0:4096].rearrange("p (t d) -> p t d", t=TT)
        wsraw = big[:, 4096:5120].rearrange("p (g j) -> p g j", g=8)
        wsT = big[:, 5120:6144].rearrange("p (g j) -> p g j", g=8)
        bsb = big[:, 6144:7168].rearrange("p (g j) -> p g j", g=8)
        sptmp = big[:, 7168:7680]
        ffw = sb("ffw", P, 6 * T)
        conv = [[ffw[:, (2 * j + b) * T:(2 * j + b + 1) * T] for b in range(2)] for j in range(2)]
        sil = [ffw[:, (4 + j) * T:(5 + j) * T] for j in range(2)]

        def carve(start, *shapes):
            got, at = [], start
            for s in shapes:
                n = s if isinstance(s, int) else s[0] * s[1]
                t = big[:, at:at + n]
                got.append(t if isinstance(s, int) else t.rearrange("p (a b) -> p a b", a=s[0]))
                at += n
            assert at <= FB * T, at
            return got

        qT, kT, vt, s_sb, p_sb, pT, o_sb, negm, rsum, mx, rinv = carve(
            0, 512, 512, (4, 128), (2, 512), (2, 512), (2, 512), 512, 8, 8, 8, 8)

        kpad, vpad, qraw, akb, avb, sqq, sqk, gsig = carve(
            5696, 520, 520, 512, 512, 512, 512, 512, 512)
        ckb = two[:, 0:1024].rearrange("p (h t) -> p h t", h=2)
        sig24 = two[0:24, 1024:1536]
        fx8 = [two[0:8, 2048 + 512 * n:2560 + 512 * n] for n in range(4)]
        rq, rk, oraw, kmix, vmix = [two[:, 4096 + 512 * n:4608 + 512 * n] for n in range(5)]
        cq = small[:, 0:32].rearrange("p (t h) -> p t h", t=TT)
        gmod = small[:, 32:48]
        qn8 = small[:, 48:52]
        favw = sb("favw", P, KB, 24)
        fbias = sb("fbias", 8, 1)
        ones8 = sb("ones8", 8, T)
        tri = sb("tri", P, P)
        bdiag = sb("bdiag", P, P)
        halfm = sb("halfm", P, P)
        maskAR = sb("maskAR", P, 256)
        mask1 = sb("mask1", P, P)
        maskT = [sb(f"maskT{n}", P, P) for n in range(6)]
        cmask = sb("cmask", P, T)
        onec = sb("onec", P, 1)
        lnxe = sb("lnxe", P, 1)
        sig_dram, cum_dram = scratch("sig_dram", 16, T), scratch("cum_dram", 8, T)

        rp, kp, vp, dd, rr, k0, vv, ld, aa, gg, Lc, Pt, Pinv, Pprev, kkn, sqr, nrm, BT, KT, AR_ = carve(
            0, *[520] * 3, *[512] * 16, 1024)
        AR = AR_.rearrange("p (t w c) -> p t w c", t=TT, w=2)
        tokA, tokB, tokK, tokV, Gm, ApT, Wm, Usb = [two[:, 512 * n:512 * n + 512] for n in range(8)]
        tiles4 = lambda x: x.rearrange("p (t c) -> p t c", t=TT)
        tokA, tokB, tokK, tokV, Gm, Wm, Usb = map(tiles4, (tokA, tokB, tokK, tokV, Gm, Wm, Usb))
        ABT = [two[:, 4096 + 1024 * h:5120 + 1024 * h].rearrange("p (t c) -> p t c", t=TT) for h in range(2)]
        AKT = [two[:, 6144 + 1024 * h:7168 + 1024 * h].rearrange("p (t c) -> p t c", t=TT) for h in range(2)]
        sqf = sq[:].rearrange("p b t -> p (b t)")
        Dm, DT, Xm = [[tiles4(sqf[:, 1024 * n + 512 * h:1024 * n + 512 * h + 512]) for h in range(2)] for n in range(3)]
        Zs = sqf[:, 3072:4096].rearrange("p (c n) -> p c n", c=8)
        Am = [tiles4(ffw[:, 512 * h:512 * h + 512]) for h in range(2)]
        ztmp = ffw[:, 1024:1152]
        y_sb, y_sq = ffw[:, 2048:2560], ffw[:, 2560:3072]
        st8 = ss4
        lwa, lg0 = rms[:], rstd[:]
        lg1 = prow[0:32, 0:4, :].rearrange("p a b -> p (a b)")

        rwt = sb("rwt", P, KB, 64)
        rbias = sb("rbias", P, 64)
        cm8 = sb("cm8", P, 32)
        exw = [big[:, 0:6144], two[:, 0:6144]]
        flat_ring = ring[:].rearrange("p j n -> p (j n)")
        sh_gu, sh_dn = flat_ring[:, 0:4096], big[:, 6144:8192]
        hrow = [flat_ring[:, D * n:D * n + D] for n in range(2)]
        hgT = [flat_ring[:, 2048 + D * n:2048 + D * n + D].rearrange("p (b c) -> p b c", b=KB) for n in range(2)]
        yrow = [big[:, 6144 + D * n:6144 + D * n + D] for n in range(2)]
        onehot = [tiles4(big[:, 8192 + T * n:8192 + T * n + T]) for n in range(2)]
        eact = [big[:, 9216 + 256 * n:9472 + 256 * n] for n in range(2)]
        esil = [big[:, 9728 + 256 * n:9984 + 256 * n] for n in range(2)]
        place = ffw[:, 0:TT * PL].rearrange("p (t e) -> p t e", t=TT)
        count1 = ffw[:, 1152:1280]
        tokid = ffw[:, 1280:1284]
        etop = ffw[:, 1344:1408]
        wj, yposf = [ffw[:, 1408 + 32 * n:1432 + 32 * n].rearrange("p (t j) -> p t j", t=TT) for n in range(2)]
        nth_sel, ypos, over, pick = [tiles4(ffw[:, 1536 + 256 * n:1792 + 256 * n]) for n in range(4)]
        earlier, ones = maskT[0], maskT[1]
        slot_token = sb("slot_token", P, 2, dt=U32)
        yidx = sb("yidx", P, 24, dt=U32)
        overflow = sb("overflow", P, 1, dt=U32)
        h_dram, y_dram = scratch("h_dram", T, D), scratch("y_dram", ROUNDS * EXPERTS * P, D)
        htok = yT[:].rearrange("p b t -> p (b t)").rearrange("p (t d) -> p t d", t=TT)
        g2_row, fin_row = big[:, 10240:11264], flat_ring[:, 4608:5632]
        g2T = flat_ring[0:8, 4096:4224]
        g2_dram = scratch("g2_dram", 8, P)
        res = hT[:].rearrange("p b t -> p (b t)").rearrange("p (t d) -> p t d", t=TT)
        yg = [sqf[:, D * n:D * n + D] for n in range(4)] + [htok[:, n, :] for n in range(4)]
        rt = two[:, 6144:8192]
        r4 = lambda n, w: rt[:, n:n + 4 * w].rearrange("p (t e) -> p t e", t=TT)
        sco, sel, eqm, pos, wtok = [r4(256 * n, 64) for n in range(5)]
        srt = rt[:, 1280:1536].rearrange("p (u e) -> p u e", e=8)
        gsc, gsrt, gmask, geq, gpos, esrt = [r4(1536 + 32 * n, 8) for n in range(6)]
        room, wsum = r4(1728, 1), r4(1732, 1)
        xact = sqf[:, 1024:2048].rearrange("p (b t) -> p b t", b=2)
        xsil = sqf[:, 3072:4096].rearrange("p (b t) -> p b t", b=2)

        S = {}
        bc4 = lambda m: m.unsqueeze(1).to_broadcast([P, TT, P])

        def s(name):
            if name not in S:
                S[name] = sem(name)
            return S[name]

        for n in ("ring0_loaded", "ring1_loaded", "ff_prod", "ada0_loaded", "ada1_loaded", "expgu0_loaded",
                  "expgu1_loaded", "expdn0_loaded", "expdn1_loaded", "hrow0_loaded", "hrow1_loaded",
                  "y0_stored", "y1_stored", "yg0_loaded", "yg1_loaded", "exp_sil", "exp_act", "y_ready",
                  "overflow_known", "lin_prod", "mod_prod", "x_loaded", "params_loaded", "pool_order",
                  "sh_loaded", "exp_gu", "exp_down", "out_ready", "consts", "side_loaded", "ws_loaded",
                  "rel_loaded", "pool_consts", "rel_ext", "rel_stored", "norm_sq_ready", "norm_sum",
                  "ada_summed", "col_ready", "fav_sig", "sig_stored", "cum_ready", "fx_mixed", "att_sc_added",
                  "fx_rows", "rw_smt", "rw_x", "rw_am", "g2_moved", "g2_stored", "rw_y_ready", "moe_consts",
                  "h_stored", "slot_ready", "hrow_turned", "yidx_ready", "sh_added", "y_summed",
                  "norm_ss_ready", "mod_ready", "lin_added", "ff_tap0", "norm_h_ready", "ff_act", "x_turned",
                  "x_ready", "params_turned", "ws_step", "gv_taken", "norm_rms_ready", "gv_prod", "gu_taken",
                  "gu_prod", "vn_ready", "sp_prod", "gated", "v_taken", "qkv_prod", "att_o_norm",
                  "att_ot_prod", "qk_taken", "att_sc_prod", "att_p_ready", "att_pt_taken", "att_pt_prod",
                  "att_av_prod", "o_ready", "fav_prod", "cq_step", "fx_prod", "fx_sq", "fx_ms", "fx_vturned",
                  "fx_taken", "fx_qk", "fx_rms", "lora_prod", "fx_o_taken", "lora_ready", "rw_prod",
                  "fx_y_ready", "rw_sq", "rw_ms", "rw_ops", "rw_taken", "rw_turned", "rw_nrm", "rw_bonus",
                  "rw_sm", "rw_tok", "rw_d0", "rw_dt", "rw_xt", "rw_dd", "rw_g", "rw_gt", "rw_zt", "rw_u",
                  "rw_ut", "rw_z", "rw_out_step", "rt_prod", "htok_taken", "htok_turned", "sh_gu_prod",
                  "rt_masked", "places_prod", "onehot_ready", "slot_prod", "hgt_ready", "sh_act", "sh_prod",
                  "res_taken", "res_turned", "act_order", "h_scaled", "ff_tap2", "ff_silu", "vrms_ready",
                  "att_negm_ready", "f_abs", "f_log", "pads", "lora_taken", "lora_mixed", "rw_kk", "rw_L",
                  "rw_P", "rt_sig", "sh_sil", "fin_rms", "dve_order", "ff_tap1", "att_sc_max", "att_r_inv",
                  "fx_order", "rw_order"):
            s(n)
        NORMS = ["a", "f0", "att", "f1", "fin", "n1", "n2"]
        nth = lambda n: NORMS.index(n) + 1

        def h_count(n, b, out=0):
            k = NORMS.index(n)
            return KB * (k + out + (k > NORMS.index("att"))) + b + 1


        plan, steps, loads, before = {}, {}, [0, 0], None
        STAGES = [("gv", 4, 1, 1, "gv_prod", 4), ("gu", 4, 1, 1, "gu_prod", 2),
                  ("go", 4, 1, 1, "lin_prod", 2), ("f0in", 22, 2, 2, "ff_prod", 2), ("f0dn", 8, 1, 1, "lin_prod", 1),
                  ("att", 16, 2, 1, "qkv_prod", (2, 3)), ("wo", 4, 1, 1, "lin_prod", 2),
                  ("f1in", 22, 2, 2, "ff_prod", 2), ("f1dn", 8, 1, 1, "lin_prod", 1),
                  ("fx", 8, 2, 2, "fx_prod", 2), ("lora", 2, 1, 1, "lora_prod", (1, 3)),
                  ("rw", 8, 2, 5, "rw_prod", (2, 6)), ("w_out", 4, 1, 1, "lin_prod", 2)]
        for name, units, d0, d1, used, per in STAGES:
            plan[name] = (units, list(loads), (d0, d1), used, per, before, steps.get(used, 0))
            steps[used] = steps.get(used, 0) + (units // 2 * per[1] if isinstance(per, tuple) else units * per)
            loads[0] += 16 * d0 * units // 2
            loads[1] += 16 * d1 * units // 2
            before = name

        def steps_of(stage):
            per = plan[stage][4]
            return per if isinstance(per, tuple) else (per, 2 * per)

        BANKS = {"go": (0, 1, 2, 3), "f0dn": (6, 7, 0, 1), "wo": (0, 1, 2, 3), "f1dn": (6, 7, 0, 1), "w_out": (0, 6, 7, 1)}

        def used_count(stage, m):
            odd, both = steps_of(stage)
            return plan[stage][6] + both * (m // 2) + odd * (m % 2)

        def ring_ready(eng, stage, i, j):
            _, base, d, *_ = plan[stage]
            wait(eng, (S["ring0_loaded"], S["ring1_loaded"])[j], base[j] + 16 * d[j] * (i + 1))

        adaw = [two[:, 2048 * j:2048 * j + 2048].rearrange("p (k n) -> p k n", k=KB) for j in range(2)]
        ADA = FB
        ADA_UNITS = 6 * D // 256

        def slot(j, k, n):
            return ring[:, j, 0:k * n].rearrange("p (k n) -> p k n", k=k)

        def wcols(w, c0, n):
            return w.rearrange("(k p) n -> p k n", p=P)[:, :, bass.ds(c0, n)]

        w_in, w_kv, w_q = a["a_w_in"][0], a["w_kv"], a["b_w_q"][0]

        def unit_loads(stage, i, j):
            u = 2 * i + j
            if stage == "gv":
                return [(slot(j, 8, 256), wcols(w_in, D + u * 256, 256))]
            if stage == "gu":
                return [(slot(j, 8, 256), wcols(w_in, u * 256, 256))]
            if stage in ("go", "wo", "w_out"):
                w = {"go": a["a_w_out"][0], "wo": a["b_w_o"][0], "w_out": a["w_out_2"][0]}[stage]
                return [(slot(j, 8, 256), wcols(w, u * 256, 256))]
            if stage in ("f0in", "f1in"):
                w = a["f_w_in"][int(stage[1])]
                return [(slot(j, 8, 256)[:, :, b * P:(b + 1) * P], wcols(w, b * FF + u * P, P)) for b in range(2)]
            if stage in ("f0dn", "f1dn"):
                return [(slot(j, FB, P), wcols(a["f_w_down"][int(stage[1])], u * P, P))]
            if stage == "att":
                if j == 0:
                    return [(slot(0, 8, 256)[:, :, 0:P], wcols(w_q, i * P, P)),
                            (slot(0, 8, 256)[:, :, P:256], wcols(w_kv, i * P, P))]
                return [(slot(1, 8, P), wcols(w_kv, D + i * P, P))]
            w2 = a["w_in_2"][0]
            if stage == "fx":
                return [(slot(j, 8, 256)[:, :, b * P:(b + 1) * P], wcols(w2, (2 * j + b) * 512 + i * P, P))
                        for b in range(2)]
            if stage == "lora":
                return [(slot(j, 8, (P, 160)[j]), wcols(w2, (RW + 1536, RW + 1664)[j], (P, 160)[j]))]
            if stage == "rw":
                if j == 0:
                    return [(slot(0, 8, 256)[:, :, b * P:(b + 1) * P], wcols(w2, RW + b * 512 + i * P, P))
                            for b in range(2)]
                own = bass.ds(i * P, P)
                return [(slot(1, 8, P), wcols(w2, RW + 1024 + i * P, P)),
                        (ring[0:64, 1, 1024:1152], a["rw_decay_up_2"][0][:, own]),
                        (ring[64:128, 1, 1024:1152], a["rw_iclr_up_2"][0][:, own]),
                        (ring[:, 1, 1152:1280], a["rw_gate_up_2"][0][0:P, own]),
                        (ring[0:32, 1, 1280:1408], a["rw_gate_up_2"][0][P:160, own])]
            raise AssertionError(stage)

        block = ctx.enter_context(nc.Block())
        NCONST = 5
        NPARAM = 10 + 6 + 13

        def settle(eng, sem, count):
            wait(eng, sem, count)
            if not isinstance(count, int):
                eng.wait_ge(S["consts"], NCONST)

        def all_experts(eng, body, after=None):
            looped(eng, EXPERTS // 2, body)
            eng.wait_ge(s("overflow_known"), 1)
            with eng.If(eng.value_load(overflow[0:1, 0:1], min_val=0, max_val=1) > 0):
                with eng.Fori(EXPERTS // 2, ROUNDS * EXPERTS // 2) as i:
                    body(i, False)
                if after:
                    after(ROUNDS * EXPERTS)
            if after:
                with eng.Else():
                    after(EXPERTS)

        @block.sync
        def _(sp):
            def stage_loads(stage):
                units, _, _, used, per, before, base = plan[stage]

                def load(i, first):
                    for j in range(2):
                        if first and before is not None:
                            sp.wait_ge(S[plan[before][3]], used_count(before, plan[before][0] - 1 + j))
                        elif not first:
                            even, both = steps_of(stage)
                            sp.wait_ge(S[used], both * i + base - (both - even if j == 0 else 0))
                        for dst, src in unit_loads(stage, i, j):
                            sp.dma_start(dst, src).then_inc(S[f"ring{j}_loaded"], 16)
                        if stage == "f0in":
                            ada_load(2 * i + j, j)
                    if stage == "f0dn" and first:
                        for u in range(ADA, ADA_UNITS):
                            ada_load(u, u % 2)
                looped(sp, units // 2, load)

            def ada_load(u, j):
                if isinstance(u, int) and u < 2:
                    sp.wait_ge(s("lin_prod"), KB)
                else:
                    sp.wait_ge(s("mod_prod"), u - 1)
                sp.dma_start(adaw[j], wcols(a["ada_w_2"][0], u * 256, 256)).then_inc(s(f"ada{j}_loaded"), 16)

            sp.dma_start(x_tok, a["x"][0].rearrange("(t p) d -> p t d", p=P)).then_inc(s("x_loaded"), 16)
            rows = lambda ap: ap.rearrange("(r c) -> r c", c=P)
            nload = 0

            def row_load(tile, r0, flat, n=None):
                nonlocal nload
                src = rows(flat)
                sp.dma_start(prow[r0:r0 + src.shape[0], tile, 0:P], src).then_inc(s("params_loaded"), 16)
                nload += 1

            sp.wait_ge(s("pool_order"), 2)
            for r, ap in ((C_A, a["a_norm_g"][0]), (C_KV, a["kv_norm_g"]), (C_B, a["b_norm_g"][0]),
                          (C_F, a["f_norm_g"].rearrange("l d -> (l d)")), (C_FIN, a["final_norm_g"]),
                          (C_N1, a["norm1_g_2"][0]), (C_N2, a["norm2_g_2"][0]), (C_FIN2, a["final_g_2"]),
                          (C_ADAB, a["ada_b_2"][0]), (C_VN, a["a_v_norm_g"][0])):
                row_load(0, r, ap)
            for l in range(2):
                row_load(1 + 2 * l, 0, a["f_conv_w"][l, 0:2].rearrange("k c -> (k c)"))
                row_load(2 + 2 * l, 0, a["f_conv_w"][l, 2])
                row_load(2 + 2 * l, 44, a["f_conv_b"][l])
            mu = a["rw_mu_2"][0]
            for c, ap in ((C_C, a["c_2"][0]), (C_QN, a["fox_qn_g_2"][0].rearrange("h d -> (h d)")),
                          (C_KN, a["fox_kn_g_2"][0].rearrange("h d -> (h d)")),
                          (C_ON, a["fox_on_g_2"][0].rearrange("h d -> (h d)")), (C_W0, a["rw_w0_2"][0]),
                          (C_A0, a["rw_a0_2"][0]), (C_KK, a["rw_k_k_2"][0]), (C_KA, a["rw_k_a_2"][0]),
                          (C_RK, a["rw_r_k_2"][0].rearrange("h d -> (h d)")), (C_LG, a["rw_lnx_g_2"][0]),
                          (C_LB, a["rw_lnx_b_2"][0]), (C_MU, mu[0:14 * P])):
                row_load(5, c - C5, ap)
            sp.dma_start(prow[62:63, 5, 0:32], mu[14 * P:14 * P + 32].rearrange("(r c) -> r c", r=1))\
                .then_inc(s("params_loaded"), 16)
            nload += 1
            assert nload == NPARAM, nload
            for name, *_ in STAGES:
                stage_loads(name)

            sp.wait_ge(s("lin_prod"), 5 * KB)
            for k, n in ((0, "sh_w_gate_2"), (2048, "sh_w_up_2")):
                sp.dma_start(sh_gu[:, k:k + 2048].rearrange("p (k n) -> p k n", k=KB),
                             a[n][0].rearrange("(k p) n -> p k n", p=P)).then_inc(s("sh_loaded"), 16)
            sp.dma_start(sh_dn.rearrange("p (k n) -> p k n", k=2),
                         a["sh_w_down_2"][0].rearrange("(k p) n -> p k n", p=P)).then_inc(s("sh_loaded"), 16)

            def expert_loads(i, first, r=0):
                for par in range(2):
                    w = exw[par]
                    e = bass.ds(2 * i + par - EXPERTS * r, 1)
                    one = lambda n: a[n][0][e].rearrange("o r c -> (o r) c")
                    wait(sp, s("exp_gu"), 4 * i + 2 * par - 2)
                    for k, n in ((0, "exp_w_gate_2"), (2048, "exp_w_up_2")):
                        sp.dma_start(w[:, k:k + 2048].rearrange("p (k n) -> p k n", k=KB),
                                     one(n).rearrange("(k p) n -> p k n", p=P)).then_inc(s(f"expgu{par}_loaded"), 16)
                    wait(sp, s("exp_down"), 4 * i + 2 * par - 2)
                    sp.dma_start(w[:, 4096:6144].rearrange("p (k n) -> p k n", k=2),
                                 one("exp_w_down_2").rearrange("(k p) n -> p k n", p=P))\
                        .then_inc(s(f"expdn{par}_loaded"), 16)

            looped(sp, EXPERTS // 2, expert_loads)
            sp.wait_ge(s("overflow_known"), 1)
            with sp.If(sp.value_load(overflow[0:1, 0:1], min_val=0, max_val=1) > 0):
                for r in range(1, ROUNDS):
                    with sp.Fori(r * EXPERTS // 2, (r + 1) * EXPERTS // 2) as i:
                        expert_loads(i, False, r)
            for t in range(TT):
                sp.wait_ge(s("out_ready"), t + 1)
                sp.dma_start(out[0, t * P:(t + 1) * P, :], res[:, t, :]).then_inc(s("x_loaded"), 16)
            sp.wait_ge(s("x_loaded"), 16 + 16 * TT)

        @block.gpsimd
        def _(pool):
            pool.memset(prow[:, 5, :], 0.0).then_inc(s("pool_order"), 1)
            pool.memset(ident[:], 0.0).then_inc(s("pool_order"), 1)
            pool.memset(mean[:], 1.0 / D).then_inc(s("consts"), 1)
            pool.memset(epsc[:], EPS).then_inc(s("consts"), 1)
            pool.wait_ge(s("pool_order"), 2)
            pool.affine_select(out=ident[:], in_=ident[:], compare_op=ALU.not_equal, fill=1.0, base=0,
                               pattern=[[-1, P]], channel_multiplier=1).then_inc(s("consts"), 1)
            pool.dma_start(favw[:], wcols(a["w_in_2"][0], 2048, 24)).then_inc(s("side_loaded"), 16)
            pool.dma_start(fbias[:], a["fox_forget_b_2"][0].rearrange("(h o) -> h o", o=1)).then_inc(s("side_loaded"), 16)
            pool.dma_start(rwt[:], a["router_w_2"][0].rearrange("(k p) n -> p k n", p=P)).then_inc(s("side_loaded"), 16)
            pool.dma_start(rbias[:], a["router_bias_2"][0].partition_broadcast(P)).then_inc(s("side_loaded"), 16)
            pool.dma_start(wsraw, a["a_w_s"][0].rearrange("g i j -> i g j")).then_inc(s("ws_loaded"), 16)
            pool.dma_start(bsb, a["a_b_s"][0].rearrange("g i -> (g i)").partition_broadcast(P)
                           .rearrange("p (g i) -> p g i", g=8)).then_inc(s("ws_loaded"), 16)
            pool.dma_start(relE[:, 0:REL], a["b_rel_bias"][0]).then_inc(s("rel_loaded"), 16)
            porder = Order(pool, s("pool_consts"))
            porder(pool.memset(lnxe[:], 64e-5))
            porder(pool.memset(ones8[:], 1.0))
            porder(pool.memset(cmask[:], 1.0))
            porder(pool.memset(cmask[:].rearrange("p (c n) -> p c n", n=64)[:, :, 0:1], 0.0))
            porder(pool.memset(cm8[:], 1.0))
            porder(pool.memset(cm8[:].rearrange("p (c n) -> p c n", n=8)[:, :, 0:1], 0.0))
            porder(pool.memset(tri[:], 0.0))
            porder(pool.affine_select(out=tri[:], in_=tri[:], compare_op=ALU.is_ge, fill=NEG, base=0,
                               pattern=[[-1, P]], channel_multiplier=1))
            for tile, v in ((bdiag, 1.0), (halfm, 1.0 / HD)):
                porder(pool.memset(tile[:], v))
                porder(pool.memset(tile[0:64, 64:128], 0.0))
                porder(pool.memset(tile[64:128, 0:64], 0.0))
            porder(pool.memset(maskAR[:], 1.0))
            for w, op in ((0, ALU.is_gt), (1, ALU.is_ge)):
                half = maskAR[:, w * P:(w + 1) * P]
                porder(pool.affine_select(out=half, in_=half, compare_op=op, fill=0.0, base=0,
                                          pattern=[[1, P]], channel_multiplier=-1))
                porder(pool.memset(maskAR[0:64, w * P + 64:(w + 1) * P], 0.0))
            porder(pool.memset(mask1[:], 0.0))
            view = mask1[:].rearrange("p (b w) -> p b w", w=2)
            porder(pool.memset(view[:, :, 0:1], 1.0))
            porder(pool.affine_select(out=view, in_=view, compare_op=ALU.is_equal, fill=0.0, base=-1,
                               pattern=[[-2, 64], [0, 2]], channel_multiplier=1))
            for n in range(6):
                w = 1 << n
                view = maskT[n][:].rearrange("p (b w c) -> p b w c", w=2, c=w)
                porder(pool.memset(maskT[n][:], 0.0))
                porder(pool.memset(view[:, :, 1:2, :], 1.0))
                porder(pool.affine_select(out=view, in_=view, compare_op=ALU.is_ge, fill=0.0, base=0,
                                          pattern=[[-2 * w, 64 // w], [0, 2], [0, w]], channel_multiplier=1))
                porder(pool.affine_select(out=view, in_=view, compare_op=ALU.is_ge, fill=0.0, base=w - 1,
                                   pattern=[[2 * w, 64 // w], [0, 2], [0, w]], channel_multiplier=-1))
            pool.memset(onec[:], 1.0).then_inc(s("consts"), 1)
            pool.wait_ge(s("rel_ext"), 2)
            pool.dma_start(rel_dram[:, :, 0:RELW], relR[:].unsqueeze(1).to_broadcast([16, P, RELW]))\
                .then_inc(s("rel_stored"), 16)
            pool.wait_ge(s("rel_stored"), 16)
            pool.dma_start(biasT, bass.AP(rel_dram.tensor, 127, [[RELW, P], [P * (RELW + 1), 16], [1, 256]]))\
                .then_inc(s("rel_stored"), 16)
            pool.wait_ge(s("rel_stored"), 32)
            pool.memset(biasT[0:64, :, 192:256], NEG).then_inc(s("consts"), 1)

            def square_sums(n):
                for b in range(1, KB - 1):
                    pool.wait_ge(s("norm_sq_ready"), KB * (nth(n) - 1) + b + 1)
                    if b > 1:
                        pool.wait_ge(s("norm_sum"), 6 * (nth(n) - 2) + b - 1)
                    nc.gpsimd.tensor_tensor(sq[:, 0, :], sq[:, 0, :], sq[:, b, :], ALU.add).then_inc(s("norm_sum"), 1)

            def ada(i, first):
                for j in range(2):
                    ada_unit(2 * i + j, j)

            def ada_unit(u, j):
                def step(k, ins):
                    ins.then_inc(s("ada_summed"), 1)
                    if k < 4:
                        settle(pool, s("ada_summed"), 4 * u + k)

                w = adaw[j]
                settle(pool, s(f"ada{j}_loaded"), 16 * (u // 2) + 16 if isinstance(u, int) else 8 * (u - j) + 16)
                step(1, nc.gpsimd.tensor_tensor(w, w, csil[:].unsqueeze(2).to_broadcast([P, KB, 256]), ALU.mult))
                for k, n in ((2, 4), (3, 2), (4, 1)):
                    step(k, nc.gpsimd.tensor_tensor(w[:, 0:n, :], w[:, 0:n, :], w[:, n:2 * n, :], ALU.add))

            square_sums("f0")
            pool.wait_ge(s("col_ready"), len(PARAM_ROWS) + 1)
            looped(pool, ADA // 2, ada)
            for u in range(ADA, ADA_UNITS):
                ada_unit(u, u % 2)
            for n in ("att", "f1", "fin", "n1"):
                square_sums(n)
            pool.wait_ge(s("fav_sig"), 1)
            pool.dma_start(sig_dram, sig24[8:24, :]).then_inc(s("sig_stored"), 16)
            pool.wait_ge(s("cum_ready"), 1)
            pool.dma_start(cum_dram, fx8[3]).then_inc(s("sig_stored"), 16)
            pool.wait_ge(s("sig_stored"), 32)

            def fox_rows(i, first):
                if not first:
                    settle(pool, s("fx_mixed"), 2 * i)
                    settle(pool, s("att_sc_added"), 64 + 8 * i)
                for h in range(2):
                    for n, dst in enumerate((akb, avb)):
                        pool.dma_start(dst[64 * h:64 * h + 64, :],
                                       sig_dram[bass.ds(8 * n + 2 * i + h, 1), :].rearrange("o t -> (o t)")
                                       .partition_broadcast(64)).then_inc(s("fx_rows"), 16)
                pool.dma_start(ckb, cum_dram[bass.ds(2 * i, 2), :].partition_broadcast(P)).then_inc(s("fx_rows"), 16)
            looped(pool, 4, fox_rows)

            def level_masks(i, first):
                for n in range(1, 6):
                    for h in range(2):
                        k = 2 * (n - 1) + h
                        if n == 1:
                            settle(pool, s("rw_smt"), 10 * i + 5 * h + 5)
                        else:
                            settle(pool, s("rw_x"), 10 * i + k - 1)
                        nc.gpsimd.tensor_tensor(Am[h], ABT[h][:, :, 0:P], bc4(maskT[n][:]), ALU.mult)\
                            .then_inc(s("rw_am"), 1)
            looped(pool, 4, level_masks)

            square_sums("n2")
            pool.wait_ge(s("lin_prod"), 5 * KB)
            pool.dma_start(fin_row, a["final_g_2"].partition_broadcast(P)).then_inc(s("g2_moved"), 16)
            pool.wait_ge(s("g2_stored"), 16)
            pool.dma_start(g2_row, g2_dram.rearrange("b p -> (b p)").partition_broadcast(P)).then_inc(s("g2_moved"), 16)
            pool.wait_ge(s("rw_y_ready"), 4)
            pool.memset(ones[:], 1.0).then_inc(s("moe_consts"), 1)
            pool.wait_ge(s("moe_consts"), 1)
            pool.affine_select(out=earlier[:], in_=ones[:], compare_op=ALU.is_gt, fill=0.0, base=0,
                               pattern=[[1, P]], channel_multiplier=-1).then_inc(s("moe_consts"), 1)
            for dst, step, n, base, ch in ((count1, 1, P, 1, 0), (tokid, -P, TT, T, -1), (etop, P, EXPERTS, -1, 0)):
                pool.iota(dst, [[step, n]], base=base, channel_multiplier=ch,
                          allow_small_or_imprecise_dtypes=True).then_inc(s("moe_consts"), 1)
            pool.wait_ge(s("h_stored"), 32)

            def gather(n, par):
                ready, turned = n + 1, 2 * n - 2
                if not isinstance(n, int):
                    ready, turned = pool.to_reg(ready), pool.to_reg(turned)
                    pool.wait_ge(s("consts"), NCONST)
                wait(pool, s("slot_ready"), ready)
                wait(pool, s("hrow_turned"), turned)
                pool.indirect_dma_start(hrow[par], None, h_dram, bass.IndirectOffsetOnAxis(slot_token[:, par:par + 1], 0),
                                        bounds_check=T - 1, oob_is_err=False)\
                    .then_inc(s(f"hrow{par}_loaded"), 16)

            gather(0, 0)
            gather(1, 1)

            def experts(i, first):
                for par in range(2):
                    gather(2 * i + par + 2, par)

            def token_results(n):
                for par in range(2):
                    pool.wait_ge(s(f"y{par}_stored"), 8 * n)
                pool.wait_ge(s("yidx_ready"), 1)
                pool.wait_ge(s("sh_added"), KB)
                for k in range(6 * TT):
                    if k % 4 == 0 and k >= 8:
                        pool.wait_ge(s("y_summed"), k - 4)
                    pool.indirect_dma_start(yg[k % 8], None, y_dram[0:n * P, :], bass.IndirectOffsetOnAxis(yidx[:, k:k + 1], 0))\
                        .then_inc(s(f"yg{k // 4 % 2}_loaded"), 16)

            all_experts(pool, experts, token_results)

        @block.tensor
        def _(pe):
            def mean_squares(n):
                if n == "a":
                    blocks = range(KB)
                else:
                    blocks = (0, KB - 1)
                    pe.wait_ge(s("norm_sum"), 6 * (nth(n) - 1))
                for b in blocks:
                    pe.wait_ge(s("norm_sq_ready"), KB * (nth(n) - 1) + b + 1)
                    mm = pe.matmul(ps[7][:], mean[:], sq[:, b, :], start=(b == 0), stop=(b == KB - 1))
                mm.then_inc(s("norm_ss_ready"), 1)

            def ada_unit(u, j):
                pe.wait_ge(s("ada_summed"), 4 * u + 4)
                wait(pe, s("mod_ready"), u - 1)
                for b in range(2):
                    mm = pe.matmul(ps[4 + j][:, b:b + 1], adaw[j][:, 0, b * P:(b + 1) * P], onec[:],
                                   start=True, stop=True)
                mm.then_inc(s("mod_prod"), 1)

            def linear_step(stage, rhs, kb, n, k):
                per = plan[stage][4]
                w = slot(n // per % 2, kb, per * P)
                if k == 0 and n % per == 0:
                    ring_ready(pe, stage, n // per // 2, n // per % 2)
                mm = pe.matmul(ps[BANKS[stage][n % 4]][:], w[:, k, n % per * P:(n % per + 1) * P], rhs[:, k, :],
                               start=(k == 0), stop=(k == kb - 1))
                if k == kb - 1:
                    mm.then_inc(S[plan[stage][3]], 1)

            def linear(stage, rhs, kb, ready, done=(), between={}):
                base = plan[stage][6]
                for n in range(KB):
                    if n >= 4:
                        pe.wait_ge(s("lin_added"), base + n - 3)
                    for k in range(done[n] if n < len(done) else 0, kb):
                        if n == 0:
                            ready(k)
                        linear_step(stage, rhs, kb, n, k)
                    if n in between:
                        ada_unit(between[n], between[n] % 2)

            def feed_forward(l):
                stage = f"f{l}in"

                def body(i, first):
                    for j in range(2):
                        ring_ready(pe, stage, i, j)
                        w = slot(j, 8, 256)
                        for b in range(2):
                            if not first:
                                pe.wait_ge(s("ff_tap0"), 44 * l + 4 * i + 2 * j + b - 3)
                            for k in range(KB):
                                if first and j == 0 and b == 0:
                                    pe.wait_ge(s("norm_h_ready"), h_count(f"f{l}", k))
                                mm = pe.matmul(ps[2 * j + b][:], w[:, k, b * P:(b + 1) * P], hT[:, k, :],
                                               start=(k == 0), stop=(k == KB - 1))
                            mm.then_inc(s("ff_prod"), 1)
                        if l == 0:
                            ada_unit(2 * i + j, j)
                looped(pe, FB // 2, body)
                linear(f"f{l}dn", act, FB, lambda k: pe.wait_ge(s("ff_act"), l * FB + k + 1),
                       between={2: ADA, 4: ADA + 1} if l == 0 else {})

            pe.wait_ge(s("consts"), 3)
            pe.wait_ge(s("x_loaded"), 16)
            for b in range(KB):
                for t in range(TT):
                    tr = pe.transpose(ps[b][:, t * P:(t + 1) * P], x_tok[:, t, b * P:(b + 1) * P], ident[:])
                tr.then_inc(s("x_turned"), 1)
            pe.wait_ge(s("params_loaded"), 16 * NPARAM)
            for t, rows in enumerate(PARAM_ROWS):
                wait(pe, s("x_ready"), t + 1)
                pe.transpose(ps[t][:, 0:rows], prow[0:rows, t, :], ident[0:rows, 0:rows])\
                    .then_inc(s("params_turned"), 1)
            pe.wait_ge(s("x_ready"), KB)
            pe.wait_ge(s("ws_step"), 1)
            for g in range(8):
                tr = pe.transpose(ps[6 + g // 4][:, (g % 4) * P:(g % 4 + 1) * P], wsraw[:, g, :], ident[:])
            tr.then_inc(s("ws_step"), 1)


            pe.wait_ge(s("ws_step"), 3)
            mean_squares("a")
            for u in range(4):
                ring_ready(pe, "gv", u // 2, u % 2)
                for t in range(TT):
                    wait(pe, s("gv_taken"), 4 * (u - 2) + t + 1)
                    if u == 1 and t == 3:
                        pe.wait_ge(s("norm_rms_ready"), nth("a"))
                    for k in range(KB):
                        if u == 0 and t == 0:
                            pe.wait_ge(s("norm_h_ready"), h_count("a", k))
                        mm = pe.matmul(ps[4 * (u % 2) + t][:, 0:256], hT[:, k, t * P:(t + 1) * P],
                                       slot(u % 2, 8, 256)[:, k, :], start=(k == 0), stop=(k == KB - 1))
                    mm.then_inc(s("gv_prod"), 1)
            pe.wait_ge(s("gv_taken"), 16)
            for u in range(4):
                ring_ready(pe, "gu", u // 2, u % 2)
                for b in range(2):
                    n = 2 * u + b
                    wait(pe, s("gu_taken"), n - 3)
                    for k in range(KB):
                        mm = pe.matmul(ps[n % 4][:], slot(u % 2, 8, 256)[:, k, b * P:(b + 1) * P], hT[:, k, :],
                                       start=(k == 0), stop=(k == KB - 1))
                    mm.then_inc(s("gu_prod"), 1)
            pe.wait_ge(s("vn_ready"), 4)
            for g in range(8):
                if g < 4:
                    bank = 4 + g
                else:
                    bank = g - 4
                    pe.wait_ge(s("gu_taken"), 8)
                for n in range(TT):
                    mm = pe.matmul(ps[bank][:, n * P:(n + 1) * P], vtok[:, n, g * P:(g + 1) * P], wsT[:, g, :],
                                   start=True, stop=True)
                mm.then_inc(s("sp_prod"), 1)
            pe.wait_ge(s("gated"), 8)
            linear("go", gT, KB, lambda k: None)
            mean_squares("f0")
            feed_forward(0)

            mean_squares("att")

            def projection(i, m, ks, first=False):
                if ks[0] == 0 and m != 1:
                    ring_ready(pe, "att", i, m // 2)
                if m < 2:
                    src = (hT, gT)[m]
                    for k in ks:
                        if first:
                            pe.wait_ge(s("norm_h_ready"), h_count("att", k, m))
                        mm = pe.matmul(ps[m][:], slot(0, 8, 256)[:, k, m * P:(m + 1) * P], src[:, k, :],
                                       start=(k == 0), stop=(k == KB - 1))
                else:
                    if ks[0] == 0 and not first:
                        pe.wait_ge(s("v_taken"), i)
                    for t in range(ks[0] // 2, (ks[-1] + 1) // 2):
                        for k in range(KB):
                            mm = pe.matmul(ps[2][:, t * P:(t + 1) * P], gT[:, k, t * P:(t + 1) * P],
                                           slot(1, 8, P)[:, k, :], start=(k == 0), stop=(k == KB - 1))
                if ks[-1] == KB - 1:
                    mm.then_inc(s("qkv_prod"), 1)

            def turn_output(i):
                pe.wait_ge(s("att_o_norm"), i + 1)
                for t in range(TT):
                    tr = pe.transpose(ps[7][:, t * P:(t + 1) * P], o_sb[:, t * P:(t + 1) * P], ident[:])
                tr.then_inc(s("att_ot_prod"), 1)

            HALVES = (range(0, 4), range(4, 8))

            def pair(i, first, last):
                pe.wait_ge(s("qk_taken"), 2 * i + 2)
                attention_core(i, first, (lambda u: u < 6 and projection(i + 1, u // 2, HALVES[u % 2])) if not last else None,
                               lambda: turn_output(i - 1), ("o_ready", i))

            def attention_core(i, first, between, before_turns, values_free):

                def scores(u):
                    h, qt = u // TT, u % TT
                    if not (first and u < 2):
                        pe.wait_ge(s("att_sc_added"), 8 * i + u - 1)
                    pe.matmul(ps[3 + u % 2][:, 0:(qt + 1) * P], qT[64 * h:64 * h + 64, qt * P:(qt + 1) * P],
                              kT[64 * h:64 * h + 64, 0:(qt + 1) * P], start=True, stop=True).then_inc(s("att_sc_prod"), 1)

                def turn(u):
                    pe.wait_ge(s("att_p_ready"), 8 * i + u + 1)
                    if not (first and u < 2):
                        pe.wait_ge(s("att_pt_taken"), 8 * i + u - 1)
                    for b in range(u % TT + 1):
                        tr = pe.transpose(ps[5 + u % 2][:, b * P:(b + 1) * P],
                                          p_sb[:, u % 2, b * P:(b + 1) * P], ident[:])
                    tr.then_inc(s("att_pt_prod"), 1)

                def values(u):
                    h, qt = u // TT, u % TT
                    pe.wait_ge(s("att_pt_taken"), 8 * i + u + 1)
                    if u == 0:
                        pe.wait_ge(s("v_taken"), i + 1)
                        if not first:
                            pe.wait_ge(S[values_free[0]], values_free[1])
                    for b in range(qt + 1):
                        mm = pe.matmul(ps[7][:, qt * P + 64 * h:qt * P + 64 * h + 64],
                                       pT[:, u % 2, b * P:(b + 1) * P], vt[:, b, 64 * h:64 * h + 64],
                                       start=(b == 0), stop=(b == qt))
                    mm.then_inc(s("att_av_prod"), 1)

                scores(0)
                scores(1)
                if before_turns and not first:
                    before_turns()
                for u in range(8):
                    turn(u)
                    if u + 2 < 8:
                        scores(u + 2)
                    if between:
                        between(u)
                    if u >= 1:
                        values(u - 1)
                values(7)

            for m in range(3):
                projection(0, m, range(KB), True)
            pipelined(pe, PAIRS, pair)
            for k in range(KB - 1):
                pe.wait_ge(s("o_ready"), k + 1)
                linear_step("wo", yT, KB, 0, k)
            turn_output(PAIRS - 1)
            linear("wo", yT, KB, lambda k: pe.wait_ge(s("o_ready"), k + 1), done=[KB - 1])
            mean_squares("f1")
            feed_forward(1)
            mean_squares("fin")
            mean_squares("n1")
            pe.wait_ge(s("side_loaded"), 64)
            for k in range(KB):
                pe.wait_ge(s("norm_h_ready"), h_count("n1", k))
                mm = pe.matmul(ps[0][0:24, :], favw[:, k, :], hT[:, k, :], start=(k == 0), stop=(k == KB - 1))
            mm.then_inc(s("fav_prod"), 1)
            pe.wait_ge(s("cum_ready"), 1)
            for t in range(TT):
                tr = pe.transpose(ps[1][:, 8 * t:8 * t + 8], fx8[3][:, t * P:(t + 1) * P], ident[0:8, 0:8])
            tr.then_inc(s("cq_step"), 1)
            pe.wait_ge(s("cq_step"), 2)

            def fox_projection(i, n, ks, first=False):
                if ks[0] == 0 and n % 2 == 0:
                    ring_ready(pe, "fx", i, n // 2)
                if ks[0] == 0 and n == 2 and not first:
                    pe.wait_ge(s("v_taken"), PAIRS + i)
                if ks[0] == 0 and n == 3 and not first:
                    pe.wait_ge(s("att_sc_added"), 64 + 8 * i)
                for k in ks:
                    mm = pe.matmul(ps[n][:], slot(n // 2, 8, 256)[:, k, n % 2 * P:(n % 2 + 1) * P], hT[:, k, :],
                                   start=(k == 0), stop=(k == KB - 1))
                if ks[-1] == KB - 1:
                    mm.then_inc(s("fx_prod"), 1)

            def fox_pair(i, first, last):
                fox_projection(i, 3, range(KB), first)
                for n, src in enumerate((sqq, sqk)):
                    pe.wait_ge(s("fx_sq"), 3 * i + n + 1)
                    pe.matmul(ps[n][:], halfm[:], src, start=True, stop=True).then_inc(s("fx_ms"), 1)
                pe.wait_ge(s("fx_mixed"), 2 * i + 2)
                for t in range(TT):
                    tr = pe.transpose(ps[2][:, t * P:(t + 1) * P], vmix[:, t * P:(t + 1) * P], ident[:])
                tr.then_inc(s("fx_vturned"), 1)
                pe.wait_ge(s("fx_taken"), 4 * i + 4)
                pe.wait_ge(s("fx_qk"), 2 * i + 2)
                attention_core(PAIRS + i, first, (lambda u: u < 6 and fox_projection(i + 1, u // 2, HALVES[u % 2]))
                               if not last else None, None, ("fx_o_taken", i))
                turn_output(PAIRS + i)
                pe.wait_ge(s("fx_sq"), 3 * i + 3)
                pe.matmul(ps[5][:], halfm[:], sqq, start=True, stop=True).then_inc(s("fx_ms"), 1)

            for n in range(3):
                fox_projection(0, n, range(KB), True)
            pipelined(pe, 4, fox_pair)

            ring_ready(pe, "lora", 0, 0)
            pe.wait_ge(s("fx_rms"), 12)
            for k in range(KB):
                mm = pe.matmul(ps[0][:], slot(0, 8, P)[:, k, :], hT[:, k, :], start=(k == 0), stop=(k == KB - 1))
            mm.then_inc(s("lora_prod"), 1)
            ring_ready(pe, "lora", 0, 1)
            pe.wait_ge(s("fx_o_taken"), 4)
            for n, (c, m) in enumerate(((0, P), (P, 32))):
                for k in range(KB):
                    mm = pe.matmul(ps[1 + n][0:m, :], slot(1, 8, 160)[:, k, c:c + m], hT[:, k, :],
                                   start=(k == 0), stop=(k == KB - 1))
                mm.then_inc(s("lora_prod"), 1)
            pe.wait_ge(s("lora_ready"), 4)

            def rw_projection(i, m, k):
                if k == 0 and m != 1:
                    ring_ready(pe, "rw", i, m // 2)
                w = slot(0, 8, 256)[:, k, m * P:(m + 1) * P] if m < 2 else slot(1, 8, P)[:, k, :]
                mm = pe.matmul(ps[(0, 7, 6)[m]][:], w, hT[:, k, :], start=(k == 0), stop=(k == KB - 1))
                if k == KB - 1:
                    mm.then_inc(s("rw_prod"), 1)

            def rw_lora():
                for h in range(2):
                    pe.matmul(ps[1 + h][:], ring[64 * h:64 * h + 64, 1, 1024:1152], lwa[64 * h:64 * h + 64, :],
                              start=True, stop=True).then_inc(s("rw_prod"), 1)
                pe.matmul(ps[3][:], ring[:, 1, 1152:1280], lg0, start=True, stop=False)
                pe.matmul(ps[3][:], ring[0:32, 1, 1280:1408], lg1, start=False, stop=True).then_inc(s("rw_prod"), 1)

            for m in range(3):
                for k in range(KB):
                    rw_projection(0, m, k)
            rw_lora()

            def rw_pair(i, first, last):
                def fill(step):
                    if not last:
                        rw_projection(i + 1, step // KB, step % KB)
                    elif step < 3 * (KB - 1):
                        if step == 0:
                            pe.wait_ge(s("fx_y_ready"), 4)
                            pe.wait_ge(s("rw_y_ready"), 3)
                        linear_step("w_out", yT, KB, step // (KB - 1), step % (KB - 1))

                for n in range(2):
                    pe.wait_ge(s("rw_sq"), 2 * i + n + 1)
                    pe.matmul(ps[6 + n][:], halfm[:], sqr, start=True, stop=True).then_inc(s("rw_ms"), 1)
                for n, src in enumerate((None, BT, KT, vv)):
                    if n == 0:
                        pe.wait_ge(s("rw_ops"), 4 * i + 4)
                        pe.wait_ge(s("rw_taken"), 6 * i + 6)
                    for t in range(TT):
                        tr = pe.transpose(ps[n][:, t * P:(t + 1) * P],
                                          AR[:, t, 0, :] if n == 0 else src[:, t * P:(t + 1) * P], ident[:])
                    tr.then_inc(s("rw_turned"), 1)
                for h in range(2):
                    own = slice(64 * h, 64 * h + 64)
                    for m, lhs in enumerate((BT, KT)):
                        for half in range(2):
                            n = 4 + 2 * m + half
                            if h == 1:
                                pe.wait_ge(s("rw_smt"), 10 * i + 2 * m + half + 1)
                            elif n == 5 and not first:
                                pe.wait_ge(s("rw_y_ready"), i)
                            elif n == 6:
                                pe.wait_ge(s("rw_nrm"), i + 1)
                            elif n == 7:
                                pe.wait_ge(s("rw_bonus"), i + 1)
                            for t in range(2 * half, 2 * half + 2):
                                mm = pe.matmul(ps[n][:, (t % 2) * 256:(t % 2) * 256 + 256],
                                               lhs[own, t * P:(t + 1) * P], AR[own, t, :, :], start=True, stop=True)
                            mm.then_inc(s("rw_sm"), 1)
                    pe.wait_ge(s("rw_tok"), 4 * i + 4)
                    for t in range(TT):
                        mm = pe.matmul(ps[h][:, t * P:(t + 1) * P], AR[own, t, 0, :], BT[own, t * P:(t + 1) * P],
                                       start=True, stop=True)
                    mm.then_inc(s("rw_sm"), 1)
                for n in range(1, 6):
                    for h in range(2):
                        k = 2 * (n - 1) + h
                        pe.wait_ge(s("rw_am"), 10 * i + k + 1)
                        if n == 1:
                            pe.wait_ge(s("rw_d0"), 4 * i + 2 * h + 2)
                        else:
                            pe.wait_ge(s("rw_dt"), 20 * i + 2 * k - 2)
                        for t in range(TT):
                            mm = pe.matmul(ps[h][:, t * P:(t + 1) * P], Am[h][:, t, :], Dm[h][:, t, :],
                                           start=True, stop=True)
                        mm.then_inc(s("rw_x"), 1)
                    for h in range(2):
                        k = 2 * (n - 1) + h
                        pe.wait_ge(s("rw_xt"), 10 * i + k + 1)
                        if n == 1 and h == 0:
                            pe.wait_ge(s("rw_smt"), 10 * i + 10)
                        for w in range(2):
                            for t in range(TT):
                                mm = pe.matmul(ps[2 + 2 * w + h][:, t * P:(t + 1) * P], (DT, Xm)[w][h][:, t, :],
                                               (Xm, DT)[w][h][:, t, :], start=True, stop=True)
                            mm.then_inc(s("rw_dd"), 1)
                for t in range(TT):
                    for h in range(2):
                        mm = pe.matmul(ps[6][:, t * P + 64 * h:t * P + 64 * h + 64], AKT[h][:, t, 0:P],
                                       tokV[:, t, 64 * h:64 * h + 64], start=True, stop=True)
                mm.then_inc(s("rw_g"), 1)
                pe.wait_ge(s("rw_dt"), 20 * i + 20)
                for h in range(2):
                    for t in range(TT):
                        mm = pe.matmul(ps[0][64 * h:64 * h + 64, t * P:(t + 1) * P], tokA[:, t, 64 * h:64 * h + 64],
                                       DT[h][:, t, :], start=True, stop=True)
                mm.then_inc(s("rw_g"), 1)
                pe.wait_ge(s("rw_gt"), 3 * i + 1)
                for t in range(TT):
                    for h in range(2):
                        mm = pe.matmul(ps[7][:, t * P + 64 * h:t * P + 64 * h + 64], DT[h][:, t, :],
                                       Gm[:, t, 64 * h:64 * h + 64], start=True, stop=True)
                mm.then_inc(s("rw_g"), 1)
                pe.wait_ge(s("rw_gt"), 3 * i + 3)
                for c in range(8):
                    t, e = c // 2, c % 2
                    own = slice(64 * e, 64 * e + 64)
                    pe.wait_ge(s("rw_zt"), 8 * i + c + 1)
                    pe.matmul(ps[1 + e][own, 0:P], ApT[:, c * 64:c * 64 + 64], Zs[:, c, :], start=True, stop=True)\
                        .then_inc(s("rw_u"), 1)
                    if c < 7:
                        pe.matmul(ps[3 + e][:, 0:P], tokK[own, t, :], tokV[own, t, :], start=True, stop=False)
                    fill(3 * c)
                    if c < 7:
                        pe.wait_ge(s("rw_ut"), 8 * i + c + 1)
                        pe.matmul(ps[3 + e][:, 0:P], tokB[own, t, :], Usb[own, t, :], start=False, stop=True)\
                            .then_inc(s("rw_z"), 1)
                    fill(3 * c + 1)
                    fill(3 * c + 2)
                pe.wait_ge(s("rw_ut"), 8 * i + 8)
                for t in range(TT):
                    for e in range(2):
                        pe.matmul(ps[5][64 * e:64 * e + 64, t * P:(t + 1) * P], AR[:, t, 1, 64 * e:64 * e + 64],
                                  Zs[:, 2 * t + e, :], start=True, stop=False, skip_group_check=True)
                    for h in range(2):
                        cols = slice(64 * h, 64 * h + 64)
                        for m, (lhs, rhs) in enumerate(((ABT, Usb), (AKT, tokV))):
                            mm = pe.matmul(ps[5][:, t * P + 64 * h:t * P + 64 * h + 64], lhs[h][:, t, P:256],
                                           rhs[:, t, cols], start=False, stop=(m == 1), skip_group_check=True)
                mm.then_inc(s("rw_out_step"), 1)
                if not last:
                    rw_lora()
                else:
                    for k in range(KB - 1):
                        linear_step("w_out", yT, KB, 3, k)
                pe.wait_ge(s("rw_out_step"), 8 * i + 7)
                for t in range(TT):
                    tr = pe.transpose(ps[5][:, t * P:(t + 1) * P], y_sb[:, t * P:(t + 1) * P], ident[:])
                tr.then_inc(s("rw_out_step"), 1)
            pipelined(pe, 4, rw_pair)
            linear("w_out", yT, KB, lambda k: pe.wait_ge(s("rw_y_ready"), 4), done=[KB - 1] * 4)

            mean_squares("n2")
            pe.wait_ge(s("side_loaded"), 64)
            for t in range(TT):
                for k in range(KB):
                    if t == 0:
                        pe.wait_ge(s("norm_h_ready"), h_count("n2", k))
                    mm = pe.matmul(ps[0][:, t * 64:t * 64 + 64], hT[:, k, t * P:(t + 1) * P], rwt[:, k, :],
                                   start=(k == 0), stop=(k == KB - 1))
            mm.then_inc(s("rt_prod"), 1)
            pe.wait_ge(s("mod_ready"), ADA_UNITS)
            pe.transpose(ps[1][0:8, 0:P], mod[:, 40:48], ident[:]).then_inc(s("rt_prod"), 1)
            for t in range(TT):
                for half in range(2):
                    wait(pe, s("htok_taken"), 2 * (t - 1) + half + 1)
                    for b in range(4):
                        tr = pe.transpose(ps[2 + half][:, b * P:(b + 1) * P], hT[:, 4 * half + b, t * P:(t + 1) * P], ident[:])
                    tr.then_inc(s("htok_turned"), 1)
            pe.wait_ge(s("sh_loaded"), 48)
            w8 = sh_gu.rearrange("p (m k n) -> p m k n", m=2, k=KB)
            for m in range(2):
                for b in range(2):
                    for k in range(KB):
                        mm = pe.matmul(ps[4 + 2 * m + b][:], w8[:, m, k, b * P:(b + 1) * P], hT[:, k, :],
                                       start=(k == 0), stop=(k == KB - 1))
                    mm.then_inc(s("sh_gu_prod"), 1)
            pe.wait_ge(s("rt_masked"), 1)
            pe.wait_ge(s("moe_consts"), 5)
            for t in range(TT):
                for u in range(t + 1):
                    mm = pe.matmul(ps[0][:, t * 64:t * 64 + 64], (earlier if u == t else ones)[:], wtok[:, u, :],
                                   start=(u == 0), stop=(u == t))
            for t in range(TT):
                mm = pe.matmul(ps[1][:, 0:64], ones[:], wtok[:, t, :], start=(t == 0), stop=(t == TT - 1))
            mm.then_inc(s("places_prod"), 1)

            def places_tokens(n, par):
                pe.wait_ge(s("onehot_ready"), n + 1)
                wait(pe, s("slot_ready"), n)
                for t in range(TT):
                    mm = pe.matmul(ps[0][:, 0:1], onehot[par][:, t, :], tokid[:, t:t + 1],
                                   start=(t == 0), stop=(t == TT - 1))
                mm.then_inc(s("slot_prod"), 1)

            def turn_rows(n, par):
                pe.wait_ge(s(f"hrow{par}_loaded"), 8 * (n - par) + 16)
                wait(pe, s("hgt_ready"), 2 * n)
                for half in range(2):
                    for b in range(4):
                        tr = pe.transpose(ps[1 + half][:, b * P:(b + 1) * P],
                                          hrow[par][:, (4 * half + b) * P:(4 * half + b + 1) * P], ident[:])
                    tr.then_inc(s("hrow_turned"), 1)

            places_tokens(0, 0)
            places_tokens(1, 1)
            wd = sh_dn.rearrange("p (k n) -> p k n", k=2)
            pe.wait_ge(s("sh_act"), 2)
            for b in range(KB):
                wait(pe, s("sh_added"), b - 3)
                for k in range(2):
                    mm = pe.matmul(ps[4 + b % 4][:], wd[:, k, b * P:(b + 1) * P], xact[:, k, :],
                                   start=(k == 0), stop=(k == 1))
                mm.then_inc(s("sh_prod"), 1)
            turn_rows(0, 0)
            pe.wait_ge(s("sh_added"), KB)
            for t in range(TT):
                for half in range(2):
                    m = 2 * t + half
                    wait(pe, s("res_taken"), m - 3)
                    for b in range(4):
                        tr = pe.transpose(ps[4 + m % 4][:, b * P:(b + 1) * P], xT[:, 4 * half + b, t * P:(t + 1) * P], ident[:])
                    tr.then_inc(s("res_turned"), 1)
            pe.wait_ge(s("res_taken"), 2 * TT)

            def expert(n, par):
                w = exw[par]
                w8 = w[:, 0:4096].rearrange("p (m k n) -> p m k n", m=2, k=KB)
                wd = w[:, 4096:6144].rearrange("p (k n) -> p k n", k=2)
                pe.wait_ge(s(f"expgu{par}_loaded"), 16 * (n - par) + 32)
                pe.wait_ge(s("hgt_ready"), 2 * n + 2)
                for m in range(2):
                    wait(pe, s(("exp_sil", "exp_act")[m]), n)
                    for b in range(2):
                        for k in range(KB):
                            mm = pe.matmul(ps[3 + m][:, b * P:(b + 1) * P], w8[:, m, k, b * P:(b + 1) * P],
                                           hgT[par][:, k, :], start=(k == 0), stop=(k == KB - 1))
                    mm.then_inc(s("exp_gu"), 1)
                turn_rows(n + 1, 1 - par)
                places_tokens(n + 2, par)
                pe.wait_ge(s("exp_act"), n + 1)
                pe.wait_ge(s(f"expdn{par}_loaded"), 8 * (n - par) + 16)
                for half in range(2):
                    wait(pe, s("y_ready"), 2 * n + half - 1)
                    for k in range(2):
                        mm = pe.matmul(ps[5 + half][:], eact[par][:, k * P:(k + 1) * P],
                                       wd[:, k, half * 512:(half + 1) * 512], start=(k == 0), stop=(k == 1))
                    mm.then_inc(s("exp_down"), 1)

            def experts(i, first):
                for par in range(2):
                    expert(2 * i + par, par)
            all_experts(pe, experts)

        @block.scalar
        def _(act_e):
            order = Order(act_e, s("act_order"))

            def squares(n, ready, count):
                for b in range(KB):
                    act_e.wait_ge(S[ready], count - KB + b + 1)
                    nc.scalar.activation(sq[:, b, :], xT[:, b, :], ACT.Square).then_inc(s("norm_sq_ready"), 1)
                act_e.wait_ge(s("norm_ss_ready"), nth(n))
                nc.scalar.activation(rms[:], ps[7][:], ACT.Sqrt, bias=epsc[:]).then_inc(s("norm_rms_ready"), 1)

            def shift(n, c):
                for b in range(KB):
                    act_e.wait_ge(s("h_scaled"), KB * (n == "n2") + b + 1)
                    nc.scalar.activation(hT[:, b, :], hT[:, b, :], ACT.Identity, bias=mod[:, c + b:c + b + 1])\
                        .then_inc(s("norm_h_ready"), 1)

            def feed_forward(l):
                c0 = C_CONV + 256 * l

                def body(i, first):
                    for j in range(2):
                        for b in range(2):
                            blk = 2 * i + j + 22 * b
                            settle(act_e, s("ff_prod"), 44 * l + 4 * i + 2 * j + b + 1)
                            if not first:
                                settle(act_e, s("ff_act"), 22 * l + 2 * i + j - 1)
                            nc.scalar.activation(conv[j][b], ps[2 * j + b][:], ACT.Identity,
                                                 scale=col[:, bass.ds(c0 + P + blk, 1)],
                                                 bias=col[:, bass.ds(c0 + P + 44 + blk, 1)])\
                                .then_inc(s("ff_tap2"), 1)
                    for j in range(2):
                        settle(act_e, s("ff_tap0"), 44 * l + 4 * i + 2 * j + 2)
                        nc.scalar.activation(sil[j], conv[j][1], ACT.Silu).then_inc(s("ff_silu"), 1)
                looped(act_e, FB // 2, body)

            for b in range(0, KB, 2):
                act_e.wait_ge(s("x_turned"), b + 1)
                act_e.wait_ge(s("x_ready"), b) if b else None
                nc.scalar.copy(xT[:, b, :], ps[b][:]).then_inc(s("x_ready"), 1)
            act_e.wait_ge(s("col_ready"), 6)
            nc.scalar.activation(csil[:], col[:, C_C:C_C + 8], ACT.Silu).then_inc(s("col_ready"), 1)
            squares("a", "x_ready", KB)
            act_e.wait_ge(s("consts"), NCONST)
            for u in range(4):
                for t in range(TT):
                    act_e.wait_ge(s("gv_prod"), 4 * u + t + 1)
                    nc.scalar.activation(vtok[:, t, u * 256:(u + 1) * 256], ps[4 * (u % 2) + t][:, 0:256],
                                         ACT.Gelu_apprx_tanh).then_inc(s("gv_taken"), 1)
            act_e.wait_ge(s("gv_taken"), 16)
            for t in range(TT):
                order(nc.scalar.activation(sq[:, 0:2, :], vtok[:, t, :].rearrange("p (a b) -> p a b", a=2), ACT.Square,
                                           accum_out=ss4[:, t:t + 1]))
            nc.scalar.activation(ss4[:, 4:8], ss4[:, 0:4], ACT.Sqrt, scale=1.0 / D, bias=epsc[:])\
                .then_inc(s("vrms_ready"), 1)
            for n in range(8):
                act_e.wait_ge(s("gu_prod"), n + 1)
                nc.scalar.activation(gT[:, n, :], ps[n % 4][:], ACT.Gelu_apprx_tanh).then_inc(s("gu_taken"), 1)
            squares("f0", "lin_added", KB)
            feed_forward(0)
            squares("att", "lin_added", 2 * KB)

            def pair(i, first):
                for b in range(2):
                    settle(act_e, s("qkv_prod"), 3 * i + b + 1)
                    if b == 0 and not first:
                        settle(act_e, s("att_sc_prod"), 8 * i)
                    nc.scalar.activation((qT, kT)[b], ps[b][:], ACT.Copy, scale=(HD ** -0.5, 1.0)[b])\
                        .then_inc(s("qk_taken"), 1)
                attention_core(i, first, lambda: take_output(i - 1))

            def take_output(i):
                settle(act_e, s("att_ot_prod"), i + 1)
                at = slice(i, i + 1) if isinstance(i, int) else bass.ds(i, 1)
                nc.scalar.copy(yT[:, at, :], ps[7][:].rearrange("p (a b) -> p a b", a=1)).then_inc(s("o_ready"), 1)

            def attention_core(i, first, behind_first=None):
                def exps(u):
                    n = (u % TT + 1) * P
                    settle(act_e, s("att_negm_ready"), 8 * i + u + 1)
                    if not (first and u < 2):
                        settle(act_e, s("att_pt_prod"), 8 * i + u - 1)
                    nc.scalar.activation(p_sb[:, u % 2, 0:n], s_sb[:, u % 2, 0:n], ACT.Exp, bias=negm[:, u:u + 1],
                                         accum_out=rsum[:, u:u + 1]).then_inc(s("att_p_ready"), 1)

                exps(0)
                if behind_first and not first:
                    behind_first()
                for u in range(8):
                    if u < 7:
                        exps(u + 1)
                    n = (u % TT + 1) * P
                    settle(act_e, s("att_pt_prod"), 8 * i + u + 1)
                    if not (first and u < 2):
                        settle(act_e, s("att_av_prod"), 8 * i + u - 1)
                    nc.scalar.copy(pT[:, u % 2, 0:n], ps[5 + u % 2][:, 0:n]).then_inc(s("att_pt_taken"), 1)
            looped(act_e, PAIRS, pair)
            take_output(PAIRS - 1)
            squares("f1", "lin_added", 3 * KB)
            feed_forward(1)
            squares("fin", "lin_added", 4 * KB)
            squares("n1", "norm_h_ready", h_count("fin", KB - 1))
            shift("n1", 0)
            act_e.wait_ge(s("fav_prod"), 1)
            nc.scalar.activation(sig24, ps[0][0:24, :], ACT.Sigmoid).then_inc(s("fav_sig"), 1)
            act_e.wait_ge(s("f_abs"), 1)
            order(nc.scalar.activation(fx8[2], fx8[1], ACT.Exp, scale=-1.0))
            nc.scalar.activation(fx8[2], fx8[2], ACT.Ln, bias=onec[0:8, :]).then_inc(s("f_log"), 1)

            def fox_take(i, n):
                dst, fn = ((qraw, ACT.Copy), (kpad[:, 1:T + 1], ACT.Copy), (vpad[:, 1:T + 1], ACT.Copy), (gsig, ACT.Sigmoid))[n]
                settle(act_e, s("fx_prod"), 4 * i + n + 1)
                nc.scalar.activation(dst, ps[n][:], fn).then_inc(s("fx_taken"), 1)

            act_e.wait_ge(s("pads"), 1)
            for n in range(3):
                fox_take(0, n)

            def fox_pair(i, first, last):
                if not first:
                    settle(act_e, s("fx_y_ready"), i)
                fox_take(i, 3)
                settle(act_e, s("fx_taken"), 4 * i + 1)
                nc.scalar.activation(sqq, qraw, ACT.Square).then_inc(s("fx_sq"), 1)
                settle(act_e, s("fx_mixed"), 2 * i + 1)
                nc.scalar.activation(sqk, kmix, ACT.Square).then_inc(s("fx_sq"), 1)
                for n, dst in enumerate((rq, rk)):
                    settle(act_e, s("fx_ms"), 3 * i + n + 1)
                    nc.scalar.activation(dst, ps[n][:], ACT.Sqrt, bias=epsc[:]).then_inc(s("fx_rms"), 1)
                attention_core(PAIRS + i, first)
                if not last:
                    for n in range(3):
                        fox_take(i + 1, n)
                settle(act_e, s("att_ot_prod"), PAIRS + i + 1)
                nc.scalar.copy(oraw, ps[7][:]).then_inc(s("fx_o_taken"), 1)
                settle(act_e, s("fx_o_taken"), i + 1)
                nc.scalar.activation(sqq, oraw, ACT.Square).then_inc(s("fx_sq"), 1)
                settle(act_e, s("fx_ms"), 3 * i + 3)
                nc.scalar.activation(rq, ps[5][:], ACT.Sqrt, bias=epsc[:]).then_inc(s("fx_rms"), 1)
            pipelined(act_e, 4, fox_pair)

            act_e.wait_ge(s("fx_y_ready"), 4)
            for n, (dst, m) in enumerate(((rp, P), (kp, P), (vp, 32))):
                act_e.wait_ge(s("lora_prod"), n + 1)
                act_e.wait_ge(s("pads"), 2)
                nc.scalar.copy(dst[0:m, 1:T + 1], ps[n][0:m, :]).then_inc(s("lora_taken"), 1)
            act_e.wait_ge(s("lora_mixed"), 3)
            nc.scalar.activation(lwa[0:64, :], rr[0:64, :], ACT.Tanh).then_inc(s("lora_ready"), 1)
            nc.scalar.copy(lwa[64:128, :], rr[64:128, :]).then_inc(s("lora_ready"), 1)
            nc.scalar.activation(lg0, k0, ACT.Sigmoid).then_inc(s("lora_ready"), 1)
            nc.scalar.activation(lg1, vv[0:32, :], ACT.Sigmoid).then_inc(s("lora_ready"), 1)

            def take_projections(i):
                for n, dst in enumerate((rp, kp, vp)):
                    settle(act_e, s("rw_prod"), 6 * i + n + 1)
                    nc.scalar.copy(dst[:, 1:T + 1], ps[(0, 7, 6)[n]][:]).then_inc(s("rw_taken"), 1)

            def take_lora(i):
                one = lambda c: col[:, c + i:c + i + 1] if isinstance(i, int) else col[:, bass.ds(c + i, 1)]
                for n, (dst, b) in enumerate(((ld, one(C_W0)), (aa, one(C_A0)))):
                    settle(act_e, s("rw_prod"), 6 * i + n + 4)
                    nc.scalar.activation(dst, ps[1 + n][:], ACT.Sigmoid, bias=b).then_inc(s("rw_taken"), 1)

            act_e.wait_ge(s("lora_ready"), 4)
            take_projections(0)
            take_lora(0)

            def rw_pair(i, first, last):
                settle(act_e, s("rw_prod"), 6 * i + 6)
                if not first:
                    settle(act_e, s("rw_y_ready"), i)
                nc.scalar.copy(gg, ps[3][:]).then_inc(s("rw_taken"), 1)
                settle(act_e, s("rw_kk"), i + 1)
                nc.scalar.activation(sqr, kkn, ACT.Square).then_inc(s("rw_sq"), 1)
                settle(act_e, s("rw_ms"), 2 * i + 1)
                nc.scalar.activation(nrm, ps[6][:], ACT.Sqrt, scale=float(HD)).then_inc(s("rw_nrm"), 1)
                settle(act_e, s("rw_L"), 2 * i + 2)
                for dst, src, sc in ((Pt, Lc, 1.0), (Pinv, Lc, -1.0), (Pprev, Pprev, 1.0)):
                    nc.scalar.activation(dst, src, ACT.Exp, scale=sc).then_inc(s("rw_P"), 1)
                for n, dst in enumerate((tokA, tokB, tokK, tokV)):
                    settle(act_e, s("rw_turned"), 4 * i + n + 1)
                    nc.scalar.copy(dst, tiles4(ps[n][:])).then_inc(s("rw_tok"), 1)
                for n in range(1, 6):
                    for h in range(2):
                        k = 2 * (n - 1) + h
                        settle(act_e, s("rw_x"), 10 * i + k + 1)
                        if n > 1:
                            settle(act_e, s("rw_dd"), 20 * i + 2 * k - 2)
                        nc.scalar.copy(Xm[h], tiles4(ps[h][:])).then_inc(s("rw_xt"), 1)
                settle(act_e, s("rw_g"), 3 * i + 1)
                nc.scalar.copy(Gm, tiles4(ps[6][:])).then_inc(s("rw_gt"), 1)
                settle(act_e, s("rw_g"), 3 * i + 2)
                nc.scalar.copy(ApT, ps[0][:]).then_inc(s("rw_gt"), 1)
                settle(act_e, s("rw_g"), 3 * i + 3)
                nc.scalar.copy(Wm, tiles4(ps[7][:])).then_inc(s("rw_gt"), 1)
                if not last:
                    take_projections(i + 1)
                settle(act_e, s("rw_out_step"), 8 * i + 1)
                nc.scalar.copy(y_sb, ps[5][:]).then_inc(s("rw_out_step"), 1)
                settle(act_e, s("rw_out_step"), 8 * i + 3)
                nc.scalar.activation(y_sq, y_sb, ACT.Square).then_inc(s("rw_out_step"), 1)
                settle(act_e, s("rw_out_step"), 8 * i + 5)
                nc.scalar.activation(st8[:, 0:8], st8[:, 8:16], ACT.Sqrt, scale=1.0 / HD, bias=lnxe[:])\
                    .then_inc(s("rw_out_step"), 1)
                if not last:
                    take_lora(i + 1)
            pipelined(act_e, 4, rw_pair)

            squares("n2", "lin_added", 5 * KB)
            shift("n2", 24)
            act_e.wait_ge(s("rt_prod"), 1)
            nc.scalar.activation(sco, ps[0][:, 0:256].rearrange("p (t e) -> p t e", t=TT), ACT.Sigmoid)\
                .then_inc(s("rt_sig"), 1)

            act_e.wait_ge(s("rt_prod"), 2)
            order(nc.scalar.copy(g2T, ps[1][0:8, 0:P]))
            act_e.dma_start(g2_dram, g2T).then_inc(s("g2_stored"), 16)
            for t in range(TT):
                for half in range(2):
                    act_e.wait_ge(s("htok_turned"), 2 * t + half + 1)
                    nc.scalar.copy(htok[:, t, half * 512:(half + 1) * 512], ps[2 + half][:]).then_inc(s("htok_taken"), 1)
                if t % 2:
                    act_e.wait_ge(s("htok_taken"), 2 * t + 2)
                    act_e.dma_start(h_dram[(t - 1) * P:(t + 1) * P, :].rearrange("(t p) d -> p t d", p=P),
                                    htok[:, t - 1:t + 1, :]).then_inc(s("h_stored"), 16)
            for b in range(2):
                act_e.wait_ge(s("sh_gu_prod"), b + 1)
                nc.scalar.activation(xsil[:, b, :], ps[4 + b][:], ACT.Silu).then_inc(s("sh_sil"), 1)

            def rows_turned(n, par):
                for half in range(2):
                    settle(act_e, s("hrow_turned"), 2 * n + half + 1)
                    settle(act_e, s("exp_gu"), 2 * n - 2)
                    nc.scalar.copy(hgT[par][:, 4 * half:4 * half + 4, :], tiles4(ps[1 + half][:])).then_inc(s("hgt_ready"), 1)

            rows_turned(0, 0)
            for m in range(2 * TT):
                act_e.wait_ge(s("res_turned"), m + 1)
                nc.scalar.copy(res[:, m // 2, m % 2 * 512:(m % 2 + 1) * 512], ps[4 + m % 4][:]).then_inc(s("res_taken"), 1)

            def expert(n, par):
                settle(act_e, s("exp_gu"), 2 * n + 1)
                settle(act_e, s("exp_act"), n - 1)
                nc.scalar.activation(esil[par], ps[3][:, 0:256], ACT.Silu).then_inc(s("exp_sil"), 1)
                rows_turned(n + 1, 1 - par)
                settle(act_e, s("y_ready"), 2 * n + 2)
                act_e.dma_start(y_dram[bass.ds(n * P, P), :], yrow[par]).then_inc(s(f"y{par}_stored"), 16)

            def experts(i, first):
                for par in range(2):
                    expert(2 * i + par, par)
            all_experts(act_e, experts)
            for t in range(TT):
                act_e.wait_ge(s("y_summed"), 6 * t + 6)
                order(nc.scalar.activation(ffw[:, 0:D], res[:, t, :], ACT.Square, accum_out=ss4[:, t:t + 1]))
                nc.scalar.activation(ss4[:, 4 + t:5 + t], ss4[:, t:t + 1], ACT.Sqrt, scale=1.0 / D, bias=epsc[:])\
                    .then_inc(s("fin_rms"), 1)

        @block.vector
        def _(dve):
            order = Order(dve, s("dve_order"))

            def normalise(n, outs):
                dve.wait_ge(s("norm_rms_ready"), nth(n))
                order(nc.vector.reciprocal(rstd[:], rms[:]))
                for dst, gain in outs:
                    for b in range(KB):
                        nc.vector.scalar_tensor_tensor(out=dst[:, b, :], in0=xT[:, b, :],
                                                       scalar=col[:, gain + b:gain + b + 1], in1=rstd[:],
                                                       op0=ALU.mult, op1=ALU.mult).then_inc(s("norm_h_ready"), 1)

            def add_linear(stage, between={}):
                base = plan[stage][6]
                for n in range(KB):
                    dve.wait_ge(s("lin_prod"), base + n + 1)
                    nc.vector.tensor_tensor(xT[:, n, :], ps[BANKS[stage][n % 4]][:], xT[:, n, :], ALU.add)\
                        .then_inc(s("lin_added"), 1)
                    if n in between:
                        ada_unit(between[n], between[n] % 2)

            def feed_forward(l):
                c0 = C_CONV + 256 * l

                def body(i, first):
                    for j in range(2):
                        for b in range(2):
                            blk = 2 * i + j + 22 * b
                            c = conv[j][b]
                            n = 44 * l + 4 * i + 2 * j + b + 1
                            settle(dve, s("ff_tap2"), n)
                            nc.vector.scalar_tensor_tensor(
                                out=c[:, 1:T], in0=ps[2 * j + b][:, 0:T - 1],
                                scalar=col[:, bass.ds(c0 + 44 + blk, 1)], in1=c[:, 1:T],
                                op0=ALU.mult, op1=ALU.add).then_inc(s("ff_tap1"), 1)
                            settle(dve, s("ff_tap1"), n)
                            nc.vector.scalar_tensor_tensor(
                                out=c[:, 2:T], in0=ps[2 * j + b][:, 0:T - 2],
                                scalar=col[:, bass.ds(c0 + blk, 1)], in1=c[:, 2:T],
                                op0=ALU.mult, op1=ALU.add).then_inc(s("ff_tap0"), 1)
                        if l == 0:
                            ada_unit(2 * i + j, j)
                    for j in range(2):
                        settle(dve, s("ff_silu"), 22 * l + 2 * i + j + 1)
                        nc.vector.tensor_tensor(act[:, bass.ds(2 * i + j, 1), :],
                                                sil[j].rearrange("p (a b) -> p a b", a=1),
                                                conv[j][0].rearrange("p (a b) -> p a b", a=1), ALU.mult)\
                            .then_inc(s("ff_act"), 1)
                looped(dve, FB // 2, body)
                add_linear(f"f{l}dn", {3: ADA, 5: ADA + 1} if l == 0 else {})

            for b in range(1, KB, 2):
                dve.wait_ge(s("x_turned"), b + 1)
                dve.wait_ge(s("x_ready"), b)
                nc.vector.tensor_copy(xT[:, b, :], ps[b][:]).then_inc(s("x_ready"), 1)
            for t, rows in enumerate(PARAM_ROWS):
                dve.wait_ge(s("params_turned"), t + 1)
                nc.vector.tensor_copy(col[:, t * P:t * P + rows], ps[t][:, 0:rows]).then_inc(s("col_ready"), 1)
            dve.wait_ge(s("rel_loaded"), 16)
            nc.vector.tensor_copy(relE[:, REL:RELW], relE[:, REL - 1:REL].to_broadcast([16, RELW - REL]))\
                .then_inc(s("rel_ext"), 1)
            dve.wait_ge(s("rel_ext"), 1)
            nc.vector.tensor_copy(relR[:], relE[:, ::-1]).then_inc(s("rel_ext"), 1)
            dve.wait_ge(s("ws_loaded"), 32)
            nc.vector.memset(wsraw[0:64, :, 64:128], 0.0).then_inc(s("ws_step"), 1)
            dve.wait_ge(s("ws_step"), 2)
            order(nc.vector.tensor_copy(wsT[:, 0:4, :], ps[6][:].rearrange("p (g j) -> p g j", g=4)))
            nc.vector.tensor_copy(wsT[:, 4:8, :], ps[7][:].rearrange("p (g j) -> p g j", g=4)).then_inc(s("ws_step"), 1)

            def ada_unit(u, j):
                settle(dve, s("mod_prod"), u + 1)
                nc.vector.tensor_tensor(mod[:, bass.ds(2 * u, 2)], ps[4 + j][:, 0:2],
                                        col[:, bass.ds(C_ADAB + 2 * u, 2)], ALU.add).then_inc(s("mod_ready"), 1)

            normalise("a", [(hT, C_A)])
            dve.wait_ge(s("vrms_ready"), 1)
            order(nc.vector.reciprocal(ss4[:, 8:12], ss4[:, 4:8]))
            for t in range(TT):
                nc.vector.tensor_scalar(vtok[:, t, :], vtok[:, t, :], ss4[:, 8 + t:9 + t], None, ALU.mult)\
                    .then_inc(s("vn_ready"), 1)
            dve.wait_ge(s("ws_loaded"), 32)
            dve.wait_ge(s("gu_taken"), 8)
            for g in range(8):
                dve.wait_ge(s("sp_prod"), g + 1)
                bank = 4 + g if g < 4 else g - 4
                order(nc.vector.scalar_tensor_tensor(
                    out=sptmp.rearrange("p (n i) -> p n i", n=TT), in0=ps[bank][:].rearrange("p (n i) -> p n i", n=TT),
                    scalar=col[:, C_VN + g:C_VN + g + 1],
                    in1=bsb[:, g, :].unsqueeze(1).to_broadcast([P, TT, P]), op0=ALU.mult, op1=ALU.add))
                nc.vector.tensor_tensor(gT[:, g, :], gT[:, g, :], sptmp, ALU.mult).then_inc(s("gated"), 1)
                dve.wait_ge(s("gated"), g + 1)
            add_linear("go")
            normalise("f0", [(hT, C_F)])
            feed_forward(0)
            normalise("att", [(hT, C_B), (gT, C_KV)])
            dve.wait_ge(s("consts"), NCONST)
            dve.wait_ge(s("rel_stored"), 32)

            def pair(i, first):
                dve.wait_ge(s("qkv_prod"), 3 * i + 3)
                if not first:
                    dve.wait_ge(s("att_av_prod"), 8 * i)
                nc.vector.tensor_copy(vt, ps[2][:].rearrange("p (t c) -> p t c", t=TT)).then_inc(s("v_taken"), 1)
                for u in range(8):
                    h, qt = u // TT, u % TT
                    n, far = (qt + 1) * P, max(qt - 1, 0) * P
                    sc = ps[3 + u % 2]
                    settle(dve, s("att_sc_prod"), 8 * i + u + 1)
                    if not (first and u < 2):
                        settle(dve, s("att_p_ready"), 8 * i + u - 1)
                    if far:
                        nc.vector.tensor_scalar(s_sb[:, u % 2, 0:far], sc[:, 0:far],
                                                biasT[:, bass.ds(2 * i + h, 1), 0:1].rearrange("p a b -> p (a b)"), None, ALU.add)
                    nc.vector.tensor_tensor(s_sb[:, u % 2, far:n].unsqueeze(1), sc[:, far:n].unsqueeze(1),
                                            biasT[:, bass.ds(2 * i + h, 1), 256 - (n - far):256],
                                            ALU.add).then_inc(s("att_sc_added"), 1)
                    row_max(i, u, n)
                attention_out(i, first)

            def row_max(i, u, n):
                dve.wait_ge(s("att_sc_added"), 8 * i + u + 1)
                nc.vector.tensor_reduce(mx[:, u:u + 1], s_sb[:, u % 2, 0:n], AX.X, ALU.max).then_inc(s("att_sc_max"), 1)
                settle(dve, s("att_sc_max"), 8 * i + u + 1)
                nc.vector.tensor_scalar(negm[:, u:u + 1], mx[:, u:u + 1], -1.0, None, ALU.mult)\
                    .then_inc(s("att_negm_ready"), 1)

            def attention_out(i, first):
                settle(dve, s("att_p_ready"), 8 * i + 8)
                nc.vector.reciprocal(rinv, rsum).then_inc(s("att_r_inv"), 1)
                settle(dve, s("att_r_inv"), i + 1)
                dve.wait_ge(s("att_av_prod"), 8 * i + 8)
                if not first:
                    dve.wait_ge(s("att_ot_prod"), i)
                nc.vector.tensor_tensor(o_sb.rearrange("p (t h d) -> p h t d", t=TT, h=2),
                                        ps[7][:].rearrange("p (t h d) -> p h t d", t=TT, h=2),
                                        rinv.rearrange("p (h t) -> p h t", h=2).unsqueeze(3)
                                        .to_broadcast([P, 2, TT, HD]), ALU.mult).then_inc(s("att_o_norm"), 1)
            looped(dve, PAIRS, pair)
            add_linear("wo")
            normalise("f1", [(hT, C_F + 8)])
            feed_forward(1)
            normalise("fin", [(xT, C_FIN)])

            def normalise_mod(n, gain):
                dve.wait_ge(s("norm_rms_ready"), nth(n))
                order(nc.vector.reciprocal(rstd[:], rms[:]))
                for b in range(KB):
                    nc.vector.scalar_tensor_tensor(out=hT[:, b, :], in0=xT[:, b, :], scalar=gmod[:, gain + b:gain + b + 1],
                                                   in1=rstd[:], op0=ALU.mult, op1=ALU.mult).then_inc(s("h_scaled"), 1)

            dve.wait_ge(s("mod_ready"), ADA_UNITS)
            nc.vector.scalar_tensor_tensor(out=gmod[:, 0:8], in0=mod[:, 8:16], scalar=1.0, in1=col[:, C_N1:C_N1 + 8],
                                           op0=ALU.add, op1=ALU.mult)
            nc.vector.scalar_tensor_tensor(out=gmod[:, 8:16], in0=mod[:, 32:40], scalar=1.0, in1=col[:, C_N2:C_N2 + 8],
                                           op0=ALU.add, op1=ALU.mult)
            order(nc.vector.tensor_scalar(qn8, col[:, C_QN:C_QN + 4], HD ** -0.5, None, ALU.mult))
            normalise_mod("n1", 0)
            nc.vector.memset(kpad[:, 0:1], 0.0)
            nc.vector.memset(vpad[:, 0:1], 0.0).then_inc(s("pads"), 1)
            dve.wait_ge(s("side_loaded"), 64)
            dve.wait_ge(s("fav_sig"), 1)
            order(nc.vector.tensor_scalar(fx8[0], ps[0][0:8, :], fbias[:], None, ALU.add))
            nc.vector.scalar_tensor_tensor(out=fx8[1], in0=fx8[0], scalar=-1.0, in1=fx8[0], op0=ALU.mult, op1=ALU.max)\
                .then_inc(s("f_abs"), 1)
            dve.wait_ge(s("f_log"), 1)
            order(nc.vector.scalar_tensor_tensor(out=fx8[1], in0=fx8[0], scalar=0.0, in1=fx8[2], op0=ALU.min,
                                                 op1=ALU.subtract))
            nc.vector.tensor_tensor_scan(fx8[3], ones8[:], fx8[1], 0.0, ALU.mult, ALU.add).then_inc(s("cum_ready"), 1)
            dve.wait_ge(s("cq_step"), 1)
            nc.vector.tensor_copy(cq, ps[1][:, 0:32].rearrange("p (t h) -> p t h", t=TT)).then_inc(s("cq_step"), 1)
            dve.wait_ge(s("cq_step"), 2)
            dve.wait_ge(s("pads"), 1)
            steps = Order(dve, s("fx_order"), (s("consts"), NCONST))

            def token_shift(dst, pad, gate):
                steps(nc.vector.tensor_tensor(dst, pad[:, 0:T], pad[:, 1:T + 1], ALU.subtract))
                steps(nc.vector.tensor_tensor(dst, dst, gate, ALU.mult))
                nc.vector.tensor_tensor(dst, dst, pad[:, 1:T + 1], ALU.add).then_inc(s("fx_mixed"), 1)

            def fox_pair(i, first):
                steps.round(i, 16)
                settle(dve, s("fx_rows"), 80 * i + 80)
                if not first:
                    settle(dve, s("fx_y_ready"), i)
                settle(dve, s("fx_taken"), 4 * i + 2)
                token_shift(kmix, kpad, akb)
                settle(dve, s("fx_taken"), 4 * i + 3)
                token_shift(vmix, vpad, avb)
                settle(dve, s("fx_mixed"), 2 * i + 2)
                for n, (dst, src, r, gain) in enumerate(((qT, qraw, rq, small[:, bass.ds(48 + i, 1)]),
                                                         (kT, kmix, rk, col[:, bass.ds(C_KN + i, 1)]))):
                    settle(dve, s("fx_rms"), 3 * i + n + 1)
                    steps(nc.vector.reciprocal(r, r))
                    nc.vector.scalar_tensor_tensor(out=dst, in0=src, scalar=gain, in1=r, op0=ALU.mult, op1=ALU.mult)\
                        .then_inc(s("fx_qk"), 1)
                settle(dve, s("fx_vturned"), i + 1)
                nc.vector.tensor_copy(vt, ps[2][:].rearrange("p (t c) -> p t c", t=TT)).then_inc(s("v_taken"), 1)
                for u in range(8):
                    h, qt = u // TT, u % TT
                    n = (qt + 1) * P
                    settle(dve, s("att_sc_prod"), 64 + 8 * i + u + 1)
                    if not (first and u < 2):
                        settle(dve, s("att_p_ready"), 64 + 8 * i + u - 1)
                    row = s_sb[:, u % 2, :]
                    steps(nc.vector.scalar_tensor_tensor(out=row[:, 0:n], in0=ps[3 + u % 2][:, 0:n],
                                                         scalar=cq[:, qt, bass.ds(2 * i + h, 1)], in1=ckb[:, h, 0:n],
                                                         op0=ALU.add, op1=ALU.subtract))
                    nc.vector.tensor_tensor(row[:, n - P:n], row[:, n - P:n], tri[:], ALU.add)\
                        .then_inc(s("att_sc_added"), 1)
                    row_max(PAIRS + i, u, n)
                attention_out(PAIRS + i, first)
                settle(dve, s("fx_rms"), 3 * i + 3)
                steps(nc.vector.reciprocal(rq, rq))
                steps(nc.vector.scalar_tensor_tensor(out=kmix, in0=oraw, scalar=col[:, bass.ds(C_ON + i, 1)], in1=rq,
                                                     op0=ALU.mult, op1=ALU.mult))
                one = lambda x: x.rearrange("p (a b) -> p a b", a=1)
                nc.vector.tensor_tensor(yT[:, bass.ds(i, 1), :], one(kmix), one(gsig), ALU.mult)\
                    .then_inc(s("fx_y_ready"), 1)
            looped(dve, 4, fox_pair)

            dve.wait_ge(s("fx_y_ready"), 4)
            dve.wait_ge(s("att_av_prod"), 96)
            nc.vector.memset(rp[:, 0:1], 0.0)
            nc.vector.memset(kp[:, 0:1], 0.0)
            nc.vector.memset(vp[:, 0:1], 0.0).then_inc(s("pads"), 1)
            dve.wait_ge(s("pads"), 2)

            def shifted(step, dst, pad, mu, m=P):
                step(nc.vector.tensor_tensor(dd[0:m, :], pad[0:m, 0:T], pad[0:m, 1:T + 1], ALU.subtract))
                return nc.vector.scalar_tensor_tensor(out=dst[0:m, :], in0=dd[0:m, :], scalar=mu, in1=pad[0:m, 1:T + 1],
                                                      op0=ALU.mult, op1=ALU.add)

            for n, (dst, pad, m) in enumerate(((rr, rp, P), (k0, kp, P), (vv, vp, 32))):
                dve.wait_ge(s("lora_taken"), n + 1)
                shifted(order, dst, pad, col[0:m, C_MU + 12 + n:C_MU + 13 + n], m).then_inc(s("lora_mixed"), 1)
                dve.wait_ge(s("lora_mixed"), n + 1)
            dve.wait_ge(s("lora_ready"), 4)
            rsteps = Order(dve, s("rw_order"), (s("consts"), NCONST))
            ar4 = lambda x: x.rearrange("p (t c) -> p t c", t=TT)

            def mix(i):
                for n, (dst, pad) in enumerate(((rr, rp), (k0, kp), (vv, vp))):
                    settle(dve, s("rw_taken"), 6 * i + n + 1)
                    rsteps(shifted(rsteps, dst, pad, col[:, bass.ds(C_MU + 4 * n + i, 1)]))
                nc.vector.tensor_scalar(kkn, k0, col[:, bass.ds(C_KK + i, 1)], None, ALU.mult).then_inc(s("rw_kk"), 1)

            mix(0)

            def rw_pair(i, first, last):
                rsteps.round(i, 27, 6)
                settle(dve, s("rw_taken"), 6 * i + 4)
                rsteps(nc.vector.tensor_scalar(ld, ld, -E_DECAY, None, ALU.mult))
                nc.vector.tensor_tensor_scan(Lc, cmask[:], ld, 0.0, ALU.mult, ALU.add).then_inc(s("rw_L"), 1)
                settle(dve, s("rw_L"), 2 * i + 1)
                nc.vector.tensor_tensor(Pprev, Lc, ld, ALU.subtract).then_inc(s("rw_L"), 1)
                settle(dve, s("rw_nrm"), i + 1)
                rsteps(nc.vector.tensor_scalar(nrm, nrm, 1e-12, None, ALU.max))
                rsteps(nc.vector.reciprocal(nrm, nrm))
                rsteps(nc.vector.tensor_tensor(kkn, kkn, nrm, ALU.mult))
                settle(dve, s("rw_taken"), 6 * i + 5)
                rsteps(nc.vector.tensor_scalar(dd, aa, 1.0, col[:, bass.ds(C_KA + i, 1)], ALU.subtract, ALU.mult))
                rsteps(nc.vector.scalar_tensor_tensor(out=k0, in0=dd, scalar=1.0, in1=k0, op0=ALU.add, op1=ALU.mult))
                settle(dve, s("rw_ms"), 2 * i + 1)
                nc.vector.scalar_tensor_tensor(out=sqr, in0=rr, scalar=col[:, bass.ds(C_RK + i, 1)], in1=k0,
                                               op0=ALU.mult, op1=ALU.mult).then_inc(s("rw_sq"), 1)
                rsteps(nc.vector.tensor_tensor(dd, kkn, aa, ALU.mult))
                settle(dve, s("rw_P"), 3 * i + 3)
                nc.vector.scalar_tensor_tensor(out=AR[:, :, 0, :], in0=ar4(kkn), scalar=-1.0, in1=ar4(Pprev),
                                               op0=ALU.mult, op1=ALU.mult).then_inc(s("rw_ops"), 1)
                nc.vector.tensor_tensor(AR[:, :, 1, :], ar4(rr), ar4(Pt), ALU.mult).then_inc(s("rw_ops"), 1)
                nc.vector.tensor_tensor(BT, dd, Pinv, ALU.mult).then_inc(s("rw_ops"), 1)
                nc.vector.tensor_tensor(KT, k0, Pinv, ALU.mult).then_inc(s("rw_ops"), 1)
                settle(dve, s("rw_ms"), 2 * i + 2)
                nc.vector.scalar_tensor_tensor(out=nrm, in0=ps[7][:], scalar=float(HD), in1=vv, op0=ALU.mult,
                                               op1=ALU.mult).then_inc(s("rw_bonus"), 1)
                nc.vector.memset(Zs[:, 0, :], 0.0).then_inc(s("rw_zt"), 1)
                for h in range(2):
                    for n in range(4):
                        settle(dve, s("rw_sm"), 10 * i + 5 * h + n + 1)
                        half = n % 2
                        dst = (ABT, AKT)[n // 2][h][:, 2 * half:2 * half + 2, :]
                        nc.vector.tensor_tensor(dst, ps[4 + n][:].rearrange("p (t c) -> p t c", t=2),
                                                maskAR[:].unsqueeze(1).to_broadcast([P, 2, 256]), ALU.mult)\
                            .then_inc(s("rw_smt"), 1)
                    settle(dve, s("rw_sm"), 10 * i + 5 * h + 5)
                    nc.vector.tensor_tensor(Dm[h], tiles4(ps[h][:]), bc4(mask1[:]), ALU.mult).then_inc(s("rw_smt"), 1)
                    settle(dve, s("rw_smt"), 10 * i + 5 * h + 5)
                    rsteps(nc.vector.tensor_tensor(DT[h], ABT[h][:, :, 0:P], bc4(maskT[0][:]), ALU.mult))
                    nc.vector.tensor_tensor(Dm[h], Dm[h], bc4(ident[:]), ALU.add).then_inc(s("rw_d0"), 1)
                    nc.vector.tensor_tensor(DT[h], DT[h], bc4(ident[:]), ALU.add).then_inc(s("rw_d0"), 1)
                settle(dve, s("rw_d0"), 4 * i + 4)
                for n in range(1, 6):
                    for h in range(2):
                        for w in range(2):
                            k = 4 * (n - 1) + 2 * h + w
                            settle(dve, s("rw_dd"), 20 * i + 4 * (n - 1) + 2 * h + 2)
                            m = (Dm, DT)[w][h]
                            nc.vector.tensor_tensor(m, tiles4(ps[2 + 2 * w + h][:]), m, ALU.add).then_inc(s("rw_dt"), 1)
                    settle(dve, s("rw_dt"), 20 * i + 4 * n)
                settle(dve, s("rw_gt"), 3 * i + 3)
                for c in range(8):
                    t, e = c // 2, c % 2
                    own = slice(64 * e, 64 * e + 64)
                    settle(dve, s("rw_u"), 8 * i + c + 1)
                    nc.vector.tensor_tensor(Usb[own, t, :], ps[1 + e][own, 0:P], Wm[own, t, :], ALU.add)\
                        .then_inc(s("rw_ut"), 1)
                    if c < 7:
                        decay = Pt[:, 64 * c + 63:64 * c + 64]
                        settle(dve, s("rw_z"), 7 * i + c + 1)
                        rsteps(nc.vector.scalar_tensor_tensor(out=ztmp, in0=ps[3 + e][:, 0:P], scalar=decay, in1=bdiag[:],
                                                              op0=ALU.mult, op1=ALU.mult))
                        nc.vector.scalar_tensor_tensor(out=Zs[:, c + 1, :], in0=Zs[:, c, :], scalar=decay, in1=ztmp,
                                                       op0=ALU.mult, op1=ALU.add).then_inc(s("rw_zt"), 1)
                        settle(dve, s("rw_zt"), 8 * i + c + 2)
                if not last:
                    mix(i + 1)
                y8 = y_sb.rearrange("p (u d) -> p u d", d=HD)
                bc8 = lambda x: x.unsqueeze(2).to_broadcast([P, 8, HD])
                settle(dve, s("rw_out_step"), 8 * i + 2)
                rsteps(nc.vector.tensor_reduce(st8[:, 0:8], y8, AX.X, ALU.add))
                rsteps(nc.vector.tensor_scalar(st8[:, 0:8], st8[:, 0:8], 1.0 / HD, None, ALU.mult))
                nc.vector.tensor_tensor(y8, y8, bc8(st8[:, 0:8]), ALU.subtract).then_inc(s("rw_out_step"), 1)
                settle(dve, s("rw_out_step"), 8 * i + 4)
                nc.vector.tensor_reduce(st8[:, 8:16], y_sq.rearrange("p (u d) -> p u d", d=HD), AX.X, ALU.add)\
                    .then_inc(s("rw_out_step"), 1)
                settle(dve, s("rw_out_step"), 8 * i + 6)
                rsteps(nc.vector.reciprocal(st8[:, 0:8], st8[:, 0:8]))
                settle(dve, s("rw_out_step"), 8 * i + 3)
                nc.vector.tensor_tensor(y8, y8, bc8(st8[:, 0:8]), ALU.mult).then_inc(s("rw_out_step"), 1)
                settle(dve, s("rw_out_step"), 8 * i + 8)
                rsteps(nc.vector.tensor_scalar(dd, ps[5][:], col[:, bass.ds(C_LG + i, 1)],
                                               col[:, bass.ds(C_LB + i, 1)], ALU.mult, ALU.add))
                rsteps(nc.vector.tensor_tensor(dd, dd, nrm, ALU.add))
                one = lambda x: x.rearrange("p (a b) -> p a b", a=1)
                settle(dve, s("rw_taken"), 6 * i + 6)
                nc.vector.tensor_tensor(yT[:, bass.ds(4 + i, 1), :], one(dd), one(gg), ALU.mult)\
                    .then_inc(s("rw_y_ready"), 1)
            pipelined(dve, 4, rw_pair)

            for n in range(KB):
                dve.wait_ge(s("lin_prod"), 4 * KB + n + 1)
                nc.vector.scalar_tensor_tensor(out=xT[:, n, :], in0=ps[BANKS["w_out"][n % 4]][:], scalar=mod[:, 16 + n:17 + n],
                                               in1=xT[:, n, :], op0=ALU.mult, op1=ALU.add)\
                    .then_inc(s("lin_added"), 1)

            normalise_mod("n2", 8)
            dve.wait_ge(s("side_loaded"), 64)
            dve.wait_ge(s("rt_sig"), 1)

            def top(vals, kth, k, mask, eq, at, starts, n):
                kb = kth.to_broadcast([P, TT, n])
                flat = lambda x: x.rearrange("p t e -> p (t e)")
                order(nc.vector.tensor_tensor(mask, vals, kb, ALU.is_gt))
                order(nc.vector.tensor_tensor(eq, vals, kb, ALU.is_equal))
                order(nc.vector.tensor_reduce(room, mask, AX.X, ALU.add))
                order(nc.vector.tensor_scalar(room, room, -1.0, float(k), ALU.mult, ALU.add))
                order(nc.vector.tensor_tensor_scan(flat(at), starts, flat(eq), 0.0, ALU.mult, ALU.add))
                order(nc.vector.tensor_tensor(at, at, room.to_broadcast([P, TT, n]), ALU.is_le))
                order(nc.vector.tensor_tensor(eq, eq, at, ALU.mult))
                order(nc.vector.tensor_tensor(mask, mask, eq, ALU.add))

            u8 = lambda x: x.rearrange("p t (g e) -> p (t g) e", e=8)
            order(nc.vector.tensor_tensor(sel, sco, rbias[:].unsqueeze(1).to_broadcast([P, TT, 64]), ALU.add))
            for u in range(32):
                mxi = nc.vector.max(srt[:, u, :], u8(sel)[:, u, :])
            order(mxi)
            order(nc.vector.tensor_tensor(gsc.rearrange("p t (g o) -> p (t g) o", o=1), srt[:, :, 0:1], srt[:, :, 1:2], ALU.add))
            for t in range(TT):
                mxi = nc.vector.max(gsrt[:, t, :], gsc[:, t, :])
            order(mxi)
            top(gsc, gsrt[:, :, 3:4], 4, gmask, geq, gpos, cm8[:], 8)
            order(nc.vector.tensor_scalar(gmask, gmask, 1.0, 1e30, ALU.subtract, ALU.mult))
            order(nc.vector.tensor_tensor(u8(sel), u8(sel), gmask.rearrange("p t (g o) -> p (t g) o", o=1)
                                          .to_broadcast([P, 32, 8]), ALU.add))
            for t in range(TT):
                mxi = nc.vector.max(esrt[:, t, :], sel[:, t, :])
            order(mxi)
            top(sel, esrt[:, :, 5:6], 6, wtok, eqm, pos, cmask[:, 0:256], 64)
            nc.vector.tensor_tensor(sco, wtok, sco, ALU.mult).then_inc(s("rt_masked"), 1)
            dve.wait_ge(s("rt_masked"), 1)
            order(nc.vector.tensor_reduce(wsum, sco, AX.X, ALU.add))
            order(nc.vector.reciprocal(wsum, wsum))
            order(nc.vector.tensor_scalar(wsum, wsum, 2.5, None, ALU.mult))
            order(nc.vector.tensor_tensor(sco, sco, wsum.to_broadcast([P, TT, EXPERTS]), ALU.mult))
            order(nc.vector.memset(place[:, :, ROUNDS * EXPERTS:PL], 0.0))
            dve.wait_ge(s("places_prod"), 1)
            order(nc.vector.scalar_tensor_tensor(out=place[:, :, 0:EXPERTS], in0=ps[0][:, 0:256].rearrange("p (t e) -> p t e", t=TT),
                                                 scalar=1.0, in1=wtok, op0=ALU.add, op1=ALU.mult))
            order(nc.vector.tensor_reduce(room[:, 0, :], ps[1][:, 0:EXPERTS], AX.X, ALU.max))
            nc.vector.tensor_scalar(overflow[:], room[:, 0, :], float(P), None, ALU.is_gt).then_inc(s("overflow_known"), 1)

            def onehots(n, par):
                settle(dve, s("slot_prod"), n - 1)
                for t in range(TT):
                    ins = nc.vector.tensor_scalar(onehot[par][:, t, :], count1, place[:, t, bass.ds(n, 1)], None, ALU.is_equal)
                ins.then_inc(s("onehot_ready"), 1)

            def slot_tokens(n, par):
                settle(dve, s("slot_prod"), n + 1)
                settle(dve, s(f"hrow{par}_loaded"), 8 * (n - par))
                nc.vector.tensor_scalar(slot_token[:, par:par + 1], ps[0][:, 0:1], -1.0, float(T), ALU.mult, ALU.add)\
                    .then_inc(s("slot_ready"), 1)

            onehots(0, 0)
            onehots(1, 1)
            for r in range(1, ROUNDS):
                ins = nc.vector.tensor_scalar(place[:, :, r * EXPERTS:(r + 1) * EXPERTS], place[:, :, 0:EXPERTS],
                                              float(-r * P), None, ALU.add)
            order(ins)
            slot_tokens(0, 0)
            onehots(2, 0)
            slot_tokens(1, 1)
            for b in range(2):
                dve.wait_ge(s("sh_gu_prod"), 3 + b)
                dve.wait_ge(s("sh_sil"), b + 1)
                nc.vector.tensor_tensor(xact[:, b, :], ps[6 + b][:], xsil[:, b, :], ALU.mult).then_inc(s("sh_act"), 1)
            for b in range(KB):
                dve.wait_ge(s("sh_prod"), b + 1)
                nc.vector.scalar_tensor_tensor(out=xT[:, b, :], in0=ps[4 + b % 4][:], scalar=mod[:, 40 + b:41 + b],
                                               in1=xT[:, b, :], op0=ALU.mult, op1=ALU.add).then_inc(s("sh_added"), 1)
            dve.wait_ge(s("g2_moved"), 32)

            def row_places():
                flat = lambda x: x.rearrange("p t e -> p (t e)")
                order(nc.vector.tensor_tensor_scan(flat(nth_sel), cmask[:, 0:256], flat(wtok), 0.0, ALU.mult, ALU.add))
                order(nc.vector.tensor_tensor(nth_sel, nth_sel, wtok, ALU.mult))
                order(nc.vector.tensor_tensor(ypos, place[:, :, 0:EXPERTS], etop.unsqueeze(1).to_broadcast([P, TT, EXPERTS]), ALU.add))
                for r in range(1, ROUNDS):
                    order(nc.vector.tensor_scalar(over, place[:, :, 0:EXPERTS], r * P + 0.5, float((EXPERTS - 1) * P), ALU.is_gt, ALU.mult))
                    order(nc.vector.tensor_tensor(ypos, ypos, over, ALU.add))

            def rows_of(js):
                for j in js:
                    order(nc.vector.tensor_scalar(over, nth_sel, float(j + 1), None, ALU.is_equal))
                    for v, dst in ((ypos, yposf), (sco, wj)):
                        order(nc.vector.tensor_tensor(pick, over, v, ALU.mult))
                        order(nc.vector.tensor_reduce(dst[:, :, j:j + 1], pick, AX.X, ALU.add))

            def expert(n, par):
                onehots(n + 3, 1 - par)
                settle(dve, s("exp_gu"), 2 * n + 2)
                settle(dve, s("exp_sil"), n + 1)
                settle(dve, s("exp_down"), 2 * n - 2)
                nc.vector.tensor_tensor(eact[par], ps[4][:, 0:256], esil[par], ALU.mult).then_inc(s("exp_act"), 1)
                slot_tokens(n + 2, par)
                for half in range(2):
                    settle(dve, s("exp_down"), 2 * n + half + 1)
                    if half == 0:
                        settle(dve, s(f"y{par}_stored"), 8 * (n - par))
                    cols = slice(512 * half, 512 * half + 512)
                    nc.vector.tensor_tensor(yrow[par][:, cols], ps[5 + half][:], g2_row[:, cols], ALU.mult)\
                        .then_inc(s("y_ready"), 1)

            def experts(i, first):
                for par in range(2):
                    expert(2 * i + par, par)
                    if first and par == 0:
                        row_places()
                        rows_of((0, 1))
                    elif first:
                        rows_of((2, 3, 4, 5))
                        nc.vector.tensor_copy(yidx[:].rearrange("p (t j) -> p t j", t=TT), yposf).then_inc(s("yidx_ready"), 1)
            all_experts(dve, experts)
            dve.wait_ge(s("res_taken"), 2 * TT)

            def last_norm(t):
                dve.wait_ge(s("fin_rms"), t + 1)
                order(nc.vector.reciprocal(ss4[:, 8 + t:9 + t], ss4[:, 4 + t:5 + t]))
                nc.vector.scalar_tensor_tensor(out=res[:, t, :], in0=res[:, t, :], scalar=ss4[:, 8 + t:9 + t], in1=fin_row,
                                               op0=ALU.mult, op1=ALU.mult).then_inc(s("out_ready"), 1)

            for t in range(TT):
                for j in range(6):
                    k = 6 * t + j
                    if k % 4 == 0:
                        dve.wait_ge(s(f"yg{k // 4 % 2}_loaded"), 64 * (k // 8 + 1))
                    wait(dve, s("y_summed"), k if j else 0)
                    nc.vector.scalar_tensor_tensor(out=res[:, t, :], in0=yg[k % 8], scalar=wj[:, t, j:j + 1], in1=res[:, t, :],
                                                   op0=ALU.mult, op1=ALU.add).then_inc(s("y_summed"), 1)
                if t:
                    last_norm(t - 1)
            last_norm(TT - 1)


def kernel(**inputs):
    import numpy as np
    import concourse.bacc as bacc
    from concourse.bass_utils import run_bass_kernel_spmd

    nc = bacc.Bacc("TRN2", target_bir_lowering=False, num_devices=1)
    arrays = {name: np.ascontiguousarray(value) for name, value in inputs.items()}
    a = {name: nc.dram_tensor(name, v.shape, mybir.dt.from_np(v.dtype), kind="ExternalInput").ap()
         for name, v in arrays.items()}
    out = nc.dram_tensor("out", [1, T, D], F32, kind="ExternalOutput").ap()
    program(nc, a, out)
    return run_bass_kernel_spmd(nc, [arrays], core_ids=[0]).results[0]["out"]
```
